# Optimizing a Trainium2 kernel written in Bass

```python
import math
import jax, jax.numpy as jnp
from jax import lax
import numpy as np
import jax
import jax.numpy as jnp

D_MODEL = 1024
BATCH = 1
SEQ = 512
DEPTH = 1

RET_HEADS = 4
RET_DK = 128
RET_DV = 256
RET_CHUNK = 128
ROPE_BASE = 10000.0
ATT_PATTERNS = ((128, 1), (512, 4), (2048, 16))
ATT_GROUPS = 3
ATT_HEADS_PER_GROUP = 4
ATT_HEADS = ATT_GROUPS * ATT_HEADS_PER_GROUP
ATT_DH = 128
ATT_QBLOCK = 128
REL_BUCKETS = 32
REL_MAX_EXACT = REL_BUCKETS // 2
REL_MAX_DIST = 2048
N_EXPERTS = 32
TOP_K = 4
D_EXPERT = D_MODEL
SWIGLU_LIMIT = 7.0
SWIGLU_ALPHA = 1.702
MOE_BLOCK = 128
EPS = 1e-6
GN_EPS = 1e-5

RET_QK_W = RET_HEADS * RET_DK
RET_V_W = RET_HEADS * RET_DV
ATT_W = ATT_HEADS * ATT_DH
ATT_OUT_W = ATT_HEADS_PER_GROUP * ATT_DH
IN_SPLITS = (RET_QK_W, RET_QK_W, RET_V_W, RET_V_W, ATT_W, ATT_W, ATT_W, D_MODEL, D_MODEL)
IN_W = 9728


def _split_points(sizes):
    pts, acc = [], 0
    for s in sizes[:-1]:
        acc += s
        pts.append(acc)
    return pts

def rms_norm(x, g):
    xf = x.astype(jnp.float32)
    return xf * lax.rsqrt(jnp.mean(xf * xf, axis=-1, keepdims=True) + EPS) * g

def modulate(h, shift, scale):
    return h * (1.0 + scale[:, None, :]) + shift[:, None, :]

def rotary(t, pos):
    half = t.shape[-1] // 2
    inv = ROPE_BASE ** (-jnp.arange(half, dtype=jnp.float32) / half)
    ang = pos[:, None] * inv[None, :]
    cos, sin = jnp.cos(ang)[:, None, :], jnp.sin(ang)[:, None, :]
    t1, t2 = t[..., :half], t[..., half:]
    return jnp.concatenate([t1 * cos - t2 * sin, t1 * sin + t2 * cos], axis=-1)

def retention(q, k, v, g):
    B, S = q.shape[:2]
    H, dk, dv, C = RET_HEADS, RET_DK, RET_DV, RET_CHUNK
    nC = S // C
    pos = jnp.arange(S, dtype=jnp.float32)
    q = rotary(q.astype(jnp.float32).reshape(B, S, H, dk), pos)
    k = rotary(k.astype(jnp.float32).reshape(B, S, H, dk), pos) * (dk ** -0.5)
    v = v.astype(jnp.float32).reshape(B, S, H, dv)
    log_g = jnp.log1p(-jnp.exp2(-5.0 - jnp.arange(H, dtype=jnp.float32)))
    i = jnp.arange(C, dtype=jnp.float32)
    diff = i[:, None] - i[None, :]
    decay = jnp.where(diff[None] >= 0, jnp.exp(jnp.maximum(diff, 0.0)[None] * log_g[:, None, None]), 0.0)
    qc = q.reshape(B, nC, C, H, dk)
    kc = k.reshape(B, nC, C, H, dk)
    vc = v.reshape(B, nC, C, H, dv)
    scores = jnp.einsum('bnihd,bnjhd->bnhij', qc, kc) * decay
    inner = jnp.einsum('bnhij,bnjhe->bnihe', scores, vc)
    zeta = jnp.exp((C - 1.0 - i)[:, None] * log_g[None, :])
    kv = jnp.einsum('bnjhd,bnjhe->nbhde', kc * zeta[:, :, None], vc)
    g_chunk = jnp.exp(C * log_g)[None, :, None, None]

    def step(R, kv_n):
        return g_chunk * R + kv_n, R

    _, R_prev = lax.scan(step, jnp.zeros_like(kv[0]), kv)
    xi = jnp.exp((i + 1.0)[:, None] * log_g[None, :])
    cross = jnp.einsum('bnihd,nbhde->bnihe', qc * xi[:, :, None], R_prev)
    y = (inner + cross).reshape(B, S, H, dv)
    mu = jnp.mean(y, axis=-1, keepdims=True)
    var = jnp.mean(jnp.square(y - mu), axis=-1, keepdims=True)
    y = (y - mu) * lax.rsqrt(var + GN_EPS)
    return jax.nn.silu(g.astype(jnp.float32)) * y.reshape(B, S, H * dv)

def t5_bucket(dist):
    is_small = dist < REL_MAX_EXACT
    ratio = jnp.log(jnp.maximum(dist, 1).astype(jnp.float32) / REL_MAX_EXACT) / math.log(REL_MAX_DIST / REL_MAX_EXACT)
    large = REL_MAX_EXACT + (ratio * (REL_BUCKETS - REL_MAX_EXACT)).astype(jnp.int32)
    large = jnp.minimum(large, REL_BUCKETS - 1)
    return jnp.where(is_small, dist, large)

def dilated_attention(q, k, v, rel_bias):
    B, S = q.shape[:2]
    G, Hg, dh, QB = ATT_GROUPS, ATT_HEADS_PER_GROUP, ATT_DH, ATT_QBLOCK
    nb = S // QB
    q = q.reshape(B, S, G, Hg, dh)
    k = k.reshape(B, S, G, Hg, dh)
    v = v.reshape(B, S, G, Hg, dh)
    qb = q.reshape(B, nb, QB, G, Hg, dh).transpose(1, 0, 2, 3, 4, 5)
    ks = [k[:, :, g] for g in range(G)]
    vs = [v[:, :, g] for g in range(G)]
    biases = []
    for g, (w, r) in enumerate(ATT_PATTERNS):
        nk = w // r + 1
        bkt = t5_bucket(r * jnp.arange(nk, dtype=jnp.int32))
        biases.append(rel_bias[bkt, g * Hg:(g + 1) * Hg].T.astype(jnp.float32))
    scale = dh ** -0.5

    def block(args):
        n, qn = args
        pos = n * QB + jnp.arange(QB, dtype=jnp.int32)
        outs, lses = [], []
        for g, (w, r) in enumerate(ATT_PATTERNS):
            nk = w // r + 1
            idx = pos[:, None] - r * jnp.arange(nk, dtype=jnp.int32)[None, :]
            valid = idx >= 0
            idc = jnp.maximum(idx, 0)
            kg = jnp.take(ks[g], idc, axis=1)
            vg = jnp.take(vs[g], idc, axis=1)
            s = jnp.einsum('bqhd,bqjhd->bhqj', qn[:, :, g], kg).astype(jnp.float32) * scale
            s = s + biases[g][:, None, :]
            s = jnp.where(valid[None, None], s, -jnp.inf)
            m = jnp.max(s, axis=-1, keepdims=True)
            e = jnp.exp(s - m)
            l = jnp.sum(e, axis=-1, keepdims=True)
            o = jnp.einsum('bhqj,bqjhd->bqhd', e / l, vg.astype(jnp.float32))
            outs.append(o)
            lses.append((m + jnp.log(l))[..., 0].transpose(0, 2, 1))
        alpha = jax.nn.softmax(jnp.stack(lses, axis=0), axis=0)
        out = alpha[0][..., None] * outs[0]
        for g in range(1, G):
            out = out + alpha[g][..., None] * outs[g]
        return out

    out = lax.map(block, (jnp.arange(nb, dtype=jnp.int32), qb))
    return out.transpose(1, 0, 2, 3, 4).reshape(B, S, Hg * dh)

def moe(h, w_router, b_router, w1, b1, w2, b2):
    B, S, D = h.shape
    T = B * S
    xf = h.reshape(T, D)
    logits = (xf @ w_router + b_router).astype(jnp.float32)
    top_val, top_idx = lax.top_k(logits, TOP_K)
    gates = jax.nn.softmax(top_val, axis=-1)
    A = T * TOP_K
    flat_e = top_idx.reshape(A).astype(jnp.int32)
    flat_tok = jnp.arange(A, dtype=jnp.int32) // TOP_K
    flat_gate = gates.reshape(A)
    order = jnp.argsort(flat_e, stable=True)
    se = flat_e[order]
    counts = jnp.bincount(flat_e, length=N_EXPERTS)
    starts = jnp.cumsum(counts) - counts
    padded = (counts + MOE_BLOCK - 1) // MOE_BLOCK * MOE_BLOCK
    pend = jnp.cumsum(padded)
    pstart = pend - padded
    dest = pstart[se] + jnp.arange(A, dtype=jnp.int32) - starts[se]
    nblk = -(-A // MOE_BLOCK) + N_EXPERTS
    n_rows = nblk * MOE_BLOCK
    row_tok = jnp.full((n_rows,), T, jnp.int32).at[dest].set(flat_tok[order])
    row_gate = jnp.zeros((n_rows,), jnp.float32).at[dest].set(flat_gate[order])
    block_e = jnp.minimum(jnp.searchsorted(pend, jnp.arange(nblk, dtype=jnp.int32) * MOE_BLOCK, side='right'), N_EXPERTS - 1)
    x_pad = jnp.concatenate([xf, jnp.zeros((1, D), xf.dtype)], axis=0)
    xin = x_pad[row_tok].reshape(nblk, MOE_BLOCK, D)

    def expert_block(args):
        xb, e = args
        u = xb @ w1[e] + b1[e]
        glu = jnp.minimum(u[:, ::2], SWIGLU_LIMIT)
        lin = jnp.clip(u[:, 1::2], -SWIGLU_LIMIT, SWIGLU_LIMIT)
        a = glu * jax.nn.sigmoid(SWIGLU_ALPHA * glu) * (lin + 1.0)
        return a @ w2[e] + b2[e]

    yb = lax.map(expert_block, (xin, block_e)).reshape(n_rows, D)
    y = jnp.zeros((T + 1, D), jnp.float32).at[row_tok].add(yb.astype(jnp.float32) * row_gate[:, None])
    return y[:T].reshape(B, S, D)

def first_inputs(seed: int = 0) -> dict:
    key = jax.random.key(seed)
    ks = jax.random.split(key, 20)
    D, L, E, F = D_MODEL, DEPTH, N_EXPERTS, D_EXPERT
    nrm = jax.random.normal
    f32 = jnp.float32
    return {
        "x": nrm(ks[0], (BATCH, SEQ, D), f32),
        "c": nrm(ks[1], (BATCH, D), f32),
        "w_ada": nrm(ks[2], (L, D, 6 * D), f32) * (0.5 * D ** -0.5),
        "b_ada": nrm(ks[3], (L, 6 * D), f32) * 0.02,
        "g_mix": 1.0 + 0.02 * nrm(ks[4], (L, D), f32),
        "w_in": nrm(ks[5], (L, D, IN_W), f32) * D ** -0.5,
        "rel_bias": nrm(ks[6], (REL_BUCKETS, ATT_HEADS), f32) * 0.2,
        "w_ret_o": nrm(ks[7], (L, RET_V_W, D), f32) * RET_V_W ** -0.5,
        "w_att_o": nrm(ks[8], (L, ATT_OUT_W, D), f32) * ATT_OUT_W ** -0.5,
        "w_o": nrm(ks[9], (L, D, D), f32) * D ** -0.5,
        "g_ffn": 1.0 + 0.02 * nrm(ks[10], (L, D), f32),
        "w_router": nrm(ks[11], (L, D, E), f32) * D ** -0.5,
        "b_router": nrm(ks[12], (L, E), f32) * 0.01,
        "w_mlp1": nrm(ks[13], (L, E, D, 2 * F), f32) * D ** -0.5,
        "b_mlp1": nrm(ks[14], (L, E, 2 * F), f32) * 0.01,
        "w_mlp2": nrm(ks[15], (L, E, F, D), f32) * F ** -0.5,
        "b_mlp2": nrm(ks[16], (L, E, D), f32) * 0.01,
        "g_final": 1.0 + 0.02 * nrm(ks[17], (D,), f32),
    }

def first_block(x, c, w_ada, b_ada, g_mix, w_in, rel_bias, w_ret_o, w_att_o, w_o, g_ffn,
              w_router, b_router, w_mlp1, b_mlp1, w_mlp2, b_mlp2, g_final):
    cs = jax.nn.silu(c.astype(jnp.float32))
    pts = _split_points(IN_SPLITS)
    for l in range(DEPTH):
        mod = cs @ w_ada[l] + b_ada[l]
        sh_a, sc_a, gt_a, sh_f, sc_f, gt_f = jnp.split(mod, 6, axis=-1)
        h = modulate(rms_norm(x, g_mix[l]), sh_a, sc_a)
        u = h @ w_in[l]
        rq, rk, rv, rg, aq, ak, av, ga, gb = jnp.split(u, pts, axis=-1)
        ret = retention(rq, rk, rv, rg)
        att = dilated_attention(aq, ak, av, rel_bias)
        merged = jax.nn.sigmoid(ga) * (ret @ w_ret_o[l]) + jax.nn.sigmoid(gb) * (att @ w_att_o[l])
        x = x + gt_a[:, None, :] * (merged @ w_o[l])
        h = modulate(rms_norm(x, g_ffn[l]), sh_f, sc_f)
        x = x + gt_f[:, None, :] * moe(h, w_router[l], b_router[l], w_mlp1[l], b_mlp1[l], w_mlp2[l], b_mlp2[l])
    return rms_norm(x, g_final)


MIX_WIDTH = D_MODEL
DA_HEADS = 4
DA_QK_DIM = 64
DA_V_DIM = 2 * DA_QK_DIM
DA_WIDTH = DA_HEADS * DA_V_DIM
GLA_HEADS = 4
GLA_V_DIM = 64
GLA_K_DIM = GLA_V_DIM // 2
GLA_WIDTH = GLA_HEADS * GLA_V_DIM
GLA_GATE_RANK = 16
GLA_GATE_NORM = 16.0
GLA_CHUNK = 64
POOL_WINDOWS = (2, 4, 8, 16)
POOL_GROUPS = 4
POOL_WIDTH = MIX_WIDTH - DA_WIDTH - GLA_WIDTH
POOL_GROUP_DIM = POOL_WIDTH // POOL_GROUPS
DA_Q_COLS = DA_HEADS * 2 * DA_QK_DIM
DA_K_COLS = DA_HEADS * 2 * DA_QK_DIM
DA_V_COLS = DA_WIDTH
GLA_Q_COLS = GLA_HEADS * GLA_K_DIM
GLA_K_COLS = GLA_HEADS * GLA_K_DIM
GLA_V_COLS = GLA_WIDTH
GLA_R_COLS = GLA_WIDTH
IN_SIZES = (DA_Q_COLS, DA_K_COLS, DA_V_COLS, GLA_Q_COLS, GLA_K_COLS, GLA_V_COLS, GLA_GATE_RANK, GLA_R_COLS, POOL_WIDTH)
IN_TOTAL = sum(IN_SIZES)
FFN_HIDDEN = -(-8 * D_MODEL // (3 * 256)) * 256
REL_MAX_DIST_2 = 128
Q_BLOCK = 128


def rms_norm_2(x, g):
    xf = x.astype(jnp.float32)
    y = xf * lax.rsqrt(jnp.mean(xf * xf, axis=-1, keepdims=True) + EPS)
    return (y * g.astype(jnp.float32)).astype(x.dtype)

def t5_bucket_2(dist):
    max_exact = REL_BUCKETS // 2
    d = jnp.maximum(dist, 0)
    large = max_exact + (jnp.log(jnp.maximum(d, 1).astype(jnp.float32) / max_exact)
                         / math.log(REL_MAX_DIST_2 / max_exact) * (REL_BUCKETS - max_exact)).astype(jnp.int32)
    large = jnp.minimum(large, REL_BUCKETS - 1)
    return jnp.where(d < max_exact, d, large)

def diff_attention(q, k, v, lam, bias_by_dist):
    S = q.shape[1]
    scale = DA_QK_DIM ** -0.5
    outs = []
    for i in range(S // Q_BLOCK):
        q0 = i * Q_BLOCK
        kend = q0 + Q_BLOCK
        qb = q[:, q0:kend]
        kb = k[:, :kend]
        vb = v[:, :kend]
        s = jnp.einsum('bqhmd,bkhmd->bhmqk', qb, kb).astype(jnp.float32) * scale
        dist = jnp.arange(q0, kend)[:, None] - jnp.arange(kend)[None, :]
        bias = bias_by_dist[jnp.clip(dist, 0, S - 1)].astype(jnp.float32)
        s = s + jnp.transpose(bias, (2, 0, 1))[None, :, None]
        s = jnp.where(dist[None, None, None] >= 0, s, -1e30)
        p = jax.nn.softmax(s, axis=-1)
        w = p[:, :, 0] - lam * p[:, :, 1]
        outs.append(jnp.einsum('bhqk,bkhd->bqhd', w.astype(v.dtype), vb))
    return jnp.concatenate(outs, axis=1)

def gla_chunked(q, k, v, log_a):
    B, S, H, dk = q.shape
    dv = v.shape[-1]
    C = GLA_CHUNK
    N = S // C

    def chunkify(t):
        return t.astype(jnp.float32).reshape(B, N, C, H, t.shape[-1]).transpose(1, 0, 3, 2, 4)

    qc = chunkify(q) * (dk ** -0.5)
    kc = chunkify(k)
    vc = chunkify(v)
    b = jnp.cumsum(chunkify(log_a), axis=3)
    q_dec = qc * jnp.exp(b)
    k_inv = kc * jnp.exp(-b)
    k_end = kc * jnp.exp(b[..., -1:, :] - b)
    chunk_decay = jnp.exp(b[..., -1, :])
    causal = jnp.tril(jnp.ones((C, C), jnp.float32))
    attn = jnp.einsum('nbhqd,nbhkd->nbhqk', q_dec, k_inv) * causal
    o_intra = jnp.einsum('nbhqk,nbhkv->nbhqv', attn, vc)

    def step(state, inp):
        q_c, k_c, v_c, dec_c = inp
        o_inter = jnp.einsum('bhqd,bhdv->bhqv', q_c, state)
        state = state * dec_c[..., None] + jnp.einsum('bhkd,bhkv->bhdv', k_c, v_c)
        return state, o_inter

    state0 = jnp.zeros((B, H, dk, dv), jnp.float32)
    _, o_inter = lax.scan(step, state0, (q_dec, k_end, vc, chunk_decay))
    o = o_intra + o_inter
    return o.transpose(1, 0, 3, 2, 4).reshape(B, S, H, dv).astype(v.dtype)

def multiscale_pool(u, pool_w, pool_scale):
    B, S, _ = u.shape
    uf = u.astype(jnp.float32)
    cs = jnp.concatenate([jnp.zeros((B, 1, POOL_WIDTH), jnp.float32), jnp.cumsum(uf, axis=1)], axis=1)
    t = jnp.arange(S)
    outs = []
    for g, win in enumerate(POOL_WINDOWS):
        lo, hi = g * POOL_GROUP_DIM, (g + 1) * POOL_GROUP_DIM
        csg = cs[..., lo:hi]
        prev = jnp.concatenate([jnp.zeros((B, win - 1, POOL_GROUP_DIM), jnp.float32), csg[:, :S + 1 - win]], axis=1)
        count = jnp.minimum(t + 1, win).astype(jnp.float32)
        pooled = (csg[:, 1:] - prev) / count[None, :, None] - uf[..., lo:hi]
        outs.append(jnp.einsum('bsc,cd->bsd', pooled, pool_w[g].astype(jnp.float32)))
    y = jnp.concatenate(outs, axis=-1) * pool_scale.astype(jnp.float32)
    return y.astype(u.dtype)

def second_inputs(seed: int = 0) -> dict:
    key = jax.random.key(seed)
    ks = jax.random.split(key, 18)
    f32 = jnp.float32

    def nrm(k, shape, scale):
        return jax.random.normal(k, shape, f32) * scale

    def gain(k, shape):
        return 1.0 + 0.1 * jax.random.normal(k, shape, f32)

    return {
        'x': nrm(ks[0], (BATCH, SEQ, D_MODEL), 1.0),
        'attn_norm_g': gain(ks[1], (DEPTH, D_MODEL)),
        'w_in': nrm(ks[2], (DEPTH, D_MODEL, IN_TOTAL), D_MODEL ** -0.5),
        'q_norm_g': gain(ks[3], (DEPTH, DA_QK_DIM)),
        'k_norm_g': gain(ks[4], (DEPTH, DA_QK_DIM)),
        'lambda_vecs': nrm(ks[5], (DEPTH, 4, DA_QK_DIM), 0.1),
        'da_subln_g': gain(ks[6], (DEPTH, DA_V_DIM)),
        'rel_bias': nrm(ks[7], (REL_BUCKETS, DA_HEADS), 0.5),
        'gla_gate_w': nrm(ks[8], (DEPTH, GLA_GATE_RANK, GLA_HEADS * GLA_K_DIM), GLA_GATE_RANK ** -0.5),
        'gla_gate_b': nrm(ks[9], (DEPTH, GLA_HEADS * GLA_K_DIM), 0.1),
        'gla_norm_g': gain(ks[10], (DEPTH, GLA_V_DIM)),
        'pool_w': nrm(ks[11], (DEPTH, POOL_GROUPS, POOL_GROUP_DIM, POOL_GROUP_DIM), POOL_GROUP_DIM ** -0.5),
        'pool_scale': gain(ks[12], (DEPTH, POOL_WIDTH)),
        'w_out': nrm(ks[13], (DEPTH, MIX_WIDTH, D_MODEL), MIX_WIDTH ** -0.5),
        'ffn_norm_g': gain(ks[14], (DEPTH, D_MODEL)),
        'w_gate': nrm(ks[15], (DEPTH, D_MODEL, FFN_HIDDEN), D_MODEL ** -0.5),
        'w_up': nrm(ks[16], (DEPTH, D_MODEL, FFN_HIDDEN), D_MODEL ** -0.5),
        'w_down': nrm(ks[17], (DEPTH, FFN_HIDDEN, D_MODEL), FFN_HIDDEN ** -0.5),
    }

def second_block(x, attn_norm_g, w_in, q_norm_g, k_norm_g, lambda_vecs, da_subln_g, rel_bias,
              gla_gate_w, gla_gate_b, gla_norm_g, pool_w, pool_scale, w_out,
              ffn_norm_g, w_gate, w_up, w_down):
    B, S, _ = x.shape
    split_points = np.cumsum(IN_SIZES)[:-1].tolist()
    bias_by_dist = rel_bias[t5_bucket_2(jnp.arange(S))]
    h = x
    for l in range(DEPTH):
        hn = rms_norm_2(h, attn_norm_g[l])
        proj = jnp.einsum('bsd,de->bse', hn, w_in[l])
        da_q, da_k, da_v, g_q, g_k, g_v, g_lr, g_r, pool_u = jnp.split(proj, split_points, axis=-1)

        q = rms_norm_2(da_q.reshape(B, S, DA_HEADS, 2, DA_QK_DIM), q_norm_g[l])
        k = rms_norm_2(da_k.reshape(B, S, DA_HEADS, 2, DA_QK_DIM), k_norm_g[l])
        v = da_v.reshape(B, S, DA_HEADS, DA_V_DIM)
        lv = lambda_vecs[l].astype(jnp.float32)
        lam_init = 0.8 - 0.6 * math.exp(-0.3 * l)
        lam = jnp.exp(jnp.sum(lv[0] * lv[1])) - jnp.exp(jnp.sum(lv[2] * lv[3])) + lam_init
        a_out = diff_attention(q, k, v, lam, bias_by_dist)
        a_out = rms_norm_2(a_out, da_subln_g[l]) * (1.0 - lam_init)
        a_out = a_out.reshape(B, S, DA_WIDTH).astype(h.dtype)

        z = jnp.einsum('bsr,rk->bsk', g_lr, gla_gate_w[l]) + gla_gate_b[l]
        log_a = jax.nn.log_sigmoid(z.astype(jnp.float32)) / GLA_GATE_NORM
        o = gla_chunked(g_q.reshape(B, S, GLA_HEADS, GLA_K_DIM),
                        g_k.reshape(B, S, GLA_HEADS, GLA_K_DIM),
                        g_v.reshape(B, S, GLA_HEADS, GLA_V_DIM),
                        log_a.reshape(B, S, GLA_HEADS, GLA_K_DIM))
        o = rms_norm_2(o, gla_norm_g[l]).reshape(B, S, GLA_WIDTH)
        b_out = (o * jax.nn.silu(g_r)).astype(h.dtype)

        c_out = multiscale_pool(pool_u, pool_w[l], pool_scale[l]).astype(h.dtype)

        mixed = jnp.concatenate([a_out, b_out, c_out], axis=-1)
        h = h + jnp.einsum('bse,ed->bsd', mixed, w_out[l])

        hn = rms_norm_2(h, ffn_norm_g[l])
        ff = jax.nn.silu(jnp.einsum('bsd,df->bsf', hn, w_gate[l])) * jnp.einsum('bsd,df->bsf', hn, w_up[l])
        h = h + jnp.einsum('bsf,fd->bsd', ff, w_down[l])
    return h


HEAD_DIM = 64
FOX_HEADS = 4
RWKV_HEADS = 8
MOBA_HEADS = 4
FOX_W = FOX_HEADS * HEAD_DIM
RWKV_W = RWKV_HEADS * HEAD_DIM
MOBA_W = MOBA_HEADS * HEAD_DIM
D_MIX = FOX_W + RWKV_W + MOBA_W
DECAY_LORA = 64
AAA_LORA = 64
GATE_LORA = 128
MOBA_BLOCK = 256
MOBA_TOPK = 3
FOX_Q_BLOCK = 128
MOBA_Q_BLOCK = 64
D_FF = 2816
CONV_W = 3
NORM_EPS = 1e-6
GN_EPS_3 = 64e-5

FOX_COLS = 3 * FOX_W + FOX_HEADS
RWKV_COLS = 3 * RWKV_W + DECAY_LORA + AAA_LORA + GATE_LORA
MOBA_COLS = 3 * MOBA_W
D_IN = FOX_COLS + RWKV_COLS + MOBA_COLS
RWKV_SPLITS = [RWKV_W, 2 * RWKV_W, 3 * RWKV_W, 3 * RWKV_W + DECAY_LORA, 3 * RWKV_W + DECAY_LORA + AAA_LORA]


def _rmsnorm(x, g):
    xf = x.astype(jnp.float32)
    y = xf * lax.rsqrt(jnp.mean(xf * xf, axis=-1, keepdims=True) + NORM_EPS)
    return (y * g).astype(x.dtype)

def _split_heads(t, n_heads):
    b, s, _ = t.shape
    return t.reshape(b, s, n_heads, HEAD_DIM).transpose(0, 2, 1, 3)

def _merge_heads(t):
    b, h, s, d = t.shape
    return t.transpose(0, 2, 1, 3).reshape(b, s, h * d)

def _shift_right(t, n):
    return jnp.pad(t, ((0, 0), (n, 0), (0, 0)))[:, : t.shape[1]]

def fox_attention(q, k, v, f_logit, f_bias):
    b, s, _ = q.shape
    q, k, v = (_split_heads(t, FOX_HEADS) for t in (q, k, v))
    log_f = jax.nn.log_sigmoid(f_logit.astype(jnp.float32) + f_bias.astype(jnp.float32))
    cum = jnp.cumsum(log_f, axis=1).transpose(0, 2, 1)
    n_blk = s // FOX_Q_BLOCK
    q_blocks = q.reshape(b, FOX_HEADS, n_blk, FOX_Q_BLOCK, HEAD_DIM).transpose(2, 0, 1, 3, 4)
    cum_blocks = cum.reshape(b, FOX_HEADS, n_blk, FOX_Q_BLOCK).transpose(2, 0, 1, 3)
    k_pos = jnp.arange(s)
    scale = HEAD_DIM ** -0.5

    def one_block(args):
        q_i, cum_i, i = args
        q_pos = i * FOX_Q_BLOCK + jnp.arange(FOX_Q_BLOCK)
        logits = jnp.einsum('bhqd,bhkd->bhqk', q_i, k).astype(jnp.float32) * scale
        logits = logits + cum_i[..., :, None] - cum[..., None, :]
        logits = jnp.where(k_pos[None, :] <= q_pos[:, None], logits, -jnp.inf)
        probs = jax.nn.softmax(logits, axis=-1).astype(v.dtype)
        return jnp.einsum('bhqk,bhkd->bhqd', probs, v)

    out = lax.map(one_block, (q_blocks, cum_blocks, jnp.arange(n_blk)))
    return _merge_heads(out.transpose(1, 2, 0, 3, 4).reshape(b, FOX_HEADS, s, HEAD_DIM))

def rwkv7_time_mix(feat, mu, w0, w2, a0, a2, g2, k_k, k_a, r_k, ln_w, ln_b):
    b, s, _ = feat.shape
    feat = feat + (_shift_right(feat, 1) - feat) * mu
    r, k, v, w_lo, a_lo, g_lo = jnp.split(feat, RWKV_SPLITS, axis=-1)
    log_w = -jax.nn.softplus(-(w0 + jnp.tanh(w_lo) @ w2)) - 0.5
    decay = jnp.exp(-jnp.exp(log_w.astype(jnp.float32)))
    a = jax.nn.sigmoid(a0 + a_lo @ a2)
    g = jax.nn.sigmoid(g_lo) @ g2
    kk = (k * k_k).astype(jnp.float32).reshape(b, s, RWKV_HEADS, HEAD_DIM)
    kk = kk / jnp.maximum(jnp.sqrt(jnp.sum(kk * kk, axis=-1, keepdims=True)), 1e-12)
    k = k * (1.0 + (a - 1.0) * k_a)

    def heads(t):
        return t.astype(jnp.float32).reshape(b, s, RWKV_HEADS, HEAD_DIM)

    rh, kh, vh, ah, wh = heads(r), heads(k), heads(v), heads(a), heads(decay)
    xs = tuple(t.transpose(1, 0, 2, 3) for t in (rh, wh, kh, vh, kk, ah))

    def step(state, inp):
        r_t, w_t, k_t, v_t, kk_t, a_t = inp
        removed = jnp.einsum('bhvk,bhk->bhv', state, kk_t)
        state = (state * w_t[:, :, None, :]
                 - removed[..., None] * (kk_t * a_t)[:, :, None, :]
                 + v_t[..., None] * k_t[:, :, None, :])
        return state, jnp.einsum('bhvk,bhk->bhv', state, r_t)

    state0 = jnp.zeros((b, RWKV_HEADS, HEAD_DIM, HEAD_DIM), jnp.float32)
    _, y = lax.scan(step, state0, xs)
    y = y.transpose(1, 0, 2, 3)
    mean = jnp.mean(y, axis=-1, keepdims=True)
    var = jnp.mean(jnp.square(y - mean), axis=-1, keepdims=True)
    y = ((y - mean) * lax.rsqrt(var + GN_EPS_3)).reshape(b, s, RWKV_W) * ln_w + ln_b
    bonus = jnp.sum(rh * kh * r_k, axis=-1, keepdims=True) * vh
    y = (y + bonus.reshape(b, s, RWKV_W)) * g
    return y.astype(feat.dtype)

def moba_attention(q, k, v):
    b, s, _ = q.shape
    q, k, v = (_split_heads(t, MOBA_HEADS) for t in (q, k, v))
    n_kb = -(-s // MOBA_BLOCK)
    s_pad = n_kb * MOBA_BLOCK
    pad = ((0, 0), (0, 0), (0, s_pad - s), (0, 0))
    k_p, v_p = jnp.pad(k, pad), jnp.pad(v, pad)
    k_blocks = k_p.reshape(b, MOBA_HEADS, n_kb, MOBA_BLOCK, HEAD_DIM)
    v_blocks = v_p.reshape(b, MOBA_HEADS, n_kb, MOBA_BLOCK, HEAD_DIM)
    k_mean = jnp.mean(k_blocks.astype(jnp.float32), axis=3)
    top_k = min(MOBA_TOPK, n_kb)
    n_qc = s // MOBA_Q_BLOCK
    q_chunks = q.reshape(b, MOBA_HEADS, n_qc, MOBA_Q_BLOCK, HEAD_DIM).transpose(2, 0, 1, 3, 4)
    gather_blocks = jax.vmap(jax.vmap(lambda blocks, idx: blocks[idx]))
    blk_ids = jnp.arange(n_kb)
    own_offsets = jnp.arange(MOBA_BLOCK)
    scale = HEAD_DIM ** -0.5

    def one_chunk(args):
        q_i, ci = args
        q_pos = ci * MOBA_Q_BLOCK + jnp.arange(MOBA_Q_BLOCK)
        own = (ci * MOBA_Q_BLOCK) // MOBA_BLOCK
        gate = jnp.einsum('bhqd,bhnd->bhqn', q_i.astype(jnp.float32), k_mean)
        gate = jnp.where(blk_ids < own, gate, -jnp.inf)
        gate_val, sel = lax.top_k(gate, top_k)
        valid = jnp.isfinite(gate_val)
        k_sel = gather_blocks(k_blocks, sel)
        v_sel = gather_blocks(v_blocks, sel)
        s_sel = jnp.einsum('bhqd,bhqnkd->bhqnk', q_i, k_sel).astype(jnp.float32) * scale
        s_sel = jnp.where(valid[..., None], s_sel, -jnp.inf)
        k_own = lax.dynamic_slice_in_dim(k_p, own * MOBA_BLOCK, MOBA_BLOCK, axis=2)
        v_own = lax.dynamic_slice_in_dim(v_p, own * MOBA_BLOCK, MOBA_BLOCK, axis=2)
        s_own = jnp.einsum('bhqd,bhkd->bhqk', q_i, k_own).astype(jnp.float32) * scale
        s_own = jnp.where(own * MOBA_BLOCK + own_offsets[None, :] <= q_pos[:, None], s_own, -jnp.inf)
        logits = jnp.concatenate([s_sel.reshape(b, MOBA_HEADS, MOBA_Q_BLOCK, top_k * MOBA_BLOCK), s_own], axis=-1)
        probs = jax.nn.softmax(logits, axis=-1).astype(v.dtype)
        p_sel = probs[..., : top_k * MOBA_BLOCK].reshape(b, MOBA_HEADS, MOBA_Q_BLOCK, top_k, MOBA_BLOCK)
        p_own = probs[..., top_k * MOBA_BLOCK:]
        return (jnp.einsum('bhqnk,bhqnkd->bhqd', p_sel, v_sel)
                + jnp.einsum('bhqk,bhkd->bhqd', p_own, v_own))

    out = lax.map(one_chunk, (q_chunks, jnp.arange(n_qc)))
    return _merge_heads(out.transpose(1, 2, 0, 3, 4).reshape(b, MOBA_HEADS, s, HEAD_DIM))

def _causal_dwconv(u, w, bias):
    out = bias
    for j in range(CONV_W):
        out = out + _shift_right(u, CONV_W - 1 - j) * w[j]
    return out

def third_inputs(seed: int = 0) -> dict:
    key = jax.random.key(seed)
    ks = iter(jax.random.split(key, 32))

    def nrm(shape, scale):
        return scale * jax.random.normal(next(ks), shape, jnp.float32)

    L, D = DEPTH, D_MODEL
    return {
        "x": nrm((BATCH, SEQ, D), 1.0),
        "c": nrm((BATCH, D), 1.0),
        "w_mod": nrm((L, D, 6 * D), 0.5 * D ** -0.5),
        "b_mod": nrm((L, 6 * D), 0.02),
        "norm_mix": 1.0 + nrm((L, D), 0.02),
        "w_in": nrm((L, D, D_IN), D ** -0.5),
        "fox_f_bias": 2.0 + nrm((L, FOX_HEADS), 0.1),
        "rwkv_mu": jax.random.uniform(next(ks), (L, RWKV_COLS), jnp.float32),
        "rwkv_w0": -1.0 + nrm((L, RWKV_W), 0.5),
        "rwkv_w2": nrm((L, DECAY_LORA, RWKV_W), 0.5 * DECAY_LORA ** -0.5),
        "rwkv_a0": nrm((L, RWKV_W), 0.1),
        "rwkv_a2": nrm((L, AAA_LORA, RWKV_W), AAA_LORA ** -0.5),
        "rwkv_g2": nrm((L, GATE_LORA, RWKV_W), GATE_LORA ** -0.5),
        "rwkv_k_k": 0.85 + nrm((L, RWKV_W), 0.05),
        "rwkv_k_a": 1.0 + nrm((L, RWKV_W), 0.05),
        "rwkv_r_k": nrm((L, RWKV_HEADS, HEAD_DIM), 0.1),
        "rwkv_ln_w": 1.0 + nrm((L, RWKV_W), 0.02),
        "rwkv_ln_b": nrm((L, RWKV_W), 0.02),
        "w_out": nrm((L, D_MIX, D), D_MIX ** -0.5),
        "norm_ffn": 1.0 + nrm((L, D), 0.02),
        "w_up": nrm((L, D, 2 * D_FF), D ** -0.5),
        "conv_w": nrm((L, CONV_W, 2 * D_FF), CONV_W ** -0.5),
        "conv_b": nrm((L, 2 * D_FF), 0.02),
        "w_down": nrm((L, D_FF, D), D_FF ** -0.5),
        "norm_final": 1.0 + nrm((D,), 0.02),
    }

def third_block(x, c, w_mod, b_mod, norm_mix, w_in, fox_f_bias, rwkv_mu, rwkv_w0, rwkv_w2, rwkv_a0, rwkv_a2,
              rwkv_g2, rwkv_k_k, rwkv_k_a, rwkv_r_k, rwkv_ln_w, rwkv_ln_b, w_out, norm_ffn, w_up, conv_w,
              conv_b, w_down, norm_final):
    c_act = jax.nn.silu(c)
    for l in range(DEPTH):
        mod = c_act @ w_mod[l] + b_mod[l]
        sh1, sc1, g1, sh2, sc2, g2 = (m[:, None, :] for m in jnp.split(mod, 6, axis=-1))
        h = _rmsnorm(x, norm_mix[l]) * (1.0 + sc1) + sh1
        p = h @ w_in[l]
        p_fox, p_rwkv, p_moba = jnp.split(p, [FOX_COLS, FOX_COLS + RWKV_COLS], axis=-1)
        fq, fk, fv, ff = jnp.split(p_fox, [FOX_W, 2 * FOX_W, 3 * FOX_W], axis=-1)
        y_fox = fox_attention(fq, fk, fv, ff, fox_f_bias[l])
        y_rwkv = rwkv7_time_mix(p_rwkv, rwkv_mu[l], rwkv_w0[l], rwkv_w2[l], rwkv_a0[l], rwkv_a2[l], rwkv_g2[l],
                                rwkv_k_k[l], rwkv_k_a[l], rwkv_r_k[l], rwkv_ln_w[l], rwkv_ln_b[l])
        mq, mk, mv = jnp.split(p_moba, [MOBA_W, 2 * MOBA_W], axis=-1)
        y_moba = moba_attention(mq, mk, mv)
        y = jnp.concatenate([y_fox.astype(x.dtype), y_rwkv.astype(x.dtype), y_moba.astype(x.dtype)], axis=-1)
        x = x + g1 * (y @ w_out[l])
        h = _rmsnorm(x, norm_ffn[l]) * (1.0 + sc2) + sh2
        u = _causal_dwconv(h @ w_up[l], conv_w[l], conv_b[l])
        u_gate, u_val = jnp.split(u, 2, axis=-1)
        x = x + g2 * ((jax.nn.silu(u_gate) * u_val) @ w_down[l])
    return _rmsnorm(x, norm_final)


_first_inputs = third_inputs


def third_inputs(seed=0):
    import zlib

    import numpy as np

    out = dict(_first_inputs(seed))
    spreads = {}
    factors = {'b_mod': 2.678,
     'norm_mix': 8.0,
     'fox_f_bias': 64.0,
     'rwkv_w2': 45.84,
     'rwkv_a0': 8.0,
     'rwkv_k_k': 200.0,
     'rwkv_k_a': 8.0,
     'rwkv_ln_w': 200.0,
     'rwkv_ln_b': 200.0,
     'norm_ffn': 64.0,
     'conv_b': 64.0,
     'norm_final': 24.253,
     'rwkv_w0': 23.788}
    for name, (base, spread) in spreads.items():
        noise = np.random.default_rng([zlib.crc32(name.encode()), seed]).standard_normal(out[name].shape)
        drawn = base * np.exp(spread * noise) if base else spread * noise
        out[name] = __import__('jax').numpy.asarray(drawn.astype(out[name].dtype))
    for name, factor in factors.items():
        out[name] = (out[name] * factor).astype(out[name].dtype)
    return out


def setup_inputs(seed=0):
    out = dict(first_inputs(seed))
    for name, value in second_inputs(seed + 1).items():
        if name != "x":
            out[name + "_2"] = value
    for name, value in third_inputs(seed + 2).items():
        if name != "x":
            out[name + "_3"] = value
    return out


def reference(
    x, c, w_ada, b_ada, g_mix, w_in, rel_bias, w_ret_o, w_att_o, w_o, g_ffn, w_router, b_router,
    w_mlp1, b_mlp1, w_mlp2, b_mlp2, g_final, attn_norm_g_2, w_in_2, q_norm_g_2, k_norm_g_2,
    lambda_vecs_2, da_subln_g_2, rel_bias_2, gla_gate_w_2, gla_gate_b_2, gla_norm_g_2, pool_w_2,
    pool_scale_2, w_out_2, ffn_norm_g_2, w_gate_2, w_up_2, w_down_2, c_3, w_mod_3, b_mod_3,
    norm_mix_3, w_in_3, fox_f_bias_3, rwkv_mu_3, rwkv_w0_3, rwkv_w2_3, rwkv_a0_3, rwkv_a2_3,
    rwkv_g2_3, rwkv_k_k_3, rwkv_k_a_3, rwkv_r_k_3, rwkv_ln_w_3, rwkv_ln_b_3, w_out_3,
    norm_ffn_3, w_up_3, conv_w_3, conv_b_3, w_down_3, norm_final_3,
):
    x = first_block(
        x, c, w_ada, b_ada, g_mix, w_in, rel_bias, w_ret_o, w_att_o, w_o, g_ffn, w_router,
        b_router, w_mlp1, b_mlp1, w_mlp2, b_mlp2, g_final,
    )
    x = second_block(
        x, attn_norm_g_2, w_in_2, q_norm_g_2, k_norm_g_2, lambda_vecs_2, da_subln_g_2,
        rel_bias_2, gla_gate_w_2, gla_gate_b_2, gla_norm_g_2, pool_w_2, pool_scale_2, w_out_2,
        ffn_norm_g_2, w_gate_2, w_up_2, w_down_2,
    )
    return third_block(
        x, c_3, w_mod_3, b_mod_3, norm_mix_3, w_in_3, fox_f_bias_3, rwkv_mu_3, rwkv_w0_3,
        rwkv_w2_3, rwkv_a0_3, rwkv_a2_3, rwkv_g2_3, rwkv_k_k_3, rwkv_k_a_3, rwkv_r_k_3,
        rwkv_ln_w_3, rwkv_ln_b_3, w_out_3, norm_ffn_3, w_up_3, conv_w_3, conv_b_3, w_down_3,
        norm_final_3,
    )


_drawn_inputs = setup_inputs


def setup_inputs(seed=0):
    import zlib

    import numpy as np

    out = dict(_drawn_inputs(seed))
    spreads = {}
    factors = {'b_mlp1': 5.074,
     'b_mlp2': 5.02,
     'rwkv_k_k_3': 6.966,
     'rwkv_ln_w_3': 8.0,
     'rwkv_ln_b_3': 8.0,
     'norm_final_3': 2.692}
    for name, (base, spread) in spreads.items():
        noise = np.random.default_rng([zlib.crc32(name.encode()), seed]).standard_normal(out[name].shape)
        drawn = base * np.exp(spread * noise) if base else spread * noise
        out[name] = jnp.asarray(drawn.astype(out[name].dtype))
    for name, factor in factors.items():
        out[name] = (out[name] * factor).astype(out[name].dtype)
    return out
```

```python
import math
from contextlib import ExitStack

import numpy as np
import concourse.bass as bass
from concourse import mybir

F32 = mybir.dt.float32
I32 = mybir.dt.int32
ALU = mybir.AluOpType
ACT = mybir.ActivationFunctionType
AX = mybir.AxisListType.X

P = 128
D = 1024
S = 512
NT = S // P
KD = D // P
RING = 8
SLOT = 2048
NEG = -1.0e30
EPS = 1e-6
GN_EPS = 1e-5
EXPERTS = 32
TOPK = 4
CAP = 128
SPILLS = S * TOPK // CAP - 1
FFN = 2816
FFN_T = FFN // P
RWKV_C = 32


class Stream:

    def __init__(self):
        self.chunks, self.span, self.slot_loads, self.landed_at = [], {}, [0] * RING, []

    def add(self, stage, chunk):
        n = len(self.chunks)
        first, _ = self.span.get(stage, (n, n))
        self.span[stage] = (first, n + 1)
        self.chunks.append(chunk)
        self.slot_loads[n % RING] += len(chunk)
        self.landed_at.append(16 * self.slot_loads[n % RING])


def columns(w, *spans):
    width = sum(n for _, n in spans)
    parts, at = [], 0
    for c0, n in spans:
        parts.append((width, at, n, w[:, c0:c0 + n].rearrange("(k p) n -> p k n", p=P)))
        at += n
    return parts


def rows(w, k0, nk, c0, n=512):
    return [(n, 0, n, w[k0 * P:(k0 + nk) * P, c0:c0 + n].rearrange("(k p) n -> p k n", p=P))]


class Kit:

    def __init__(self, nc, ctx, A, out, stream):
        self.nc, self.ctx, self.A, self.out, self.stream, self.scoped = nc, ctx, A, out, stream, []
        self.ring = self.sb(ctx, "ring", [P, RING, SLOT])
        self.x = self.sb(ctx, "x_res", [P, NT, D])
        self.hT = self.sb(ctx, "hT", [P, KD, S])
        self.ident = self.sb(ctx, "identity", [P, P])
        self.ones = self.sb(ctx, "ones", [P, P])
        self.ps = ctx.enter_context(nc.psum_tensor("psum", [P, 8, 512], F32))
        self.landed = [self.sem(f"slot{i}_landed") for i in range(RING)]
        self.chunk_used = self.sem("chunk_used")
        self.act_evac, self.act_evac_n = self.sem("act_evac"), 0
        self.dve_evac, self.dve_evac_n = self.sem("dve_evac"), 0
        self.act_order, self.act_order_n = self.sem("act_order"), 0
        self.dve_order, self.dve_order_n = self.sem("dve_order"), 0
        self.loads, self.loads_n = self.sem("loads"), 0
        self.stores, self.stores_n = self.sem("stores"), 0

    def sb(self, ctx, name, shape, dt=F32):
        return ctx.enter_context(self.nc.sbuf_tensor(name, shape, dt))

    def sem(self, name):
        sem = self.ctx.enter_context(self.nc.semaphore(name))
        self.scoped.append(sem)
        return sem

    def scope(self, run):
        self.scoped = []
        with ExitStack() as ctx:
            outer, self.ctx = self.ctx, ctx
            run(self)
            with self.nc.Block() as block:
                @block.sync
                def _(sp):
                    for sem in self.scoped:
                        sp.sem_clear(sem)
            self.ctx = outer

    def load(self, eng, dst, src, **kw):
        eng.dma_start(dst, src, **kw).then_inc(self.loads, 16)
        self.loads_n += 16

    def store(self, eng, dst, src, **kw):
        eng.dma_start(dst, src, **kw).then_inc(self.stores, 16)
        self.stores_n += 16

    def act_link(self, ins):
        self.act_order_n += 1
        ins.then_inc(self.act_order, 1)
        self.nc.scalar.wait_ge(self.act_order, self.act_order_n)

    def dve_link(self, ins):
        self.dve_order_n += 1
        ins.then_inc(self.dve_order, 1)
        self.nc.vector.wait_ge(self.dve_order, self.dve_order_n)

    def slot(self, n, width=512):
        return self.ring[:, n % RING, :].rearrange("p (k n) -> p k n", n=width)

    def issue(self, sp, n):
        for width, at, cols, src in self.stream.chunks[n]:
            nk = src.shape[1]
            dst = self.ring[:, n % RING, 0:nk * width].rearrange("p (k n) -> p k n", n=width)
            sp.dma_start(dst[:, :, at:at + cols], src).then_inc(self.landed[n % RING], 16)

    def refill(self, sp, first, last):
        for n in range(first, last):
            if n + RING < len(self.stream.chunks):
                sp.wait_ge(self.chunk_used, n + 1)
                self.issue(sp, n + RING)

    def wait_chunk(self, pe, n):
        pe.wait_ge(self.landed[n % RING], self.stream.landed_at[n])

    def use_T(self, pe, n, width, tile, src, out, last, m=P, sub=slice(None), nk=KD):
        w = self.slot(n, width)
        for k in range(nk):
            ins = self.nc.tensor.matmul(out, w[:, k, tile * P:tile * P + m], src[:, k, sub], start=(k == 0),
                                        stop=(k == nk - 1))
        if last:
            ins.then_inc(self.chunk_used, 1)
        return ins


def linear(K, stage, kind, src, per_unit, act=None, dve=None, act_runs_ahead=2):
    nc = K.nc
    first, last = K.stream.span[stage]
    units = (last - first) // per_unit
    assert units * per_unit == last - first
    banks = 2 * per_unit if kind == "T" else NT
    flight = 8 // banks
    freed, freed0 = (K.dve_evac, K.dve_evac_n) if dve else (K.act_evac, K.act_evac_n)
    act0, dve0 = K.act_evac_n, K.dve_evac_n

    def unit_banks(j):
        b = (j % flight) * banks
        return K.ps[:, b:b + banks, :]

    with nc.Block() as block:
        @block.sync
        def _(sp):
            K.refill(sp, first, last)

        @block.tensor
        def _(pe):
            for j in range(units):
                if j >= flight:
                    pe.wait_ge(freed, freed0 + j - flight + 1)
                out = unit_banks(j)
                k0 = 0
                total = sum(K.stream.chunks[first + j * per_unit + c][0][3].shape[1] for c in range(per_unit))
                for c in range(per_unit):
                    n = first + j * per_unit + c
                    K.wait_chunk(pe, n)
                    width = K.stream.chunks[n][0][0]
                    nk = K.stream.chunks[n][0][3].shape[1]
                    if kind == "T":
                        K.use_T(pe, n, width, 0, src, out[:, 2 * c, :], False)
                        K.use_T(pe, n, width, 1, src, out[:, 2 * c + 1, :], True)
                        continue
                    w = K.slot(n, width)
                    for t in range(NT):
                        for k in range(nk):
                            ins = nc.tensor.matmul(out[:, t, 0:width], src[:, k0 + k, t * P:(t + 1) * P], w[:, k, :],
                                                   start=(k0 + k == 0), stop=(k0 + k == total - 1))
                    ins.then_inc(K.chunk_used, 1)
                    k0 += nk

        if act:
            @block.scalar
            def _(sc):
                for j in range(units):
                    sc.wait_ge(K.chunk_used, first + (j + 1) * per_unit)
                    if dve and j >= act_runs_ahead:
                        sc.wait_ge(K.dve_evac, dve0 + j - act_runs_ahead + 1)
                    act(j, unit_banks(j)).then_inc(K.act_evac, 1)

        if dve:
            @block.vector
            def _(ve):
                for j in range(units):
                    if act:
                        ve.wait_ge(K.act_evac, act0 + j + 1)
                    ve.wait_ge(K.chunk_used, first + (j + 1) * per_unit)
                    dve(j, unit_banks(j)).then_inc(K.dve_evac, 1)
    if act:
        K.act_evac_n += units
    if dve:
        K.dve_evac_n += units


def load_columns(K, name, vectors, ctx):
    nc = K.nc
    at, r = {}, 0
    for key, v in vectors:
        at[key] = r
        r += v.shape[0] // P
    assert r <= P
    cols = K.sb(ctx, name, [P, r])
    turned, copied = K.sem(f"{name}_turned"), K.sem(f"{name}_copied")
    with nc.sbuf_tensor(f"{name}_rows", [P, P], F32) as raw:
        with nc.Block() as block:
            @block.sync
            def _(sp):
                for key, v in vectors:
                    n = v.shape[0] // P
                    K.load(sp, raw[at[key]:at[key] + n, :], v.rearrange("(k p) -> k p", p=P))

            @block.tensor
            def _(pe):
                pe.wait_ge(K.loads, K.loads_n)
                nc.tensor.transpose(K.ps[:, 0, 0:r], raw[0:r, :], K.ident[0:r, 0:r]).then_inc(turned, 1)

            @block.vector
            def _(ve):
                ve.wait_ge(turned, 1)
                nc.vector.tensor_copy(cols[:, :], K.ps[:, 0, 0:r]).then_inc(copied, 1)
    return cols, at


def modulation(K, stage, c_cols, bias, gates, scale1, shift1, scale2, shift2, g1, g2):
    nc = K.nc
    first, last = K.stream.span[stage]
    sig_done, cs_done, evac = K.sem(f"{stage}_sig"), K.sem(f"{stage}_cs"), K.sem(f"{stage}_evac")
    with ExitStack() as ctx:
        sg = K.sb(ctx, f"{stage}_sg", [P, KD])
        cs = K.sb(ctx, f"{stage}_c", [P, KD, P])
        cv = K.sb(ctx, f"{stage}_cv", [P, KD])
        brow = K.sb(ctx, f"{stage}_b", [P, 512])
        sel = K.sb(ctx, f"{stage}_sel", [P, 12, P])
        diag = K.sb(ctx, f"{stage}_diag", [P, 4, P])
        cols = K.sb(ctx, f"{stage}_cols", [P, 6, KD])
        with nc.Block() as block:
            @block.sync
            def _(sp):
                K.load(sp, brow[0:12, :], bias.rearrange("(s n) -> s n", n=512))
                K.refill(sp, first, last)

            @block.scalar
            def _(sc):
                nc.scalar.activation(sg[:, :], c_cols, ACT.Sigmoid).then_inc(sig_done, 1)

            @block.tensor
            def _(pe):
                pe.wait_ge(cs_done, 1)
                pe.wait_ge(K.loads, K.loads_n)
                for s in range(12):
                    if s >= 8:
                        pe.wait_ge(evac, s - 7)
                    out = K.ps[:, s % 8, :]
                    nc.tensor.matmul(out, sel[0:12, s, :], brow[0:12, :], start=True, stop=False)
                    for c in range(2):
                        n = first + 2 * s + c
                        K.wait_chunk(pe, n)
                        for k in range(4):
                            ins = nc.tensor.matmul(out, cs[:, 4 * c + k, :], K.slot(n)[:, k, :], start=False,
                                                   stop=(c == 1 and k == 3))
                        ins.then_inc(K.chunk_used, 1)

            @block.vector
            def _(ve):
                ve.wait_ge(sig_done, 1)
                K.dve_link(nc.vector.tensor_tensor(cv[:, :], sg[:, :], c_cols, ALU.mult))
                nc.vector.tensor_copy(sel[:, :, :], K.ident[:, 0:12].unsqueeze(2).to_broadcast([P, 12, P]))
                nc.vector.tensor_copy(cs[:, :, :], cv[:, :].unsqueeze(2).to_broadcast([P, KD, P])).then_inc(cs_done, 1)
                for s in range(12):
                    ve.wait_ge(K.chunk_used, first + 2 * s + 2)
                    out, sec, half = K.ps[:, s % 8, :], s // 2, s % 2
                    if sec in (2, 5):
                        nc.vector.tensor_copy(gates[:, sec // 3, half * 512:(half + 1) * 512], out).then_inc(evac, 1)
                        continue
                    K.dve_link(nc.vector.tensor_tensor(diag[:, :, :], out.rearrange("p (k q) -> p k q", q=P),
                                                       K.ident[:, :].unsqueeze(1).to_broadcast([P, 4, P]), ALU.mult))
                    K.dve_link(nc.vector.tensor_reduce(cols[:, sec, half * 4:half * 4 + 4], diag[:, :, :], AX,
                                                       ALU.add))
                    nc.vector.tensor_copy(sg[:, 0:1], cols[:, sec, 0:1]).then_inc(evac, 1)
                for scale, shift, g, sec in ((scale1, shift1, g1, 0), (scale2, shift2, g2, 3)):
                    K.dve_link(nc.vector.tensor_copy(shift, cols[:, sec, :]))
                    K.dve_link(nc.vector.scalar_tensor_tensor(scale, cols[:, sec + 1, :], 1.0, g, ALU.add, ALU.mult))




def normalise(K, name, xn, scale, shift, dst):
    nc = K.nc
    squared, var, root, normed, turned = (K.sem(f"{name}_{s}") for s in ("squared", "var", "root", "normed", "turned"))
    with ExitStack() as ctx:
        ss = K.sb(ctx, f"{name}_ss", [P, NT])
        sd = K.sb(ctx, f"{name}_sd", [P, NT])
        with nc.Block() as block:
            @block.scalar
            def _(sc):
                for t in range(NT):
                    ins = nc.scalar.activation(xn[:, t, :], K.x[:, t, :], ACT.Square, accum_out=ss[:, t:t + 1])
                ins.then_inc(squared, 1)
                sc.wait_ge(var, 1)
                nc.scalar.activation(sd[:, :], ss[:, :], ACT.Sqrt).then_inc(root, 1)
                for k in range(0, KD, 2):
                    sc.wait_ge(turned, k + 1)
                    bias = shift[:, k:k + 1] if shift is not None else 0.0
                    nc.scalar.activation(dst[:, k, :], K.ps[:, k, :], ACT.Identity, scale=scale[:, k:k + 1], bias=bias)

            @block.vector
            def _(ve):
                ve.wait_ge(squared, 1)
                nc.vector.tensor_scalar(ss[:, :], ss[:, :], 1.0 / D, EPS, ALU.mult, ALU.add).then_inc(var, 1)
                ve.wait_ge(root, 1)
                K.dve_link(nc.vector.reciprocal(ss[:, :], sd[:, :]))
                for t in range(NT):
                    nc.vector.tensor_scalar(xn[:, t, :], K.x[:, t, :], ss[:, t:t + 1], None, ALU.mult)\
                        .then_inc(normed, 1)
                for k in range(1, KD, 2):
                    ve.wait_ge(turned, k + 1)
                    if shift is not None:
                        nc.vector.tensor_scalar(dst[:, k, :], K.ps[:, k, :], scale[:, k:k + 1], shift[:, k:k + 1],
                                                ALU.mult, ALU.add)
                    else:
                        nc.vector.tensor_scalar(dst[:, k, :], K.ps[:, k, :], scale[:, k:k + 1], None, ALU.mult)

            @block.tensor
            def _(pe):
                pe.wait_ge(normed, NT)
                for k in range(KD):
                    for t in range(NT):
                        ins = nc.tensor.transpose(K.ps[:, k, t * P:(t + 1) * P], xn[:, t, k * P:(k + 1) * P],
                                                  K.ident[:, :])
                    ins.then_inc(turned, 1)


def final_norm(K, name, gain, write_out):
    nc = K.nc
    squared, var, root, done = (K.sem(f"{name}_{s}") for s in ("squared", "var", "root", "done"))
    with ExitStack() as ctx:
        ss = K.sb(ctx, f"{name}_ss", [P, NT])
        sd = K.sb(ctx, f"{name}_sd", [P, NT])
        gb = K.sb(ctx, f"{name}_g", [P, D])
        junk = K.sb(ctx, f"{name}_junk", [P, D])
        with nc.Block() as block:
            @block.sync
            def _(sp):
                K.load(sp, gb[:, :], gain.rearrange("(a n) -> a n", a=1).partition_broadcast(P))
                if write_out:
                    for t in range(NT):
                        sp.wait_ge(done, t + 1)
                        K.store(sp, K.out[0, t * P:(t + 1) * P, :], K.x[:, t, :])
                    sp.wait_ge(K.stores, K.stores_n)

            @block.scalar
            def _(sc):
                for t in range(NT):
                    if t:
                        sc.wait_ge(squared, t)
                    nc.scalar.activation(junk[:, :], K.x[:, t, :], ACT.Square, accum_out=ss[:, t:t + 1])\
                        .then_inc(squared, 1)
                sc.wait_ge(var, 1)
                nc.scalar.activation(sd[:, :], ss[:, :], ACT.Sqrt).then_inc(root, 1)

            @block.vector
            def _(ve):
                ve.wait_ge(squared, NT)
                nc.vector.tensor_scalar(ss[:, :], ss[:, :], 1.0 / D, EPS, ALU.mult, ALU.add).then_inc(var, 1)
                ve.wait_ge(root, 1)
                ve.wait_ge(K.loads, K.loads_n)
                K.dve_link(nc.vector.reciprocal(ss[:, :], sd[:, :]))
                for t in range(NT):
                    nc.vector.scalar_tensor_tensor(K.x[:, t, :], K.x[:, t, :], ss[:, t:t + 1], gb[:, :],
                                                   ALU.mult, ALU.mult).then_inc(done, 1)


def add_residual(K, stage, src, per_unit, gate=None):
    nc = K.nc

    def dve(j, banks):
        x = K.x[:, :, j * 512:(j + 1) * 512]
        if gate is not None:
            g = gate[:, j * 512:(j + 1) * 512].unsqueeze(1).to_broadcast([P, NT, 512])
            K.dve_link(nc.vector.tensor_tensor(banks, banks, g, ALU.mult))
        return nc.vector.tensor_tensor(x, banks, x, ALU.add)

    linear(K, stage, "N", src, per_unit, dve=dve)



RH, RDK, RDV = 4, 128, 256
AH, AG = 4, 3
RQ, RK_, RV, RG = 0, RH * RDK, 2 * RH * RDK, 2 * RH * RDK + RH * RDV
AQ = RG + RH * RDV
AK_ = AQ + AG * AH * P
AV = AK_ + AG * AH * P
GA = AV + AG * AH * P
GB = GA + D
T0W = 4 * P + 3
T12W = 2 * P


def plan_block1(st, A):
    w_ada, w_in = A["w_ada"][0], A["w_in"][0]
    for s in range(12):
        for c in range(2):
            st.add("mod1", rows(w_ada, 4 * c, 4, 512 * s))
    for h in range(RH):
        st.add("ret", columns(w_in, (RQ + h * RDK, RDK), (RK_ + h * RDK, RDK)))
        st.add("ret", columns(w_in, (RV + h * RDV, RDV)))
        st.add("ret", columns(w_in, (RG + h * RDV, RDV)))
    for i in range(4):
        st.add("gate_a", columns(w_in, (GA + 256 * i, 256)))
    for i in range(4):
        st.add("ret_o", columns(A["w_ret_o"][0], (256 * i, 256)))
    for h in range(AH):
        for g in range(AG):
            st.add("att", columns(w_in, (AQ + (g * AH + h) * P, P), (AK_ + (g * AH + h) * P, P)))
        st.add("att", columns(w_in, (AV + h * P, P), (AV + (AH + h) * P, P)))
        st.add("att", columns(w_in, (AV + (2 * AH + h) * P, P)))
    for i in range(4):
        st.add("gate_b", columns(w_in, (GB + 256 * i, 256)))
    for i in range(2):
        st.add("att_o", rows(A["w_att_o"][0], 0, 4, 512 * i))
    for j in range(2):
        for c in range(2):
            st.add("w_o", rows(A["w_o"][0], 4 * c, 4, 512 * j))
    for e in range(EXPERTS):
        for chunk in expert_chunks(A, e):
            st.add("moe", chunk)


def expert_chunks(A, e):
    w1, w2 = A["w_mlp1"][0, e], A["w_mlp2"][0, e]
    up = [rows(w1, 4 * c, 4, 512 * j) for j in range(4) for c in range(2)]
    down = [rows(w2, 4 * c, 4, 512 * j) for j in range(2) for c in range(2)]
    return up + down


def retention(K, retT):
    nc, A = K.nc, K.A
    first, _ = K.stream.span["ret"]
    raw_done, rot_done, turn_done = K.sem("ret_raw"), K.sem("ret_rot"), K.sem("ret_turned")
    sc_done, mask_done, y_done = K.sem("ret_scores"), K.sem("ret_masked"), K.sem("ret_y")
    var_done, sd_done, ret_done = K.sem("ret_var"), K.sem("ret_sd"), K.sem("ret_normed")
    tr_done, out_done, g_done = K.sem("ret_transposed"), K.sem("ret_copied"), K.sem("ret_gated")
    with ExitStack() as ctx:
        cos = K.sb(ctx, "rope_cos", [P, S])
        sin = K.sb(ctx, "rope_sin", [P, S])
        rot = K.sb(ctx, "rope_rot", [P, P])
        decay = K.sb(ctx, "decay", [P, RH, NT, P])
        raw = K.sb(ctx, "qk_raw", [P, 2, S])
        qk = K.sb(ctx, "qk_rot", [P, 2, S])
        t1 = K.sb(ctx, "rope_t1", [P, 2, S])
        v = K.sb(ctx, "ret_v", [P, NT, RDV])
        sg = K.sb(ctx, "ret_sg", [P, NT, RDV])
        pt = K.sb(ctx, "ret_pt", [P, NT, S])
        y = K.sb(ctx, "ret_yn", [P, NT, RDV])
        stats = K.sb(ctx, "ret_stats", [P, NT, 6])
        mv = K.sb(ctx, "ret_mv", [P, NT, 2])
        sd = K.sb(ctx, "ret_sdv", [P, NT])
        ps = K.ps
        with nc.Block() as block:
            @block.sync
            def _(sp):
                for dst, key in ((cos, "k_cos"), (sin, "k_sin"), (rot, "k_rot")):
                    K.load(sp, dst[:, :], A[key])
                K.load(sp, decay[:, :, :, :], A["k_decay"])
                K.refill(sp, first, first + 3 * RH)

            @block.tensor
            def _(pe):
                pe.wait_ge(K.loads, K.loads_n)
                for h in range(RH):
                    n = first + 3 * h
                    if h:
                        pe.wait_ge(out_done, h)
                    K.wait_chunk(pe, n)
                    K.use_T(pe, n, 256, 0, K.hT, ps[:, 0, :], False)
                    K.use_T(pe, n, 256, 1, K.hT, ps[:, 1, :], True)
                    if h:
                        pe.wait_ge(ret_done, h)
                    for c in (1, 2):
                        K.wait_chunk(pe, n + c)
                        w = K.slot(n + c, 256)
                        for t in range(NT):
                            out = ps[:, 2 + 2 * c + t // 2, (t % 2) * 256:(t % 2) * 256 + 256]
                            for k in range(KD):
                                ins = nc.tensor.matmul(out, K.hT[:, k, t * P:(t + 1) * P], w[:, k, :],
                                                       start=(k == 0), stop=(k == KD - 1))
                        ins.then_inc(K.chunk_used, 1)
                    pe.wait_ge(raw_done, 2 * h + 1)
                    for i in range(2):
                        ins = nc.tensor.matmul(ps[:, 2 + i, :], rot[:, :], raw[:, i, :], start=True, stop=True)
                    ins.then_inc(turn_done, 1)
                    pe.wait_ge(rot_done, h + 1)
                    for j in range(NT):
                        ins = nc.tensor.matmul(ps[:, j, j * P:], qk[:, 1, j * P:(j + 1) * P], qk[:, 0, j * P:],
                                               start=True, stop=True)
                        ins.then_inc(sc_done, 1)
                    pe.wait_ge(raw_done, 2 * h + 2)
                    pe.wait_ge(mask_done, NT * (h + 1))
                    for i in range(NT):
                        for j in range(i + 1):
                            ins = nc.tensor.matmul(ps[:, 4 + i // 2, (i % 2) * 256:(i % 2) * 256 + 256],
                                                   pt[:, j, i * P:(i + 1) * P], v[:, j, :],
                                                   start=(j == 0), stop=(j == i))
                    ins.then_inc(y_done, 1)
                    pe.wait_ge(ret_done, h + 1)
                    for e in range(2):
                        for t in range(NT):
                            ins = nc.tensor.transpose(ps[:, e, t * P:(t + 1) * P], y[:, t, e * P:(e + 1) * P],
                                                      K.ident[:, :])
                    ins.then_inc(tr_done, 1)

            @block.scalar
            def _(sc):
                for h in range(RH):
                    sc.wait_ge(K.chunk_used, first + 3 * h + 1)
                    if h:
                        sc.wait_ge(rot_done, h)
                    nc.scalar.activation(raw[:, :, :], ps[:, 0:2, :], ACT.Copy).then_inc(raw_done, 1)
                    sc.wait_ge(K.chunk_used, first + 3 * h + 2)
                    if h:
                        sc.wait_ge(y_done, h)
                    nc.scalar.activation(v[:, :, :].rearrange("p t n -> p (t n)"),
                                         ps[:, 4:6, :].rearrange("p t n -> p (t n)"), ACT.Copy).then_inc(raw_done, 1)
                    sc.wait_ge(K.chunk_used, first + 3 * h + 3)
                    if h:
                        sc.wait_ge(ret_done, h)
                    nc.scalar.activation(sg[:, :, :].rearrange("p t n -> p (t n)"),
                                         ps[:, 6:8, :].rearrange("p t n -> p (t n)"), ACT.Sigmoid).then_inc(g_done, 1)
                    sc.wait_ge(var_done, h + 1)
                    nc.scalar.activation(sd[:, :], mv[:, :, 1], ACT.Sqrt).then_inc(sd_done, 1)
                    sc.wait_ge(tr_done, h + 1)
                    nc.scalar.activation(retT[:, 2 * h:2 * h + 2, :], ps[:, 0:2, :], ACT.Copy).then_inc(out_done, 1)

            @block.vector
            def _(ve):
                ve.wait_ge(K.loads, K.loads_n)
                for h in range(RH):
                    ve.wait_ge(raw_done, 2 * h + 1)
                    K.dve_link(nc.vector.tensor_tensor(t1[:, :, :], raw[:, :, :],
                                                       cos[:, :].unsqueeze(1).to_broadcast([P, 2, S]), ALU.mult))
                    ve.wait_ge(turn_done, h + 1)
                    if h:
                        ve.wait_ge(sc_done, NT * h)
                    K.dve_link(nc.vector.tensor_tensor(qk[:, :, :], ps[:, 2:4, :],
                                                       sin[:, :].unsqueeze(1).to_broadcast([P, 2, S]), ALU.mult))
                    nc.vector.tensor_tensor(qk[:, :, :], qk[:, :, :], t1[:, :, :], ALU.add).then_inc(rot_done, 1)
                    if h:
                        ve.wait_ge(y_done, h)
                    for j in range(NT):
                        ve.wait_ge(sc_done, NT * h + j + 1)
                        w = S - j * P
                        nc.vector.tensor_tensor(pt[:, j, j * P:], ps[:, j, j * P:],
                                                decay[:, h, :, :].rearrange("p a b -> p (a b)")[:, 0:w],
                                                ALU.mult).then_inc(mask_done, 1)
                    ve.wait_ge(g_done, h + 1)
                    K.dve_link(nc.vector.tensor_tensor(sg[:, :, :].rearrange("p t n -> p (t n)"),
                                                       sg[:, :, :].rearrange("p t n -> p (t n)"),
                                                       ps[:, 6:8, :].rearrange("p t n -> p (t n)"), ALU.mult))
                    ve.wait_ge(y_done, h + 1)
                    yp = ps[:, 4:6, :].rearrange("p t (a n) -> p (t a) n", n=RDV)
                    for t in range(NT):
                        K.dve_link(nc.vector.bn_stats(stats[:, t, :], yp[:, t, :]))
                        K.dve_link(nc.vector.bn_aggr(mv[:, t, :], stats[:, t, :]))
                    nc.vector.tensor_scalar(mv[:, :, 1], mv[:, :, 1], 1.0, GN_EPS, ALU.mult, ALU.add)\
                        .then_inc(var_done, 1)
                    ve.wait_ge(sd_done, h + 1)
                    K.dve_link(nc.vector.reciprocal(sd[:, :], sd[:, :]))
                    if h:
                        ve.wait_ge(tr_done, h)
                    for t in range(NT):
                        K.dve_link(nc.vector.tensor_scalar(y[:, t, :], yp[:, t, :], mv[:, t, 0:1], sd[:, t:t + 1],
                                                           ALU.subtract, ALU.mult))
                    nc.vector.tensor_tensor(y[:, :, :], y[:, :, :], sg[:, :, :], ALU.mult).then_inc(ret_done, 1)


def sigmoid_gate(K, stage, dst):
    linear(K, stage, "T", K.hT, 1,
           act=lambda j, banks: K.nc.scalar.activation(dst[:, 2 * j:2 * j + 2, :], banks, ACT.Sigmoid))


def bias_tables(K, name, rel, hot_dram, jobs, heads):
    nc = K.nc
    row_done, ready, copied = K.sem(f"{name}_row"), K.sem(f"{name}_ready"), K.sem(f"{name}_copied")
    written, loads0 = [K.sem(f"{name}_written{i}") for i in range(2)], K.loads_n
    scratch = nc.dram_tensor(f"{name}_rows", (len(jobs), P * 1024), F32, kind="Internal").ap()
    with ExitStack() as ctx:
        rb = K.sb(ctx, f"{name}_rel", [33, heads])
        rbb = K.sb(ctx, f"{name}_relb", [33, heads, P])
        hot = K.sb(ctx, f"{name}_hot", [33, hot_dram.shape[1]])
        row = K.sb(ctx, f"{name}_rowb", [P, 2, 1024])
        with nc.Block() as block:
            @block.sync
            def _(sp):
                K.load(sp, rb[0:32, :], rel)
                K.load(sp, hot[:, :], hot_dram)
                for i, (_, _, w, _, _, _) in enumerate(jobs):
                    sp.wait_ge(copied, i + 1)
                    sp.dma_start(scratch[i, 0:P * w].rearrange("(p w) -> p w", w=w), row[:, i % 2, 0:w])\
                        .then_inc(written[i % 2], 16)
                for i, (_, _, w, step, base, table) in enumerate(jobs):
                    if i == 0:
                        for b in range(2):
                            sp.wait_ge(written[b], 16 * ((len(jobs) + 1 - b) // 2))
                    src = scratch[i, base:base + P * (w - step)].rearrange("(p w) -> p w", w=w - step)
                    K.load(sp, table, src[:, 0:table.shape[1]])
                sp.wait_ge(K.loads, K.loads_n)

            @block.vector
            def _(ve):
                nc.vector.memset(rb[32:33, :], NEG).then_inc(ready, 1)
                ve.wait_ge(ready, 1)
                ve.wait_ge(K.loads, loads0 + 32)
                nc.vector.tensor_copy(rbb[:, :, :], rb[:, :].unsqueeze(2).to_broadcast([33, heads, P]))\
                    .then_inc(ready, 1)
                for i, (_, _, w, _, _, _) in enumerate(jobs):
                    ve.wait_ge(row_done, i + 1)
                    if i >= 2:
                        ve.wait_ge(written[i % 2], 16 * (i // 2))
                    b = 2 * (i % 4)
                    nc.vector.tensor_copy(row[:, i % 2, 0:w],
                                          K.ps[:, b:b + 2, :].rearrange("p a n -> p (a n)")[:, 0:w]).then_inc(copied, 1)

            @block.tensor
            def _(pe):
                pe.wait_ge(ready, 2)
                for i, (head, q0, w, _, _, _) in enumerate(jobs):
                    if i >= 4:
                        pe.wait_ge(copied, i - 3)
                    for c in range(0, w, 512):
                        n = min(512, w - c)
                        ins = nc.tensor.matmul(K.ps[:, 2 * (i % 4) + c // 512, 0:n], rbb[:, head, :],
                                               hot[:, q0 + c:q0 + c + n], start=True, stop=True)
                    ins.then_inc(row_done, 1)


def dilated(K, attT, T0, T12):
    nc = K.nc
    first, _ = K.stream.span["att"]
    names = "proj scores softmax transposed pT av norm oT copied summed maxed".split()
    proj, scores, softmax, transposed, p_ready, av, norm, o_turned, copied, biased, maxed = (
        K.sem(f"att_{n}") for n in names)
    scale = float(P) ** -0.5
    ps = K.ps
    with ExitStack() as ctx:
        qk = K.sb(ctx, "att_qk", [P, 6, S])
        v = K.sb(ctx, "att_v", [P, AG, NT, P])
        s = K.sb(ctx, "att_s", [P, 2, 6 * P])
        pT = K.sb(ctx, "att_pT", [P, 6 * P])
        o = K.sb(ctx, "att_o_tok", [P, P])
        nm = K.sb(ctx, "att_negmax", [P, 2])
        l = K.sb(ctx, "att_sum", [P, 2])
        with nc.Block() as block:
            @block.sync
            def _(sp):
                K.refill(sp, first, first + 5 * AH)

            @block.tensor
            def _(pe):
                def score(u):
                    c = u % 4
                    if u >= 2:
                        pe.wait_ge(biased, 2 * (u - 1))
                    b = 2 * (u % 2)
                    nc.tensor.matmul(ps[:, b, :], qk[:, 0, c::4], qk[:, 1, :], start=True, stop=True)
                    nc.tensor.matmul(ps[:, b + 1, 0:P], qk[:, 2, c::4], qk[:, 3, c::4], start=True, stop=True)
                    nc.tensor.matmul(ps[:, b + 1, P:2 * P], qk[:, 4, c::4], qk[:, 5, c::4], start=True, stop=True)\
                        .then_inc(scores, 1)

                for h in range(AH):
                    n = first + 5 * h
                    if h:
                        pe.wait_ge(copied, 4 * h)
                    for g in range(AG):
                        K.wait_chunk(pe, n + g)
                        K.use_T(pe, n + g, 256, 0, K.hT, ps[:, 2 * g, :], False)
                        K.use_T(pe, n + g, 256, 1, K.hT, ps[:, 2 * g + 1, :], True)
                    for g in range(AG):
                        if g < 2:
                            K.wait_chunk(pe, n + 3)
                            w, bank = K.slot(n + 3, 256)[:, :, g * P:(g + 1) * P], 6 + g
                        else:
                            K.wait_chunk(pe, n + 4)
                            pe.wait_ge(proj, 5 * h + 1)
                            w, bank = K.slot(n + 4, P), 0
                        for t in range(NT):
                            for k in range(KD):
                                lhs = K.hT[:, k, t * P:(t + 1) * P] if g == 0 else K.hT[:, k, t::4]
                                ins = nc.tensor.matmul(ps[:, bank, t * P:(t + 1) * P], lhs, w[:, k, 0:P],
                                                       start=(k == 0), stop=(k == KD - 1))
                        if g:
                            ins.then_inc(K.chunk_used, 1)
                    pe.wait_ge(proj, 5 * h + 5)
                    score(4 * h)
                    for c in range(4):
                        u = 4 * h + c
                        if c < 3:
                            score(u + 1)
                        pe.wait_ge(softmax, u + 1)
                        for j in range(6):
                            ins = nc.tensor.transpose(ps[:, 4 + j // 4, (j % 4) * P:(j % 4 + 1) * P],
                                                      s[:, u % 2, j * P:(j + 1) * P], K.ident[:, :])
                        ins.then_inc(transposed, 1)
                        pe.wait_ge(p_ready, u + 1)
                        for j in range(6):
                            rhs = v[:, 0, j, :] if j < 4 else v[:, j - 3, c, :]
                            ins = nc.tensor.matmul(ps[:, 6, 0:P], pT[:, j * P:(j + 1) * P], rhs, start=(j == 0),
                                                   stop=(j == 5))
                        ins.then_inc(av, 1)
                        pe.wait_ge(norm, u + 1)
                        nc.tensor.transpose(ps[:, 7, 0:P], o[:, :], K.ident[:, :]).then_inc(o_turned, 1)

            @block.scalar
            def _(sc):
                for h in range(AH):
                    for g in range(AG):
                        sc.wait_ge(K.chunk_used, first + 5 * h + g + 1)
                        if h:
                            sc.wait_ge(scores, 4 * h)
                        nc.scalar.activation(qk[:, 2 * g:2 * g + 2, :], ps[:, 2 * g:2 * g + 2, :], ACT.Copy)\
                            .then_inc(proj, 1)
                    sc.wait_ge(K.chunk_used, first + 5 * h + 4)
                    nc.scalar.activation(v[:, 0:2, :, :].rearrange("p a b c -> p (a b c)"),
                                         ps[:, 6:8, :].rearrange("p a b -> p (a b)"), ACT.Copy).then_inc(proj, 1)
                    sc.wait_ge(K.chunk_used, first + 5 * h + 5)
                    nc.scalar.activation(v[:, 2, :, :].rearrange("p b c -> p (b c)"), ps[:, 0, :], ACT.Copy)\
                        .then_inc(proj, 1)
                    for c in range(4):
                        u = 4 * h + c
                        sc.wait_ge(maxed, u + 1)
                        nc.scalar.activation(s[:, u % 2, :], s[:, u % 2, :], ACT.Exp, bias=nm[:, u % 2:u % 2 + 1],
                                             scale=1.0, accum_out=l[:, u % 2:u % 2 + 1]).then_inc(softmax, 1)
                        sc.wait_ge(transposed, u + 1)
                        if u:
                            sc.wait_ge(av, u)
                        nc.scalar.activation(pT[:, :], ps[:, 4:6, :].rearrange("p a n -> p (a n)")[:, 0:6 * P],
                                             ACT.Copy).then_inc(p_ready, 1)
                        sc.wait_ge(o_turned, u + 1)
                        nc.scalar.activation(attT[:, h, c::4], ps[:, 7, 0:P], ACT.Copy).then_inc(copied, 1)

            @block.vector
            def _(ve):
                def soften(u):
                    h, c, b = u // 4, u % 4, 2 * (u % 2)
                    ve.wait_ge(scores, u + 1)
                    if u >= 2:
                        ve.wait_ge(transposed, u - 1)
                    nc.vector.scalar_tensor_tensor(s[:, u % 2, 0:S], ps[:, b, :], scale, T0[:, h, 3 - c:3 - c + S],
                                                   ALU.mult, ALU.add).then_inc(biased, 1)
                    nc.vector.scalar_tensor_tensor(s[:, u % 2, S:], ps[:, b + 1, 0:2 * P], scale, T12[:, h, :],
                                                   ALU.mult, ALU.add).then_inc(biased, 1)
                    ve.wait_ge(biased, 2 * (u + 1))
                    K.dve_link(nc.vector.tensor_reduce(nm[:, u % 2:u % 2 + 1], s[:, u % 2, :], AX, ALU.max))
                    nc.vector.tensor_scalar(nm[:, u % 2:u % 2 + 1], nm[:, u % 2:u % 2 + 1], -1.0, None, ALU.mult)\
                        .then_inc(maxed, 1)

                for h in range(AH):
                    soften(4 * h)
                    for c in range(4):
                        u = 4 * h + c
                        if c < 3:
                            soften(u + 1)
                        ve.wait_ge(softmax, u + 1)
                        K.dve_link(nc.vector.reciprocal(l[:, u % 2:u % 2 + 1], l[:, u % 2:u % 2 + 1]))
                        ve.wait_ge(av, u + 1)
                        if u:
                            ve.wait_ge(o_turned, u)
                        nc.vector.tensor_scalar(o[:, :], ps[:, 6, 0:P], l[:, u % 2:u % 2 + 1], None, ALU.mult)\
                            .then_inc(norm, 1)


def route(K, wr, br, posm, gate, extra):
    nc = K.nc
    A = K.A
    logit_done, masked, placed = K.sem("rt_logits"), K.sem("rt_masked"), K.sem("rt_placed")
    exp_in, exp_out, loads0, counted = K.sem("rt_expin"), K.sem("rt_expout"), K.loads_n, K.sem("rt_counted")
    E = EXPERTS
    with ExitStack() as ctx:
        w = K.sb(ctx, "rt_w", [P, KD, E])
        b = K.sb(ctx, "rt_b", [P, E])
        tri = K.sb(ctx, "rt_tri", [P, P])
        lg = K.sb(ctx, "rt_lg", [P, NT, E])
        m8 = K.sb(ctx, "rt_m8", [P, NT, 8])
        same = K.sb(ctx, "rt_same", [P, NT, E])
        mask = K.sb(ctx, "rt_mask", [P, NT, E])
        ssum = K.sb(ctx, "rt_sum", [P, NT])
        cnt = K.sb(ctx, "rt_cnt", [P, E])
        spans = S // CAP - 1
        held = K.sb(ctx, "rt_held", [P, E * spans])
        rank = K.sb(ctx, "rt_rank", [P, E * spans])
        code = K.sb(ctx, "rt_code", [P, 2, E * spans])
        number = K.sb(ctx, "rt_number", [P, SPILLS])
        hit = K.sb(ctx, "rt_hit", [P, SPILLS, E * spans])
        lst = K.sb(ctx, "rt_list", [P, SPILLS, E * spans])
        found = K.sb(ctx, "rt_found", [P, 2, SPILLS])
        with nc.Block() as block:
            @block.sync
            def _(sp):
                K.load(sp, w[:, :, :], wr.rearrange("(k p) e -> p k e", p=P))
                K.load(sp, b[:, :], br.rearrange("(a e) -> a e", a=1).partition_broadcast(P))
                K.load(sp, tri[:, :], A["k_before"])
                K.load(sp, code[:, :, :], A["k_spans"])
                K.load(sp, number[:, :], A["k_iota"][:, 0:SPILLS])

            @block.tensor
            def _(pe):
                pe.wait_ge(K.loads, loads0 + 80)
                for t in range(NT):
                    for k in range(KD):
                        ins = nc.tensor.matmul(K.ps[:, 0, t * E:(t + 1) * E], K.hT[:, k, t * P:(t + 1) * P],
                                               w[:, k, :], start=(k == 0), stop=(k == KD - 1))
                ins.then_inc(logit_done, 1)
                pe.wait_ge(masked, 1)
                for t in range(NT):
                    for j in range(t + 1):
                        ins = nc.tensor.matmul(K.ps[:, 1, t * E:(t + 1) * E], K.ones[:, :] if j < t else tri[:, :],
                                               mask[:, j, :], start=(j == 0), stop=(j == t))
                for j in range(NT):
                    ins = nc.tensor.matmul(K.ps[:, 2, 0:E], K.ones[:, :], mask[:, j, :], start=(j == 0),
                                           stop=(j == NT - 1))
                ins.then_inc(placed, 1)

            @block.scalar
            def _(sc):
                sc.wait_ge(exp_in, 1)
                nc.scalar.activation(gate[:, :, 0:E], lg[:, :, :], ACT.Exp).then_inc(exp_out, 1)

            @block.vector
            def _(ve):
                ve.wait_ge(K.loads, loads0 + 80)
                ve.wait_ge(logit_done, 1)
                K.dve_link(nc.vector.tensor_tensor(lg[:, :, :], K.ps[:, 0, 0:NT * E].rearrange("p (t e) -> p t e", e=E),
                                                   b[:, :].unsqueeze(1).to_broadcast([P, NT, E]), ALU.add))
                for t in range(NT):
                    nc.vector.max(m8[:, t, :], lg[:, t, :]).then_inc(counted, 1)
                ve.wait_ge(counted, NT)
                fourth = m8[:, :, 3:4].to_broadcast([P, NT, E])
                K.dve_link(nc.vector.tensor_tensor(mask[:, :, :], lg[:, :, :], fourth, ALU.is_gt))
                K.dve_link(nc.vector.tensor_tensor(same[:, :, :], lg[:, :, :], fourth, ALU.is_equal))
                K.dve_link(nc.vector.tensor_reduce(ssum[:, :], mask[:, :, :], AX, ALU.add))
                for t in range(NT):
                    K.dve_link(nc.vector.tensor_tensor_scan(cnt[:, :], K.ones[:, 0:E], same[:, t, :],
                                                            ssum[:, t:t + 1], ALU.mult, ALU.add))
                    K.dve_link(nc.vector.scalar_tensor_tensor(cnt[:, :], cnt[:, :], float(TOPK), same[:, t, :],
                                                              ALU.is_le, ALU.mult))
                    K.dve_link(nc.vector.tensor_tensor(mask[:, t, :], mask[:, t, :], cnt[:, :], ALU.add))
                nc.vector.tensor_tensor(lg[:, :, :], lg[:, :, :], m8[:, :, 0:1].to_broadcast([P, NT, E]),
                                        ALU.subtract).then_inc(masked, 1)
                ve.wait_ge(masked, 1)
                nc.vector.tensor_copy(same[:, :, :], mask[:, :, :]).then_inc(exp_in, 1)
                nc.vector.memset(gate[:, :, E:], 0.0)
                ve.wait_ge(exp_out, 1)
                g = gate[:, :, 0:E]
                K.dve_link(nc.vector.tensor_tensor(g, g, mask[:, :, :], ALU.mult))
                K.dve_link(nc.vector.tensor_reduce(ssum[:, :], g, AX, ALU.add))
                K.dve_link(nc.vector.reciprocal(ssum[:, :], ssum[:, :]))
                nc.vector.tensor_tensor(g, g, ssum[:, :].unsqueeze(2).to_broadcast([P, NT, E]), ALU.mult)
                ve.wait_ge(placed, 1)
                K.dve_link(nc.vector.memset(posm[:, :, E:], -1.0))
                K.dve_link(nc.vector.scalar_tensor_tensor(posm[:, :, 0:E],
                                                          K.ps[:, 1, 0:NT * E].rearrange("p (t e) -> p t e", e=E),
                                                          1.0, mask[:, :, :], ALU.add, ALU.mult))
                K.dve_link(nc.vector.tensor_scalar(posm[:, :, 0:E], posm[:, :, 0:E], 1.0, None, ALU.subtract))
                extra_n, extra_e, extra_at = extra
                for far in range(spans):
                    h = held[:, :].rearrange("p (e b) -> p e b", b=spans)[:, :, far]
                    K.dve_link(nc.vector.tensor_scalar(h, K.ps[:, 2, 0:E], float(CAP * (far + 1)), None, ALU.is_gt))
                K.dve_link(nc.vector.tensor_tensor_scan(rank[:, :], K.ones[:, 0:E * spans], held[:, :], -1.0,
                                                        ALU.mult, ALU.add))
                K.dve_link(nc.vector.tensor_tensor(hit[:, :, :], number[:, :].unsqueeze(2).to_broadcast(
                    [P, SPILLS, E * spans]), rank[:, :].unsqueeze(1).to_broadcast([P, SPILLS, E * spans]), ALU.is_equal))
                K.dve_link(nc.vector.tensor_tensor(hit[:, :, :], hit[:, :, :], held[:, :].unsqueeze(1).to_broadcast(
                    [P, SPILLS, E * spans]), ALU.mult))
                for i in range(2):
                    K.dve_link(nc.vector.tensor_tensor(lst[:, :, :], hit[:, :, :], code[:, i, :].unsqueeze(1)
                                                       .to_broadcast([P, SPILLS, E * spans]), ALU.mult))
                    K.dve_link(nc.vector.tensor_reduce(found[:, i, :], lst[:, :, :], AX, ALU.add))
                K.dve_link(nc.vector.tensor_copy(extra_e[:, :], found[:, 0, :]))
                K.dve_link(nc.vector.tensor_copy(extra_at[:, :], found[:, 1, :]))
                K.dve_link(nc.vector.tensor_scalar(extra_n[:, :], rank[:, E * spans - 1:], 1.0, None, ALU.add))


class Experts:

    def __init__(self, K, ctx, name, used, used0, xn, scale, shift, posm, gate, acc, b1, b2, iota,
                 added0=0):
        self.K, self.nc, self.used, self.used0, self.added0 = K, K.nc, used, used0, added0
        self.xn, self.scale, self.shift, self.posm, self.gate, self.acc = xn, scale, shift, posm, gate, acc
        self.b1, self.b2, self.iota = b1, b2, iota
        self.picked, self.gathered = K.sem(f"{name}_picked"), K.sem(f"{name}_gathered")
        self.xe_act, self.xe_dve = K.sem(f"{name}_xe_act"), K.sem(f"{name}_xe_dve")
        self.pick_turned, self.scatter_ready = K.sem(f"{name}_pick_turned"), K.sem(f"{name}_scatter_ready")
        self.sig_done, self.act_done = K.sem(f"{name}_sig"), K.sem(f"{name}_act")
        self.a_turned, self.aT_ready = K.sem(f"{name}_a_turned"), K.sem(f"{name}_aT_ready")
        self.ye_ready, self.scattered, self.added = (K.sem(f"{name}_ye"), K.sem(f"{name}_scattered"),
                                                     K.sem(f"{name}_added"))
        self.order = K.sem(f"{name}_dve_order")

    def buffers(self, ctx):
        K = self.K
        self.pick = K.sb(ctx, "moe_pick", [P, 2, NT, CAP])
        self.esel = K.sb(ctx, "moe_esel", [EXPERTS, 2, CAP])
        self.gcol = K.sb(ctx, "moe_gcol", [P, 2, NT])
        self.xeT = K.sb(ctx, "moe_xeT", [P, KD, CAP])
        self.sig = K.sb(ctx, "moe_sig", [P, 2, 256])
        self.glu = K.sb(ctx, "moe_glu", [P, 2, 256])
        self.lin = K.sb(ctx, "moe_lin", [P, 2, 256])
        self.a = K.sb(ctx, "moe_a", [P, 2, 256])
        self.aT = K.sb(ctx, "moe_aT", [P, KD, CAP])
        self.ye = K.sb(ctx, "moe_ye", [P, 2, 512])
        self.scat = K.sb(ctx, "moe_scat", [P, NT * P])

    def share(self, other):
        self.pick, self.esel, self.gcol, self.xeT, self.sig, self.glu, self.lin, self.a, self.aT, self.ye, self.scat = (
            other.pick, other.esel, other.gcol, other.xeT, other.sig, other.glu, other.lin, other.a, other.aT,
            other.ye, other.scat)

    def dve_pick(self, ve, e, par):
        nc = self.nc
        nc.vector.tensor_copy(self.esel[:, par, :], self.K.ident[0:EXPERTS, bass.ds(e, 1)].to_broadcast([EXPERTS, CAP]))
        nc.vector.tensor_copy(self.gcol[:, par, :], self.gate[:, :, bass.ds(e, 1)].rearrange("p t a -> p (t a)"))
        nc.vector.tensor_tensor(self.pick[:, par, :, :], self.iota.unsqueeze(1).to_broadcast([P, NT, CAP]),
                                self.posm[:, :, bass.ds(e, 1)].to_broadcast([P, NT, CAP]), ALU.is_equal)\
            .then_inc(self.picked, 1)

    def dve_xe(self, ve, g):
        ve.wait_ge(self.gathered, g + 1)
        for k in range(4, KD):
            ins = self.nc.vector.tensor_scalar(self.xeT[:, k, :], self.K.ps[:, 5, (k - 4) * CAP:(k - 3) * CAP],
                                               self.scale[:, k:k + 1], self.shift[:, k:k + 1], ALU.mult, ALU.add)
        ins.then_inc(self.xe_dve, 1)

    def dve_expert(self, ve, u, e_next, par, fresh, ahead=True):
        nc = self.nc
        if ahead:
            if not fresh:
                ve.wait_ge(self.scattered, u * 8)
                ve.wait_ge(self.added, u * 8)
            self.dve_pick(ve, e_next, 1 - par)
        for c in range(4):
            up = self.K.ps[:, c % 2, :].rearrange("p (n two) -> p n two", two=2)
            glu, lin = self.glu[:, c % 2, :], self.lin[:, c % 2, :]
            ve.wait_ge(self.used, u * 12 + (self.used0 + 2 * c + 2))
            nc.vector.tensor_scalar(glu, up[:, :, 0], 7.0, None, ALU.min)
            nc.vector.tensor_scalar(lin, up[:, :, 1], 7.0, -7.0, ALU.min, ALU.max).then_inc(self.order, 1)
            ve.wait_ge(self.order, u * 8 + (2 * c + 1))
            nc.vector.scalar_tensor_tensor(lin, lin, 1.0, glu, ALU.add, ALU.mult).then_inc(self.order, 1)
            ve.wait_ge(self.order, u * 8 + (2 * c + 2))
            ve.wait_ge(self.sig_done, u * 4 + (c + 1))
            if c > 1 or not fresh:
                ve.wait_ge(self.a_turned, u * 4 + max(c - 1, 0))
            nc.vector.tensor_tensor(self.a[:, c % 2, :], lin, self.sig[:, c % 2, :], ALU.mult).then_inc(self.act_done, 1)
        if ahead:
            self.dve_xe(ve, u + 1)
        for m in range(2):
            for t in range(NT):
                i = NT * m + t
                ve.wait_ge(self.scattered, u * 8 + (i + 1))
                acc = self.acc[:, t, m * 512:(m + 1) * 512]
                nc.vector.scalar_tensor_tensor(acc, self.K.ps[:, 6 + i % 2, :], self.gcol[:, par, t:t + 1], acc,
                                               ALU.mult, ALU.add).then_inc(self.added, 1)

    def act_xe(self, sc, g):
        sc.wait_ge(self.gathered, g + 1)
        for k in range(4):
            ins = self.nc.scalar.activation(self.xeT[:, k, :], self.K.ps[:, 4, k * CAP:(k + 1) * CAP], ACT.Identity,
                                            scale=self.scale[:, k:k + 1], bias=self.shift[:, k:k + 1])
        ins.then_inc(self.xe_act, 1)

    def act_expert(self, sc, u, fresh, ahead=True):
        nc = self.nc

        def turn(c):
            sc.wait_ge(self.a_turned, u * 4 + (c + 1))
            nc.scalar.activation(self.aT[:, 2 * c:2 * c + 2, :].rearrange("p a b -> p (a b)"),
                                 self.K.ps[:, 3, (c % 2) * 256:(c % 2) * 256 + 256], ACT.Copy).then_inc(self.aT_ready, 1)

        for c in range(4):
            sc.wait_ge(self.order, u * 8 + (2 * c + 1))
            if c > 1 or not fresh:
                sc.wait_ge(self.act_done, u * 4 + max(c - 1, 0))
            nc.scalar.activation(self.sig[:, c % 2, :], self.glu[:, c % 2, :], ACT.Sigmoid, scale=1.702)\
                .then_inc(self.sig_done, 1)
            if c:
                turn(c - 1)
        if ahead:
            self.act_xe(sc, u + 1)
        turn(3)
        sc.wait_ge(self.pick_turned, u + 1)
        nc.scalar.activation(self.scat[:, :], self.K.ps[:, 2, :], ACT.Copy).then_inc(self.scatter_ready, 1)
        for m in range(2):
            sc.wait_ge(self.used, u * 12 + (self.used0 + 8 + 2 * m + 2))
            nc.scalar.activation(self.ye[:, m, :], self.K.ps[:, m, :], ACT.Copy).then_inc(self.ye_ready, 1)

    def pe_gather(self, pe, g, par):
        pe.wait_ge(self.picked, g + 1)
        for k in range(KD):
            for t in range(NT):
                ins = self.nc.tensor.matmul(self.K.ps[:, 4 + k // 4, (k % 4) * CAP:(k % 4 + 1) * CAP],
                                            self.xn[:, t, k * P:(k + 1) * P], self.pick[:, par, t, :],
                                            start=(t == 0), stop=(t == NT - 1))
        ins.then_inc(self.gathered, 1)

    def pe_expert(self, pe, u, par, wait_weights, weights, fresh, ahead=True):
        nc, ps = self.nc, self.K.ps

        def turn(c):
            pe.wait_ge(self.act_done, u * 4 + (c + 1))
            if c or not fresh:
                pe.wait_ge(self.aT_ready, u * 4 + c)
            for i in range(2):
                ins = nc.tensor.transpose(ps[:, 3, (c % 2) * 256 + i * P:(c % 2) * 256 + (i + 1) * P],
                                          self.a[:, c % 2, i * P:(i + 1) * P], self.K.ident[:, :])
            ins.then_inc(self.a_turned, 1)

        def product(out, lhs, bias, j0):
            nc.tensor.matmul(out, self.esel[:, par, :], bias, start=True, stop=False)
            for j in range(2):
                wait_weights(j0 + j)
                w = weights(j0 + j)
                for k in range(4):
                    ins = nc.tensor.matmul(out, lhs[:, 4 * j + k, :], w[:, k, :], start=False,
                                           stop=(j == 1 and k == 3))
                ins.then_inc(self.used, 1)

        pe.wait_ge(self.xe_act, u + 1)
        pe.wait_ge(self.xe_dve, u + 1)
        for c in range(4):
            if c < 2 and not fresh:
                pe.wait_ge(self.ye_ready, u * 2)
            elif c > 1:
                pe.wait_ge(self.act_done, u * 4 + (c - 1))
            product(ps[:, c % 2, :], self.xeT, self.b1[:, c * 512:(c + 1) * 512], 2 * c)
            if c:
                turn(c - 1)
        if ahead:
            self.pe_gather(pe, u + 1, 1 - par)
        turn(3)
        if not fresh:
            pe.wait_ge(self.scatter_ready, u)
        for t in range(NT):
            ins = nc.tensor.transpose(ps[:, 2, t * P:(t + 1) * P], self.pick[:, par, t, :], self.K.ident[:, :])
        ins.then_inc(self.pick_turned, 1)
        pe.wait_ge(self.aT_ready, u * 4 + 4)
        for m in range(2):
            product(ps[:, m, :], self.aT, self.b2[:, m * 512:(m + 1) * 512], 8 + 2 * m)
        pe.wait_ge(self.scatter_ready, u + 1)
        for m in range(2):
            pe.wait_ge(self.ye_ready, u * 2 + (m + 1))
            for t in range(NT):
                i = NT * m + t
                if i > 1 or not fresh:
                    pe.wait_ge(self.added, u * 8 + (self.added0 + max(i - 1, 0)))
                nc.tensor.matmul(ps[:, 6 + i % 2, :], self.scat[:, t * P:(t + 1) * P], self.ye[:, m, :], start=True,
                                 stop=True).then_inc(self.scattered, 1)


def expert_source(A, e, j):
    w = A["w_mlp1"] if j < 8 else A["w_mlp2"]
    col, k0 = ((j % 8) // 2) * 512, (j % 2) * 4
    return w[0, bass.ds(e, 1), k0 * P:(k0 + 4) * P, col:col + 512].rearrange("e (k p) n -> p (e k) n", p=P)


def mixture(K, xn, scale, shift, posm, gate, extra, acc):
    nc, A, ring = K.nc, K.A, K.stream
    first, last = ring.span["moe"]
    extra_n, extra_e, extra_at = extra
    PAIRS = EXPERTS // 2
    PER = 24
    assert last - first == PER * PAIRS and PER % RING == 0
    loads0 = K.loads_n
    with ExitStack() as ctx:
        b1 = K.sb(ctx, "moe_b1", [EXPERTS, 2 * D])
        b2 = K.sb(ctx, "moe_b2", [EXPERTS, D])
        iota = K.sb(ctx, "moe_iota", [P, CAP])
        X = Experts(K, ctx, "moe", K.chunk_used, first, xn, scale, shift, posm, gate, acc, b1[:, :], b2[:, :], iota[:, :])
        X.buffers(ctx)
        spill = K.sb(ctx, "spill_w", [P, 2, SLOT])
        landed = [K.sem(f"spill_landed{i}") for i in range(2)]
        used = K.sem("spill_used")
        Y = Experts(K, ctx, "spill", used, 0, xn, scale, shift, posm, gate, acc, b1[:, :], b2[:, :], iota[:, :],
                    added0=1)
        Y.share(X)
        shifted = K.sem("spill_iota")
        spill_places = K.sb(ctx, "spill_places", [P, CAP])
        Y.iota = spill_places[:, :]

        ready = K.sem("moe_ready")
        with nc.Block() as block:
            @block.sync
            def _(sp):
                K.load(sp, b1[:, :], A["b_mlp1"][0])
                K.load(sp, b2[:, :], A["b_mlp2"][0])
                K.load(sp, iota[:, :], A["k_iota"])
                with sp.Fori(0, PAIRS - 1) as i:
                    for j in range(PER):
                        sp.wait_ge(K.chunk_used, i * PER + (first + j + 1))
                        e2, jj = (j + RING) // 12, (j + RING) % 12
                        dst = K.slot(first + j)
                        sp.dma_start(dst, expert_source(A, i * 2 + e2, jj)).then_inc(K.landed[(first + j) % RING], 16)
                K.refill(sp, last - PER, last)

            @block.vector
            def _(ve):
                nc.vector.memset(acc[:, :, :], 0.0).then_inc(ready, 1)
                nc.vector.memset(spill_places[:, :], 0.0).then_inc(Y.added, 1)
                ve.wait_ge(ready, 1)
                ve.wait_ge(K.loads, loads0 + 48)
                X.dve_pick(ve, 0, 0)
                X.dve_xe(ve, 0)
                for par in range(2):
                    X.dve_expert(ve, par, par + 1, par, fresh=par == 0)
                with ve.Fori(1, PAIRS) as i:
                    for par in range(2):
                        X.dve_expert(ve, i * 2 + par, i * 2 + (par + 1), par, fresh=False)

            @block.scalar
            def _(sc):
                X.act_xe(sc, 0)
                for par in range(2):
                    X.act_expert(sc, par, fresh=par == 0)
                with sc.Fori(1, PAIRS) as i:
                    for par in range(2):
                        X.act_expert(sc, i * 2 + par, fresh=False)

            @block.tensor
            def _(pe):
                pe.wait_ge(K.loads, loads0 + 48)
                X.pe_gather(pe, 0, 0)


                def pair(i, fresh):
                    for par in range(2):
                        n0 = first + 12 * par
                        X.pe_expert(pe, i * 2 + par, par,
                                    lambda j: pe.wait_ge(K.landed[(n0 + j) % RING],
                                                         i * (16 * PER // RING) + ring.landed_at[n0 + j]),
                                    lambda j: K.slot(n0 + j), fresh and par == 0)

                pair(0, True)
                with pe.Fori(1, PAIRS) as i:
                    pair(i, False)

        def weights(j):
            return spill[:, j % 2, :].rearrange("p (k n) -> p k n", n=512)

        def each(eng, body):
            n = eng.value_load(extra_n[0:1, 0:1], min_val=0, max_val=SPILLS)
            with eng.If(n > 0):
                with eng.Fori(0, n) as i:
                    e = eng.value_load(extra_e[0:1, bass.ds(i, 1)], min_val=0, max_val=EXPERTS - 1)
                    eng.wait_ge(Y.added, i * 8 + 1)
                    body(i, e)

        with nc.Block() as block:
            @block.sync
            def _(sp):
                def body(i, e):
                    for j in range(12):
                        if j > 1:
                            sp.wait_ge(used, i * 12 + (j - 1))
                        sp.dma_start(weights(j), expert_source(A, e, j)).then_inc(landed[j % 2], 16)
                each(sp, body)

            @block.vector
            def _(ve):
                def body(i, e):
                    nc.vector.tensor_scalar(spill_places[:, :], iota[:, :], extra_at[:, bass.ds(i, 1)], None, ALU.add)\
                        .then_inc(shifted, 1)
                    ve.wait_ge(shifted, i + 1)
                    Y.dve_pick(ve, e, 0)
                    Y.dve_xe(ve, i)
                    Y.dve_expert(ve, i, None, 0, fresh=True, ahead=False)
                each(ve, body)

            @block.scalar
            def _(sc):
                def body(i, e):
                    Y.act_xe(sc, i)
                    Y.act_expert(sc, i, fresh=True, ahead=False)
                each(sc, body)

            @block.tensor
            def _(pe):
                def body(i, e):
                    Y.pe_gather(pe, i, 0)
                    Y.pe_expert(pe, i, 0, lambda j: pe.wait_ge(landed[j % 2], i * 96 + 16 * (j // 2 + 1)), weights,
                                fresh=True, ahead=False)
                each(pe, body)


def block1(K):
    nc, A = K.nc, K.A
    with ExitStack() as ctx:
        gates = K.sb(ctx, "b1_gates", [P, 2, D])
        mods = K.sb(ctx, "b1_mods", [P, 4, KD])
        cols, at = load_columns(K, "b1_cols", [("c", A["c"][0]), ("g_mix", A["g_mix"][0]), ("g_ffn", A["g_ffn"][0])], ctx)
        col = lambda key, n: cols[:, at[key]:at[key] + n]
        modulation(K, "mod1", col("c", KD), A["b_ada"][0], gates, mods[:, 0, :], mods[:, 1, :], mods[:, 2, :],
                   mods[:, 3, :], col("g_mix", KD), col("g_ffn", KD))
        with nc.sbuf_tensor("b1_xn", [P, NT, D], F32) as xn:
            normalise(K, "b1_norm", xn, mods[:, 0, :], mods[:, 1, :], K.hT)
        with nc.sbuf_tensor("b1_merged", [P, KD, S], F32) as merged:
            with nc.sbuf_tensor("b1_gate_a", [P, KD, S], F32) as ga:
                with nc.sbuf_tensor("b1_retT", [P, KD, S], F32) as retT:
                    retention(K, retT)
                    sigmoid_gate(K, "gate_a", ga)
                    linear(K, "ret_o", "T", retT, 1,
                           dve=lambda j, b: nc.vector.tensor_tensor(merged[:, 2 * j:2 * j + 2, :], b,
                                                                    ga[:, 2 * j:2 * j + 2, :], ALU.mult))
            with nc.sbuf_tensor("b1_attT", [P, AH, S], F32) as attT:
                with nc.sbuf_tensor("b1_T0", [P, AH, T0W], F32) as T0, nc.sbuf_tensor("b1_T12", [P, AH, T12W], F32) as T12:
                    jobs = [(h, 0, 1024, 4, 508, T0[:, h, :]) for h in range(AH)]
                    for g in range(1, AG):
                        jobs += [(g * AH + h, 768 + 256 * g, 256, 1, 127, T12[:, h, (g - 1) * P:g * P])
                                 for h in range(AH)]
                    bias_tables(K, "b1_bias", A["rel_bias"], A["k_hot1"], jobs, AG * AH)
                    dilated(K, attT, T0, T12)
                with nc.sbuf_tensor("b1_gate_b", [P, KD, S], F32) as gb:
                    sigmoid_gate(K, "gate_b", gb)

                    def merge(j, banks):
                        K.dve_link(nc.vector.tensor_tensor(gb[:, 4 * j:4 * j + 4, :], banks, gb[:, 4 * j:4 * j + 4, :],
                                                           ALU.mult))
                        return nc.vector.tensor_tensor(merged[:, 4 * j:4 * j + 4, :], merged[:, 4 * j:4 * j + 4, :],
                                                       gb[:, 4 * j:4 * j + 4, :], ALU.add)
                    attention_out(K, attT, merge)
            add_residual(K, "w_o", merged, 2, gate=gates[:, 0, :])
        with ExitStack() as mctx:
            xn = K.sb(mctx, "b1_xn2", [P, NT, D])
            posm = K.sb(mctx, "moe_posm", [P, NT, EXPERTS + 1])
            gate = K.sb(mctx, "moe_gate", [P, NT, EXPERTS + 1])
            extra = (K.sb(mctx, "extra_n", [P, 1], I32), K.sb(mctx, "extra_e", [P, SPILLS], I32),
                     K.sb(mctx, "extra_at", [P, SPILLS]))
            normalise(K, "b1_norm2", xn, mods[:, 2, :], mods[:, 3, :], K.hT)
            route(K, A["w_router"][0], A["b_router"][0], posm, gate, extra)
            acc = K.sb(mctx, "moe_acc", [P, NT, D])
            mixture(K, xn, mods[:, 2, :], mods[:, 3, :], posm, gate, extra, acc)
            with nc.Block() as block:
                @block.vector
                def _(ve):
                    K.dve_link(nc.vector.tensor_tensor(acc[:, :, :], acc[:, :, :],
                                                       gates[:, 1, :].unsqueeze(1).to_broadcast([P, NT, D]), ALU.mult))
                    K.dve_link(nc.vector.tensor_tensor(K.x[:, :, :], K.x[:, :, :], acc[:, :, :], ALU.add))
        final_norm(K, "b1_out", A["g_final"], False)


def attention_out(K, attT, merge):
    nc = K.nc
    first, last = K.stream.span["att_o"]
    evac0 = K.dve_evac_n
    with nc.Block() as block:
        @block.sync
        def _(sp):
            K.refill(sp, first, last)

        @block.tensor
        def _(pe):
            for j in range(2):
                K.wait_chunk(pe, first + j)
                w = K.slot(first + j)
                for i in range(4):
                    for k in range(AH):
                        ins = nc.tensor.matmul(K.ps[:, 4 * j + i, :], w[:, k, i * P:(i + 1) * P], attT[:, k, :],
                                               start=(k == 0), stop=(k == AH - 1))
                ins.then_inc(K.chunk_used, 1)

        @block.vector
        def _(ve):
            for j in range(2):
                ve.wait_ge(K.chunk_used, first + j + 1)
                merge(j, K.ps[:, 4 * j:4 * j + 4, :]).then_inc(K.dve_evac, 1)
    K.dve_evac_n += 2



DH, DQK, DV = 4, 64, 128
GH, GDK, GDV, GC = 4, 32, 64, 64
C2_Q, C2_K, C2_V = 0, 512, 1024
C2_GQK, C2_GV, C2_GLR, C2_GR, C2_POOL = 1536, 1792, 2048, 2064, 2320
LAM_INIT = 0.8 - 0.6 * math.exp(0.0)
WINDOWS = (2, 4, 8, 16)


def plan_ffn(st, name, w_gate, gate0, w_up, up0, w_down):
    for i in range(FFN_T // 2):
        st.add(f"{name}_up", columns(w_gate, (gate0 + 256 * i, 256)))
        st.add(f"{name}_up", columns(w_up, (up0 + 256 * i, 256)))
    for j in range(2):
        for k in range(0, FFN_T, 4):
            st.add(f"{name}_down", rows(w_down, k, min(4, FFN_T - k), 512 * j))


def plan_block2(st, A):
    w = A["w_in_2"][0]
    for c0 in (C2_Q, C2_K, C2_V):
        for c in range(2):
            st.add("b2_qkv", rows(w, 4 * c, 4, c0))
    for c0 in (C2_GQK, C2_GV, C2_GR, C2_POOL):
        st.add("b2_rest", columns(w, (c0, 256)))
    st.add("b2_lr", columns(w, (C2_GLR, 16)))
    for j in range(2):
        for c in range(2):
            st.add("b2_out", rows(A["w_out_2"][0], 4 * c, 4, 512 * j))
    plan_ffn(st, "b2", A["w_gate_2"][0], 0, A["w_up_2"][0], 0, A["w_down_2"][0])


def group_norm(K, name, view, groups, width, eps, centre=False):
    nc = K.nc
    var, root = K.sem(f"{name}_var"), K.sem(f"{name}_root")
    with ExitStack() as ctx:
        sq = K.sb(ctx, f"{name}_sq", [P, groups, width])
        ms = K.sb(ctx, f"{name}_ms", [P, groups])
        sd = K.sb(ctx, f"{name}_sd", [P, groups])
        spread = ms[:, :].unsqueeze(2).to_broadcast([P, groups, width])
        with nc.Block() as block:
            @block.vector
            def _(ve):
                if centre:
                    K.dve_link(nc.vector.tensor_reduce(ms[:, :], view, AX, ALU.add))
                    K.dve_link(nc.vector.tensor_scalar(ms[:, :], ms[:, :], 1.0 / width, None, ALU.mult))
                    K.dve_link(nc.vector.tensor_tensor(view, view, spread, ALU.subtract))
                K.dve_link(nc.vector.tensor_tensor(sq[:, :, :], view, view, ALU.mult))
                K.dve_link(nc.vector.tensor_reduce(ms[:, :], sq[:, :, :], AX, ALU.add))
                nc.vector.tensor_scalar(ms[:, :], ms[:, :], 1.0 / width, eps, ALU.mult, ALU.add).then_inc(var, 1)
                ve.wait_ge(root, 1)
                K.dve_link(nc.vector.reciprocal(ms[:, :], sd[:, :]))
                K.dve_link(nc.vector.tensor_tensor(view, view, spread, ALU.mult))

            @block.scalar
            def _(sc):
                sc.wait_ge(var, 1)
                nc.scalar.activation(sd[:, :], ms[:, :], ACT.Sqrt).then_inc(root, 1)


def turn_tiles(K, name, sources, dests, scale=None):
    nc = K.nc
    turned, copied = K.sem(f"{name}_turned"), K.sem(f"{name}_copied")
    with nc.Block() as block:
        @block.tensor
        def _(pe):
            for i, src in enumerate(sources):
                if i >= 8:
                    pe.wait_ge(copied, i - 7)
                for t in range(NT):
                    ins = nc.tensor.transpose(K.ps[:, i % 8, t * P:(t + 1) * P], src(t), K.ident[:, :])
                ins.then_inc(turned, 1)

        @block.scalar
        def _(sc):
            for i, dst in enumerate(dests):
                sc.wait_ge(turned, i + 1)
                s = scale(i) if scale else None
                nc.scalar.activation(dst, K.ps[:, i % 8, :], ACT.Identity, scale=s if s is not None else 1.0, bias=0.0)\
                    .then_inc(copied, 1)


def diff_attention(K, name, qT, kT, v, TB, neg_lam, a_out):
    nc, ps = K.nc, K.ps
    scores, biased, maxed, softmax, mixed, turned, pT_ready, av, stored = (
        K.sem(f"{name}_{n}") for n in "scores biased maxed softmax mixed turned pT av stored".split())
    U = DH * NT
    with ExitStack() as ctx:
        s = K.sb(ctx, f"{name}_s", [P, 2, 2, S])
        w = K.sb(ctx, f"{name}_w", [P, 2, S])
        pT = K.sb(ctx, f"{name}_pTs", [P, S])
        nm = K.sb(ctx, f"{name}_nm", [P, 2, 2])
        l = K.sb(ctx, f"{name}_l", [P, 2, 2])
        with nc.Block() as block:
            @block.tensor
            def _(pe):
                def score(u):
                    h, i = u // NT, u % NT
                    if u >= 2:
                        pe.wait_ge(biased, u - 1)
                    for m in range(2):
                        r = slice(m * DQK, (m + 1) * DQK)
                        ins = nc.tensor.matmul(ps[:, 2 * (u % 2) + m, 0:(i + 1) * P], qT[r, h, i * P:(i + 1) * P],
                                               kT[r, h, 0:(i + 1) * P], start=True, stop=True)
                    ins.then_inc(scores, 1)

                score(0)
                for u in range(U):
                    h, i = u // NT, u % NT
                    if u + 1 < U:
                        score(u + 1)
                    pe.wait_ge(mixed, u + 1)
                    if u:
                        pe.wait_ge(pT_ready, u)
                    for j in range(i + 1):
                        ins = nc.tensor.transpose(ps[:, 4, j * P:(j + 1) * P], w[:, u % 2, j * P:(j + 1) * P],
                                                  K.ident[:, :])
                    ins.then_inc(turned, 1)
                    pe.wait_ge(pT_ready, u + 1)
                    if u >= 2:
                        pe.wait_ge(stored, u - 1)
                    for j in range(i + 1):
                        ins = nc.tensor.matmul(ps[:, 5 + u % 2, 0:DV], pT[:, j * P:(j + 1) * P],
                                               v[:, j, h * DV:(h + 1) * DV], start=(j == 0), stop=(j == i))
                    ins.then_inc(av, 1)

            @block.scalar
            def _(sc):
                for u in range(U):
                    h, i = u // NT, u % NT
                    n, b = (i + 1) * P, u % 2
                    sc.wait_ge(maxed, u + 1)
                    for m in range(2):
                        nc.scalar.activation(s[:, b, m, 0:n], s[:, b, m, 0:n], ACT.Exp, bias=nm[:, b, m:m + 1],
                                             scale=1.0, accum_out=l[:, b, m:m + 1]).then_inc(softmax, 1)
                    sc.wait_ge(turned, u + 1)
                    if u:
                        sc.wait_ge(av, u)
                    nc.scalar.activation(pT[:, 0:n], ps[:, 4, 0:n], ACT.Copy).then_inc(pT_ready, 1)
                    sc.wait_ge(av, u + 1)
                    nc.scalar.activation(a_out[:, i, h * DV:(h + 1) * DV], ps[:, 5 + u % 2, 0:DV], ACT.Copy)\
                        .then_inc(stored, 1)

            @block.vector
            def _(ve):
                def soften(u):
                    h, i = u // NT, u % NT
                    n, b = (i + 1) * P, u % 2
                    ve.wait_ge(scores, u + 1)
                    if u >= 2:
                        ve.wait_ge(mixed, u - 1)
                    nc.vector.tensor_tensor(s[:, b, :, 0:n], ps[:, 2 * b:2 * b + 2, 0:n],
                                            TB[:, h, (3 - i) * P:].unsqueeze(1).to_broadcast([P, 2, n]), ALU.add)\
                        .then_inc(biased, 1)
                    ve.wait_ge(biased, u + 1)
                    K.dve_link(nc.vector.tensor_reduce(nm[:, b, :], s[:, b, :, 0:n], AX, ALU.max))
                    nc.vector.tensor_scalar(nm[:, b, :], nm[:, b, :], -1.0, None, ALU.mult).then_inc(maxed, 1)

                soften(0)
                for u in range(U):
                    n, b = (u % NT + 1) * P, u % 2
                    if u + 1 < U:
                        soften(u + 1)
                    ve.wait_ge(softmax, 2 * u + 2)
                    K.dve_link(nc.vector.reciprocal(l[:, b, :], l[:, b, :]))
                    K.dve_link(nc.vector.tensor_tensor(l[:, b, 1:2], l[:, b, 1:2], neg_lam, ALU.mult))
                    if u >= 2:
                        ve.wait_ge(turned, u - 1)
                    K.dve_link(nc.vector.tensor_scalar(w[:, b, 0:n], s[:, b, 0, 0:n], l[:, b, 0:1], None, ALU.mult))
                    nc.vector.scalar_tensor_tensor(w[:, b, 0:n], s[:, b, 1, 0:n], l[:, b, 1:2], w[:, b, 0:n],
                                                   ALU.mult, ALU.add).then_inc(mixed, 1)


def gla(K, glrT, gqk, gv, gr, b_out):
    nc, ps, A = K.nc, K.ps, K.A
    zdone, absd, ln_in, lndone, la_ready, cum, sub, expd, decd, qk_ready, turned, qkT_ready, scored, masked = (
        K.sem(f"gla_{n}") for n in "z abs ln_in ln la cum sub exp dec qk turned qkT scored masked".split())
    kv_done, kv_used, state_ready, o_done = (K.sem(f"gla_{n}") for n in "kv kv_used state o".split())
    loads0 = K.loads_n
    W = GH * GDK
    with ExitStack() as ctx:
        gw = K.sb(ctx, "gla_w", [16, W])
        gb = K.sb(ctx, "gla_b", [P, W])
        tri = K.sb(ctx, "gla_tri", [P, 2, P])
        hm = K.sb(ctx, "gla_hm", [P, GH * GDV])
        z = K.sb(ctx, "gla_zb", [P, NT, W])
        az = K.sb(ctx, "gla_az", [P, NT, W])
        la = K.sb(ctx, "gla_lab", [P, NT, W])
        eb = K.sb(ctx, "gla_eb", [P, NT, W])
        en = K.sb(ctx, "gla_en", [P, NT, W])
        el = K.sb(ctx, "gla_el", [P, NT, W])
        qT = K.sb(ctx, "gla_qT", [P, S])
        kT = K.sb(ctx, "gla_kT", [P, S])
        at = K.sb(ctx, "gla_at", [P, NT, GH, P])
        dec = K.sb(ctx, "gla_decb", [P, 8])
        st = K.sb(ctx, "gla_st", [P, 8, GH * GDV])
        kvm = K.sb(ctx, "gla_kvm", [P, GH * GDV])
        flat = lambda a: a[:, :, :].rearrange("p t n -> p (t n)")
        with nc.Block() as block:
            @block.sync
            def _(sp):
                K.load(sp, gw[:, :], A["gla_gate_w_2"][0])
                K.load(sp, gb[:, :], A["gla_gate_b_2"][0].rearrange("(a n) -> a n", a=1).partition_broadcast(P))
                K.load(sp, tri[:, :, :], A["k_gla_tri"])
                K.load(sp, hm[:, :], A["k_gla_heads"])

            @block.tensor
            def _(pe):
                pe.wait_ge(K.loads, loads0 + 64)
                for t in range(NT):
                    ins = nc.tensor.matmul(ps[:, 0, t * W:(t + 1) * W], glrT[:, t * P:(t + 1) * P], gw[:, :],
                                           start=True, stop=True)
                ins.then_inc(zdone, 1)
                pe.wait_ge(la_ready, 1)
                for t in range(NT):
                    nc.tensor.matmul(ps[:, 1, t * W:(t + 1) * W], tri[:, 0, :], la[:, t, :], start=True, stop=True)
                    nc.tensor.matmul(ps[:, 2, t * W:(t + 1) * W], tri[:, 1, :], la[:, t, :], start=True, stop=True)
                    ins = nc.tensor.matmul(ps[:, 3, 2 * t:2 * t + 2], la[:, t, :], tri[:, 1, 0:P:GC], start=True,
                                           stop=True)
                ins.then_inc(cum, 1)
                pe.wait_ge(qk_ready, 1)
                for t in range(NT):
                    nc.tensor.transpose(ps[:, 4, t * P:(t + 1) * P], eb[:, t, :], K.ident[:, :])
                    ins = nc.tensor.transpose(ps[:, 5, t * P:(t + 1) * P], en[:, t, :], K.ident[:, :])
                ins.then_inc(turned, 1)
                pe.wait_ge(qkT_ready, 1)
                for h in range(GH):
                    r = slice(h * GDK, (h + 1) * GDK)
                    for t in range(NT):
                        ins = nc.tensor.matmul(ps[:, 4 + h, t * P:(t + 1) * P], kT[r, t * P:(t + 1) * P],
                                               qT[r, t * P:(t + 1) * P], start=True, stop=True)
                    ins.then_inc(scored, 1)
                pe.wait_ge(qk_ready, 2)
                for n in range(7):
                    t, r = n // 2, slice((n % 2) * GC, (n % 2 + 1) * GC)
                    if n >= 2:
                        pe.wait_ge(kv_used, n - 1)
                    nc.tensor.matmul(ps[:, n % 2, 0:GH * GDV], el[r, t, :], gv[r, t, :], start=True, stop=True)\
                        .then_inc(kv_done, 1)
                pe.wait_ge(masked, GH)
                pe.wait_ge(qkT_ready, 1)
                for t in range(NT):
                    for h in range(GH):
                        c = slice(h * GDV, (h + 1) * GDV)
                        ins = nc.tensor.matmul(ps[:, 2 + t // 2, (t % 2) * 256 + h * GDV:(t % 2) * 256 + (h + 1) * GDV],
                                               at[:, t, h, :], gv[:, t, c], start=True, stop=True)
                pe.wait_ge(state_ready, 8)
                for n in range(8):
                    t, r = n // 2, slice((n % 2) * GC, (n % 2 + 1) * GC)
                    ins = nc.tensor.matmul(ps[r, 4 + t // 2, (t % 2) * 256:(t % 2) * 256 + 256],
                                           qT[:, n * GC:(n + 1) * GC], st[:, n, :], start=True, stop=True)
                ins.then_inc(o_done, 1)

            @block.scalar
            def _(sc):
                sc.wait_ge(absd, 1)
                nc.scalar.activation(flat(az), flat(az), ACT.Exp, scale=-1.0).then_inc(ln_in, 1)
                sc.wait_ge(ln_in, 1)
                nc.scalar.activation(flat(az), flat(az), ACT.Ln, bias=1.0).then_inc(lndone, 1)
                sc.wait_ge(cum, 1)
                nc.scalar.activation(flat(eb), ps[:, 1, :], ACT.Exp).then_inc(expd, 1)
                nc.scalar.activation(flat(en), ps[:, 1, :], ACT.Exp, scale=-1.0).then_inc(expd, 1)
                nc.scalar.activation(dec[:, :], ps[:, 3, 0:8], ACT.Exp).then_inc(decd, 1)
                sc.wait_ge(sub, 1)
                nc.scalar.activation(flat(el), flat(el), ACT.Exp).then_inc(expd, 1)
                sc.wait_ge(turned, 1)
                nc.scalar.activation(qT[:, :], ps[:, 4, :], ACT.Copy)
                nc.scalar.activation(kT[:, :], ps[:, 5, :], ACT.Copy).then_inc(qkT_ready, 1)

            @block.vector
            def _(ve):
                ve.wait_ge(zdone, 1)
                ve.wait_ge(K.loads, loads0 + 64)
                K.dve_link(nc.vector.tensor_tensor(z[:, :, :], ps[:, 0, :].rearrange("p (t n) -> p t n", n=W),
                                                   gb[:, :].unsqueeze(1).to_broadcast([P, NT, W]), ALU.add))
                nc.vector.scalar_tensor_tensor(flat(az), flat(z), -1.0, flat(z), ALU.mult, ALU.max).then_inc(absd, 1)
                K.dve_link(nc.vector.tensor_scalar(flat(z), flat(z), 0.0, None, ALU.min))
                ve.wait_ge(lndone, 1)
                K.dve_link(nc.vector.tensor_tensor(flat(la), flat(z), flat(az), ALU.subtract))
                nc.vector.tensor_scalar(flat(la), flat(la), 1.0 / 16.0, None, ALU.mult).then_inc(la_ready, 1)
                ve.wait_ge(expd, 2)
                K.dve_link(nc.vector.tensor_copy(flat(z), ps[:, 1, :]))
                nc.vector.tensor_tensor(flat(el), ps[:, 2, :], flat(z), ALU.subtract).then_inc(sub, 1)
                ve.wait_ge(decd, 1)
                K.dve_link(nc.vector.scalar_tensor_tensor(eb[:, :, :], gqk[:, :, 0:W], float(GDK) ** -0.5, eb[:, :, :],
                                                          ALU.mult, ALU.mult))
                nc.vector.tensor_tensor(en[:, :, :], gqk[:, :, W:], en[:, :, :], ALU.mult).then_inc(qk_ready, 1)
                ve.wait_ge(expd, 3)
                nc.vector.tensor_tensor(el[:, :, :], gqk[:, :, W:], el[:, :, :], ALU.mult).then_inc(qk_ready, 1)
                for h in range(GH):
                    ve.wait_ge(scored, h + 1)
                    nc.vector.tensor_tensor(at[:, :, h, :], ps[:, 4 + h, :].rearrange("p (t n) -> p t n", n=P),
                                            tri[:, 0, :].unsqueeze(1).to_broadcast([P, NT, P]), ALU.mult)\
                        .then_inc(masked, 1)
                nc.vector.memset(st[:, 0, :], 0.0).then_inc(state_ready, 1)
                for n in range(7):
                    ve.wait_ge(kv_done, n + 1)
                    ve.wait_ge(state_ready, n + 1)
                    nc.vector.tensor_tensor(kvm[:, :], ps[:, n % 2, 0:GH * GDV], hm[:, :], ALU.mult)\
                        .then_inc(kv_used, 1)
                    ve.wait_ge(kv_used, n + 1)
                    nc.vector.scalar_tensor_tensor(st[:, n + 1, :], st[:, n, :], dec[:, n:n + 1], kvm[:, :], ALU.mult,
                                                   ALU.add).then_inc(state_ready, 1)
                ve.wait_ge(o_done, 1)
                two = lambda b: ps[:, b:b + 2, :].rearrange("p a n -> p (a n)")
                K.dve_link(nc.vector.tensor_copy(flat(b_out), two(2)))
                K.dve_link(nc.vector.tensor_tensor(flat(b_out), two(4), flat(b_out), ALU.add))
        group_norm(K, "gla_norm", b_out[:, :, :].rearrange("p t (h d) -> p (t h) d", d=GDV), NT * GH, GDV, EPS)
        gated = K.sem("gla_gated")
        gn = K.sb(ctx, "gla_gn", [P, GDV])
        with nc.Block() as block:
            @block.sync
            def _(sp):
                K.load(sp, gn[:, :], A["gla_norm_g_2"][0].rearrange("(a n) -> a n", a=1).partition_broadcast(P))

            @block.scalar
            def _(sc):
                nc.scalar.activation(flat(z), gr[:, :, 0:W], ACT.Sigmoid)
                nc.scalar.activation(flat(az), gr[:, :, W:], ACT.Sigmoid).then_inc(gated, 1)

            @block.vector
            def _(ve):
                ve.wait_ge(K.loads, K.loads_n)
                o = b_out[:, :, :].rearrange("p t (h d) -> p (t h) d", d=GDV)
                K.dve_link(nc.vector.tensor_tensor(o, o, gn[:, :].unsqueeze(1).to_broadcast([P, NT * GH, GDV]), ALU.mult))
                K.dve_link(nc.vector.tensor_tensor(b_out[:, :, :], b_out[:, :, :], gr[:, :, :], ALU.mult))
                ve.wait_ge(gated, 1)
                K.dve_link(nc.vector.tensor_tensor(b_out[:, :, 0:W], b_out[:, :, 0:W], z[:, :, :], ALU.mult))
                K.dve_link(nc.vector.tensor_tensor(b_out[:, :, W:], b_out[:, :, W:], az[:, :, :], ALU.mult))


def pooling(K, u, scale_cols, mixedT):
    nc, ps, A = K.nc, K.ps, K.A
    pooled, copied, mixed = K.sem("pool_pooled"), K.sem("pool_copied"), K.sem("pool_mixed")
    with ExitStack() as ctx:
        band = K.sb(ctx, "pool_band", [P, 4, 3, P])
        pw = K.sb(ctx, "pool_w", [P, 2, GDV])
        pT = K.sb(ctx, "pool_T", [P, 2, S])
        with nc.Block() as block:
            @block.sync
            def _(sp):
                K.load(sp, band[:, :, :, :], A["k_pool"])
                for g in range(4):
                    K.load(sp, pw[(g % 2) * 64:(g % 2) * 64 + 64, g // 2, :], A["pool_w_2"][0, g])

            @block.tensor
            def _(pe):
                pe.wait_ge(K.loads, K.loads_n)
                for g in range(4):
                    r = slice((g % 2) * 64, (g % 2) * 64 + 64)
                    for i in range(NT):
                        out = ps[r, g // 2, i * P:(i + 1) * P]
                        ins = nc.tensor.matmul(out, u[:, i, g * 64:(g + 1) * 64], band[:, g, 0 if i == 0 else 1, :],
                                               start=True, stop=(i == 0))
                        if i:
                            ins = nc.tensor.matmul(out, u[:, i - 1, g * 64:(g + 1) * 64], band[:, g, 2, :],
                                                   start=False, stop=True)
                ins.then_inc(pooled, 1)
                pe.wait_ge(copied, 1)
                for g in range(4):
                    r = slice((g % 2) * 64, (g % 2) * 64 + 64)
                    ins = nc.tensor.matmul(ps[r, 2 + g // 2, :], pw[r, g // 2, :], pT[r, g // 2, :], start=True,
                                           stop=True)
                ins.then_inc(mixed, 1)

            @block.vector
            def _(ve):
                ve.wait_ge(pooled, 1)
                nc.vector.tensor_copy(pT[:, :, :], ps[:, 0:2, :]).then_inc(copied, 1)
                ve.wait_ge(mixed, 1)
                for i in range(2):
                    nc.vector.tensor_scalar(mixedT[:, 6 + i, :], ps[:, 2 + i, :], scale_cols[:, i:i + 1], None, ALU.mult)


def swiglu_up(K, stage, ffT):
    nc = K.nc
    with nc.sbuf_tensor(f"{stage}_sig", [P, 2, 2, S], F32) as sg:
        def act(j, banks):
            return nc.scalar.activation(sg[:, j % 2, :, :], banks[:, 0:2, :], ACT.Sigmoid)

        def dve(j, banks):
            K.dve_link(nc.vector.tensor_tensor(sg[:, j % 2, :, :], sg[:, j % 2, :, :], banks[:, 0:2, :], ALU.mult))
            return nc.vector.tensor_tensor(ffT[:, 2 * j:2 * j + 2, :], sg[:, j % 2, :, :], banks[:, 2:4, :], ALU.mult)

        linear(K, stage, "T", K.hT, 2, act=act, dve=dve)


def block2(K):
    nc, A = K.nc, K.A
    with ExitStack() as ctx:
        cols, at = load_columns(K, "b2_cols", [("g1", A["attn_norm_g_2"][0]), ("g2", A["ffn_norm_g_2"][0]),
                                               ("pool", A["pool_scale_2"][0])], ctx)
        with nc.sbuf_tensor("b2_xn", [P, NT, D], F32) as xn:
            normalise(K, "b2_norm", xn, cols[:, at["g1"]:at["g1"] + KD], None, K.hT)
        with ExitStack() as mix:
            mixedT = K.sb(mix, "b2_mixedT", [P, KD, S])
            qk = K.sb(mix, "b2_qk", [P, 2, NT, 512])
            v = K.sb(mix, "b2_v", [P, NT, 512])
            rest = K.sb(mix, "b2_rest", [P, 4, NT, 256])
            glrT = K.sb(mix, "b2_glrT", [16, S])
            dests = [qk[:, 0, :, :], qk[:, 1, :, :], v[:, :, :]]
            linear(K, "b2_qkv", "N", K.hT, 2,
                   act=lambda j, b: nc.scalar.activation(dests[j], b, ACT.Copy))
            linear(K, "b2_rest", "N", K.hT, 1,
                   act=lambda j, b: nc.scalar.activation(rest[:, j, :, :], b[:, :, 0:256], ACT.Copy))
            first, last = K.stream.span["b2_lr"]
            lr_done = K.sem("b2_lr_done")
            with nc.Block() as block:
                @block.sync
                def _(sp):
                    K.refill(sp, first, last)

                @block.tensor
                def _(pe):
                    K.wait_chunk(pe, first)
                    K.use_T(pe, first, 16, 0, K.hT, K.ps[0:16, 0, :], True, m=16)

                @block.vector
                def _(ve):
                    ve.wait_ge(K.chunk_used, first + 1)
                    nc.vector.tensor_copy(glrT[:, :], K.ps[0:16, 0, :])
            with ExitStack() as da:
                group_norm(K, "b2_qkn", qk[:, :, :, :].rearrange("p a t (h d) -> p (a t h) d", d=DQK), 64, DQK, EPS)
                gq = K.sb(da, "b2_gq", [P, 2])
                lv = K.sb(da, "b2_lv", [P, 4, DQK])
                lp = K.sb(da, "b2_lp", [P, 2, DQK])
                ls = K.sb(da, "b2_ls", [P, 2])
                neg_lam = K.sb(da, "b2_neg_lam", [P, 1])
                lsum, lexp = K.sem("b2_lam_sum"), K.sem("b2_lam_exp")
                with nc.Block() as block:
                    @block.sync
                    def _(sp):
                        for i, key in enumerate(("q_norm_g_2", "k_norm_g_2")):
                            for m in range(2):
                                K.load(sp, gq[m * DQK:(m + 1) * DQK, i:i + 1],
                                       A[key][0].rearrange("(p a) -> p a", a=1))
                        K.load(sp, lv[:, :, :].rearrange("p a n -> p (a n)"),
                               A["lambda_vecs_2"].rearrange("o a n -> o (a n)").partition_broadcast(P))

                    @block.vector
                    def _(ve):
                        ve.wait_ge(K.loads, K.loads_n)
                        K.dve_link(nc.vector.scalar_tensor_tensor(gq[:, 0:1], gq[:, 0:1], float(DQK) ** -0.5,
                                                                  gq[:, 1:2], ALU.mult, ALU.mult))
                        K.dve_link(nc.vector.tensor_tensor(lp[:, :, :], lv[:, 0:4:2, :], lv[:, 1:4:2, :], ALU.mult))
                        nc.vector.tensor_reduce(ls[:, :], lp[:, :, :], AX, ALU.add).then_inc(lsum, 1)
                        ve.wait_ge(lexp, 1)
                        K.dve_link(nc.vector.tensor_tensor(neg_lam[:, :], ls[:, 1:2], ls[:, 0:1], ALU.subtract))
                        K.dve_link(nc.vector.tensor_scalar(neg_lam[:, :], neg_lam[:, :], LAM_INIT, None, ALU.subtract))

                    @block.scalar
                    def _(sc):
                        sc.wait_ge(lsum, 1)
                        nc.scalar.activation(ls[:, :], ls[:, :], ACT.Exp).then_inc(lexp, 1)
                TB = K.sb(da, "b2_TB", [P, DH, S])
                bias_tables(K, "b2_bias", A["rel_bias_2"], A["k_hot2"],
                            [(h, 0, 640, 1, 127, TB[:, h, :]) for h in range(DH)], DH)
                qkT = K.sb(da, "b2_qkT", [P, 2, DH, S])
                turn_tiles(K, "b2_qkT",
                           [(lambda t, i=i: qk[:, i // DH, t, (i % DH) * P:(i % DH + 1) * P]) for i in range(2 * DH)],
                           [qkT[:, i // DH, i % DH, :] for i in range(2 * DH)],
                           scale=lambda i: gq[:, 0:1] if i < DH else None)
                diff_attention(K, "da", qkT[:, 0, :, :], qkT[:, 1, :, :], v, TB, neg_lam[:, :], qk[:, 0, :, :])
            a_out = qk[:, 0, :, :]
            group_norm(K, "b2_subln", a_out.rearrange("p t (h d) -> p (t h) d", d=DV), NT * DH, DV, EPS)
            with nc.sbuf_tensor("b2_sg", [P, DV], F32) as sg:
                with nc.Block() as block:
                    @block.sync
                    def _(sp):
                        K.load(sp, sg[:, :], A["da_subln_g_2"][0].rearrange("(a n) -> a n", a=1).partition_broadcast(P))

                    @block.vector
                    def _(ve):
                        ve.wait_ge(K.loads, K.loads_n)
                        K.dve_link(nc.vector.tensor_scalar(sg[:, :], sg[:, :], 1.0 - LAM_INIT, None, ALU.mult))
                        o = a_out.rearrange("p t (h d) -> p (t h) d", d=DV)
                        K.dve_link(nc.vector.tensor_tensor(o, o, sg[:, :].unsqueeze(1).to_broadcast([P, NT * DH, DV]),
                                                           ALU.mult))
            with nc.sbuf_tensor("b2_bout", [P, NT, 256], F32) as b_out:
                gla(K, glrT, rest[:, 0, :, :], rest[:, 1, :, :], rest[:, 2, :, :], b_out)
                turn_tiles(K, "b2_mixT",
                           [(lambda t, i=i: a_out[:, t, i * P:(i + 1) * P]) for i in range(4)] +
                           [(lambda t, i=i: b_out[:, t, i * P:(i + 1) * P]) for i in range(2)],
                           [mixedT[:, i, :] for i in range(6)])
            pooling(K, rest[:, 3, :, :], cols[:, at["pool"]:at["pool"] + 2], mixedT)
            add_residual(K, "b2_out", mixedT, 2)
        with nc.sbuf_tensor("b2_xn2", [P, NT, D], F32) as xn:
            normalise(K, "b2_norm2", xn, cols[:, at["g2"]:at["g2"] + KD], None, K.hT)
        with nc.sbuf_tensor("b2_ffT", [P, FFN_T, S], F32) as ffT:
            swiglu_up(K, "b2_up", ffT)
            add_residual(K, "b2_down", ffT, 6)



HD = 64
C3_FQ, C3_FK, C3_FV, C3_FF = 0, 256, 512, 768
C3_RW = 772
C3_MQ, C3_MK, C3_MV = 2564, 2820, 3076
RW_T = 4
RW_H = 8
CT = P // RWKV_C
DECAY_SCALE = -math.exp(-0.5)
GN_EPS_3 = 64e-5
LEVELS = (2, 4, 8, 16)


def plan_block3(st, A):
    w = A["w_in_3"][0]
    for s in range(12):
        for c in range(2):
            st.add("mod3", rows(A["w_mod_3"][0], 4 * c, 4, 512 * s))
    for c0 in (C3_FQ, C3_FK, C3_MQ, C3_MK):
        st.add("b3_qk", columns(w, (c0, 256)))
    for c0 in (C3_FV, C3_MV):
        st.add("b3_v", columns(w, (c0, 256)))
    st.add("b3_f", columns(w, (C3_FF, 4)))
    for i in range(7):
        st.add("b3_rw", columns(w, (C3_RW + 256 * i, 256)))
    for j in range(2):
        for c in range(2):
            st.add("b3_out", rows(A["w_out_3"][0], 4 * c, 4, 512 * j))
    plan_ffn(st, "b3", A["w_up_3"][0], 0, A["w_up_3"][0], FFN, A["w_down_3"][0])


def forget_sums(K, fcols, neg_f):
    nc, ps, A = K.nc, K.ps, K.A
    absd, expd, lnd, spread, summed = (K.sem(f"ff_{n}") for n in "abs exp ln spread sum".split())
    with ExitStack() as ctx:
        fb = K.sb(ctx, "ff_b", [P, 4])
        tri = K.sb(ctx, "ff_tri", [P, P])
        az = K.sb(ctx, "ff_az", [P, NT, 4])
        lfb = K.sb(ctx, "ff_lfb", [P, NT, 4, P])
        with nc.Block() as block:
            @block.sync
            def _(sp):
                K.load(sp, fb[:, :], A["fox_f_bias_3"][0].rearrange("(a n) -> a n", a=1).partition_broadcast(P))
                K.load(sp, tri[:, :], A["k_upto"])

            @block.vector
            def _(ve):
                ve.wait_ge(K.loads, K.loads_n)
                K.dve_link(nc.vector.tensor_tensor(fcols[:, :, :], fcols[:, :, :],
                                                   fb[:, :].unsqueeze(1).to_broadcast([P, NT, 4]), ALU.add))
                nc.vector.scalar_tensor_tensor(az[:, :, :], fcols[:, :, :], -1.0, fcols[:, :, :], ALU.mult, ALU.max)\
                    .then_inc(absd, 1)
                K.dve_link(nc.vector.tensor_scalar(fcols[:, :, :], fcols[:, :, :], 0.0, None, ALU.min))
                ve.wait_ge(lnd, 1)
                K.dve_link(nc.vector.tensor_tensor(fcols[:, :, :], az[:, :, :], fcols[:, :, :], ALU.subtract))
                nc.vector.tensor_copy(lfb[:, :, :, :].rearrange("p t h n -> p (t h) n"),
                                      fcols[:, :, :].rearrange("p t h -> p (t h)").unsqueeze(2)
                                      .to_broadcast([P, NT * 4, P])).then_inc(spread, 1)
                ve.wait_ge(summed, 1)
                nc.vector.tensor_copy(neg_f, ps[:, 0:4, :])

            @block.scalar
            def _(sc):
                sc.wait_ge(absd, 1)
                nc.scalar.activation(az[:, :, :], az[:, :, :], ACT.Exp, scale=-1.0).then_inc(expd, 1)
                sc.wait_ge(expd, 1)
                nc.scalar.activation(az[:, :, :], az[:, :, :], ACT.Ln, bias=1.0).then_inc(lnd, 1)

            @block.tensor
            def _(pe):
                pe.wait_ge(spread, 1)
                for h in range(4):
                    for s in range(NT):
                        for t in range(s + 1):
                            ins = nc.tensor.matmul(ps[:, h, s * P:(s + 1) * P], lfb[:, t, h, :],
                                                   tri[:, :] if t == s else K.ones[:, :], start=(t == 0), stop=(t == s))
                ins.then_inc(summed, 1)


def causal_attention(K, qkT, v, neg_f, y):
    nc, ps, A = K.nc, K.ps, K.A
    scores, biased, diag, maxed, softmax, turned, pT_ready, av, stored = (
        K.sem(f"ca_{n}") for n in "scores biased diag maxed softmax turned pT av stored".split())
    U = 4 * NT
    with ExitStack() as ctx:
        s = K.sb(ctx, "ca_s", [P, 2, 2, S])
        pT = K.sb(ctx, "ca_pTs", [P, 2, S])
        nm = K.sb(ctx, "ca_nm", [P, 2, 2])
        l = K.sb(ctx, "ca_l", [P, 2, 2])
        mask = K.sb(ctx, "ca_mask", [P, P])
        with nc.Block() as block:
            @block.sync
            def _(sp):
                K.load(sp, mask[:, :], A["k_future"])

            @block.tensor
            def _(pe):
                def score(u):
                    g, i = u // NT, u % NT
                    q, k = 4 * (g // 2) + g % 2, 4 * (g // 2) + 2 + g % 2
                    if u >= 2:
                        pe.wait_ge(biased, u - 1)
                    for m in range(2):
                        r = slice(m * HD, (m + 1) * HD)
                        ins = nc.tensor.matmul(ps[:, 2 * (u % 2) + m, 0:(i + 1) * P], qkT[r, q, i * P:(i + 1) * P],
                                               qkT[r, k, 0:(i + 1) * P], start=True, stop=True)
                    ins.then_inc(scores, 1)

                score(0)
                for u in range(U):
                    g, i = u // NT, u % NT
                    if u + 1 < U:
                        score(u + 1)
                    pe.wait_ge(softmax, 2 * u + 2)
                    if u:
                        pe.wait_ge(pT_ready, u)
                    for m in range(2):
                        for j in range(i + 1):
                            ins = nc.tensor.transpose(ps[:, 4 + m, j * P:(j + 1) * P],
                                                      s[:, u % 2, m, j * P:(j + 1) * P], K.ident[:, :])
                    ins.then_inc(turned, 1)
                    pe.wait_ge(pT_ready, u + 1)
                    if u >= 2:
                        pe.wait_ge(stored, u - 1)
                    for m in range(2):
                        for j in range(i + 1):
                            c = (g % 2) * 128 + m * HD
                            ins = nc.tensor.matmul(ps[:, 6 + u % 2, m * HD:(m + 1) * HD], pT[:, m, j * P:(j + 1) * P],
                                                   v[:, g // 2, j, c:c + HD], start=(j == 0), stop=(j == i))
                    ins.then_inc(av, 1)

            @block.scalar
            def _(sc):
                for u in range(U):
                    n, b = (u % NT + 1) * P, u % 2
                    sc.wait_ge(maxed, u + 1)
                    for m in range(2):
                        nc.scalar.activation(s[:, b, m, 0:n], s[:, b, m, 0:n], ACT.Exp, bias=nm[:, b, m:m + 1],
                                             scale=1.0, accum_out=l[:, b, m:m + 1]).then_inc(softmax, 1)
                    sc.wait_ge(turned, u + 1)
                    if u:
                        sc.wait_ge(av, u)
                    nc.scalar.activation(pT[:, :, 0:n], ps[:, 4:6, 0:n], ACT.Copy).then_inc(pT_ready, 1)

            @block.vector
            def _(ve):
                def soften(u):
                    g, i = u // NT, u % NT
                    n, b = (i + 1) * P, u % 2
                    ve.wait_ge(scores, u + 1)
                    if u >= 2:
                        ve.wait_ge(turned, u - 1)
                    bank = ps[:, 2 * b:2 * b + 2, 0:n]
                    if g < 2:
                        nc.vector.scalar_tensor_tensor(s[:, b, :, 0:n], bank, float(HD) ** -0.5,
                                                       neg_f[:, 2 * g:2 * g + 2, 0:n], ALU.mult, ALU.add)\
                            .then_inc(biased, 1)
                    else:
                        nc.vector.tensor_scalar(s[:, b, :, 0:n], bank, float(HD) ** -0.5, None, ALU.mult)\
                            .then_inc(biased, 1)
                    ve.wait_ge(biased, u + 1)
                    nc.vector.tensor_tensor(s[:, b, :, i * P:n], s[:, b, :, i * P:n],
                                            mask[:, :].unsqueeze(1).to_broadcast([P, 2, P]), ALU.add).then_inc(diag, 1)
                    ve.wait_ge(diag, u + 1)
                    K.dve_link(nc.vector.tensor_reduce(nm[:, b, :], s[:, b, :, 0:n], AX, ALU.max))
                    nc.vector.tensor_scalar(nm[:, b, :], nm[:, b, :], -1.0, None, ALU.mult).then_inc(maxed, 1)

                ve.wait_ge(K.loads, K.loads_n)
                soften(0)
                for u in range(U):
                    g, i, b = u // NT, u % NT, u % 2
                    if u + 1 < U:
                        soften(u + 1)
                    ve.wait_ge(softmax, 2 * u + 2)
                    K.dve_link(nc.vector.reciprocal(l[:, b, :], l[:, b, :]))
                    ve.wait_ge(av, u + 1)
                    nc.vector.tensor_tensor(y[:, i, g * P:(g + 1) * P].rearrange("p (m d) -> p m d", d=HD),
                                            ps[:, 6 + b, 0:P].rearrange("p (m d) -> p m d", d=HD),
                                            l[:, b, :].unsqueeze(2).to_broadcast([P, 2, HD]), ALU.mult)\
                        .then_inc(stored, 1)


def shifted_features(K, feat, mu):
    nc = K.nc
    with nc.sbuf_tensor("rw_prev", [P, 2, 2, S + 1], F32) as prev:
        with nc.Block() as block:
            @block.vector
            def _(ve):
                nc.vector.memset(prev[:, :, :, 0:1], 0.0)

        def act(j, banks):
            return nc.scalar.activation(prev[:, j % 2, :, 1:], banks, ACT.Copy)

        def dve(j, banks):
            f = feat[:, 2 * j:2 * j + 2, :]
            K.dve_link(nc.vector.tensor_tensor(f, prev[:, j % 2, :, 0:S], banks, ALU.subtract))
            for i in range(2):
                n = 2 * j + i
                ins = nc.vector.scalar_tensor_tensor(feat[:, n, :], feat[:, n, :], mu[:, n:n + 1],
                                                     prev[:, j % 2, i, 1:], ALU.mult, ALU.add)
                if i == 0:
                    K.dve_link(ins)
            return ins

        linear(K, "b3_rw", "T", K.hT, 1, act=act, dve=dve)


def rwkv_prepare(K, feat, col, alpha, beta, decay_end, sgT, vtok, bonus):
    nc, ps, A = K.nc, K.ps, K.A
    n_ = lambda s: K.sem(f"rp_{s}")
    tanhd, wdone, sigw, adone, siga, sqd, nsum, nclamp, nroot, bsum, exps, prod, bonusd, vt, vc = (
        n_(s) for s in "tanh w sigw a siga sq nsum nclamp nroot bsum exp prod bonus vt vc".split())
    loads0 = K.loads_n
    r, k, v = feat[:, 0:4, :], feat[:, 4:8, :], feat[:, 8:12, :]
    cb = lambda key: col(key, RW_T).unsqueeze(2).to_broadcast([P, RW_T, S])
    with ExitStack() as ctx:
        w2 = K.sb(ctx, "rp_w2", [P, 512])
        same = K.sb(ctx, "rp_same", [P, P])
        hsel = K.sb(ctx, "rp_hsel", [P, 2])
        reset = K.sb(ctx, "rp_reset", [P, S])
        omk = K.sb(ctx, "rp_omk", [P, RW_T])
        ld = K.sb(ctx, "rp_ld", [P, RW_T, S])
        a = K.sb(ctx, "rp_a_", [P, RW_T, S])
        b = K.sb(ctx, "rp_b", [P, RW_T, S])
        e = K.sb(ctx, "rp_e", [P, RW_T, S])
        with nc.Block() as block:
            @block.sync
            def _(sp):
                K.load(sp, w2[0:64, :], A["rwkv_w2_3"][0])
                K.load(sp, w2[64:128, :], A["rwkv_a2_3"][0])
                K.load(sp, same[:, :], A["k_same_head"])
                K.load(sp, hsel[:, :], A["k_head_sel"])
                K.load(sp, reset[:, :], A["k_reset"])

            @block.tensor
            def _(pe):
                pe.wait_ge(K.loads, loads0 + 80)
                for t in range(NT):
                    for c in range(RW_T):
                        ins = nc.tensor.transpose(ps[:, t, c * P:(c + 1) * P], feat[:, 8 + c, t * P:(t + 1) * P],
                                                  K.ident[:, :])
                ins.then_inc(vt, 1)
                pe.wait_ge(tanhd, 1)
                for c in range(RW_T):
                    ins = nc.tensor.matmul(ps[:, 4 + c, :], w2[0:64, c * P:(c + 1) * P], feat[0:64, 12, :], start=True,
                                           stop=True)
                ins.then_inc(wdone, 1)
                pe.wait_ge(vc, 1)
                for c in range(RW_T):
                    ins = nc.tensor.matmul(ps[:, c, :], w2[64:128, c * P:(c + 1) * P], feat[64:128, 12, :], start=True,
                                           stop=True)
                ins.then_inc(adone, 1)
                pe.wait_ge(sqd, 1)
                pe.wait_ge(sigw, 1)
                for c in range(RW_T):
                    ins = nc.tensor.matmul(ps[:, 4 + c, :], same[:, :], e[:, c, :], start=True, stop=True)
                ins.then_inc(nsum, 1)
                pe.wait_ge(prod, 1)
                pe.wait_ge(siga, 1)
                for t in range(NT):
                    for c in range(RW_T):
                        ins = nc.tensor.matmul(ps[:, 0, t * 8 + 2 * c:t * 8 + 2 * c + 2], e[:, c, t * P:(t + 1) * P],
                                               hsel[:, :], start=True, stop=True)
                ins.then_inc(bonusd, 1)

            @block.scalar
            def _(sc):
                nc.scalar.activation(feat[0:64, 12, :], feat[0:64, 12, :], ACT.Tanh).then_inc(tanhd, 1)
                nc.scalar.activation(sgT, feat[:, 13, :], ACT.Sigmoid)
                sc.wait_ge(vt, 1)
                nc.scalar.activation(vtok, ps[:, 0:4, :], ACT.Copy).then_inc(vc, 1)
                sc.wait_ge(wdone, 1)
                for c in range(RW_T):
                    ins = nc.scalar.activation(ld[:, c, :], ps[:, 4 + c, :], ACT.Sigmoid, bias=col("w0", RW_T)[:, c:c + 1])
                ins.then_inc(sigw, 1)
                sc.wait_ge(adone, 1)
                for c in range(RW_T):
                    ins = nc.scalar.activation(a[:, c, :], ps[:, c, :], ACT.Sigmoid, bias=col("a0", RW_T)[:, c:c + 1])
                ins.then_inc(siga, 1)
                sc.wait_ge(nclamp, 1)
                nc.scalar.activation(beta, beta, ACT.Sqrt).then_inc(nroot, 1)
                sc.wait_ge(bsum, 1)
                nc.scalar.activation(ld[:, :, :], ld[:, :, :], ACT.Exp).then_inc(exps, 1)
                sc.wait_ge(bonusd, 1)
                nc.scalar.activation(e[:, :, :], b[:, :, :], ACT.Exp).then_inc(exps, 1)
                nc.scalar.activation(b[:, :, :], b[:, :, :], ACT.Exp, scale=-1.0).then_inc(exps, 1)

            @block.vector
            def _(ve):
                ve.wait_ge(K.loads, loads0 + 80)
                K.dve_link(nc.vector.tensor_tensor(alpha, k, cb("k_k"), ALU.mult))
                nc.vector.tensor_tensor(e[:, :, :], alpha, alpha, ALU.mult).then_inc(sqd, 1)
                ve.wait_ge(nsum, 1)
                nc.vector.tensor_scalar(beta, ps[:, 4:8, :], 1e-24, None, ALU.max).then_inc(nclamp, 1)
                ve.wait_ge(nroot, 1)
                K.dve_link(nc.vector.reciprocal(beta, beta))
                K.dve_link(nc.vector.tensor_tensor(alpha, alpha, beta, ALU.mult))
                K.dve_link(nc.vector.tensor_scalar(omk[:, :], col("k_a", RW_T), -1.0, 1.0, ALU.mult, ALU.add))
                ve.wait_ge(siga, 1)
                for c in range(RW_T):
                    K.dve_link(nc.vector.tensor_scalar(beta[:, c, :], a[:, c, :], col("k_a", RW_T)[:, c:c + 1],
                                                       omk[:, c:c + 1], ALU.mult, ALU.add))
                K.dve_link(nc.vector.tensor_tensor(k, k, beta, ALU.mult))
                K.dve_link(nc.vector.tensor_tensor(beta, r, k, ALU.mult))
                nc.vector.tensor_tensor(e[:, :, :], beta, cb("r_k"), ALU.mult).then_inc(prod, 1)
                ve.wait_ge(prod, 1)
                K.dve_link(nc.vector.tensor_tensor(beta, alpha, a[:, :, :], ALU.mult))
                ve.wait_ge(sigw, 1)
                K.dve_link(nc.vector.tensor_scalar(ld[:, :, :], ld[:, :, :], DECAY_SCALE, None, ALU.mult))
                for c in range(RW_T):
                    K.dve_link(nc.vector.tensor_tensor_scan(b[:, c, :], reset[:, :], ld[:, c, :], 0.0, ALU.mult, ALU.add))
                nc.vector.tensor_tensor(ld[:, :, :], b[:, :, :], ld[:, :, :], ALU.subtract).then_inc(bsum, 1)
                ve.wait_ge(bonusd, 1)
                nc.vector.tensor_copy(bonus, ps[:, 0, 0:NT * 8])
                ve.wait_ge(exps, 3)
                K.dve_link(nc.vector.tensor_tensor(alpha, alpha, ld[:, :, :], ALU.mult))
                K.dve_link(nc.vector.tensor_tensor(beta, beta, b[:, :, :], ALU.mult))
                K.dve_link(nc.vector.tensor_tensor(k, k, b[:, :, :], ALU.mult))
                K.dve_link(nc.vector.tensor_tensor(r, r, e[:, :, :], ALU.mult))
                K.dve_link(nc.vector.tensor_copy(decay_end, e[:, :, RWKV_C - 1::RWKV_C]))


def rwkv_scan(K, rho, alpha, beta, kappa, decay_end, vtok, y, spare):
    nc, ps, A = K.nc, K.ps, K.A
    n_ = lambda s: K.sem(f"rs_{s}")
    tr, tok_ready, ab, ak, mb, ab_m, ak_m, mb_m, t_ready, off_ready, xd, x_ready, tx, t_new = (
        n_(s) for s in "tr tok ab ak mb abm akm mbm t off x xready tx tnew".split())
    zd, r_ready, ud, u_ready, p6, rho_ready, y0_ready, ghd, gh_ready, ch, s_ready, yd, y_ready = (
        n_(s) for s in "z rready u uready p6 rho y0 gh ghready chain state y yready".split())
    loads0 = K.loads_n
    H = RW_H
    L = len(LEVELS)
    with ExitStack() as ctx:
        masks = K.sb(ctx, "rs_masks", [P, 4 + L, P])
        id2 = K.sb(ctx, "rs_id2", [P, HD])
        tok = K.sb(ctx, "rs_tokb", [P, 3, 512])
        abT = K.sb(ctx, "rs_abT", [P, H, P])
        akT = K.sb(ctx, "rs_akT", [P, H, P])
        mkT = K.sb(ctx, "rs_mkT", [P, H, P])
        mbT = K.sb(ctx, "rs_mbT", [P, H, P])
        by_head = lambda a: a.rearrange("p a (c n) -> p (a c) n", n=P)
        T, TT, X = by_head(K.hT[:, 4:6, :]), by_head(K.hT[:, 6:8, :]), by_head(spare)
        off = K.sb(ctx, "rs_offb", [P, H, P])
        halves = akT[:, :, :].rearrange("p (a b) n -> p a (b n)", a=2)
        at, un = (halves[:, i, :].rearrange("p (h d) -> p h d", d=HD) for i in range(2))
        rt = K.sb(ctx, "rs_rt", [P, RW_T, P])
        y0 = K.sb(ctx, "rs_y0b", [P, H, HD])
        st = K.sb(ctx, "rs_st", [P, CT + 1, RW_T, HD])
        G = K.hT[:, 0:2, :].rearrange("p a (b c d) -> p (a b) c d", c=RW_T, d=HD)
        Hn = K.hT[:, 2:4, :].rearrange("p a (b c d) -> p (a b) c d", c=RW_T, d=HD)
        R = off
        two = lambda b: ps[:, b:b + 2, :].rearrange("p m (c n) -> p (m c) n", n=P)
        mask = lambda i: masks[:, i, :].unsqueeze(1).to_broadcast([P, H, P])
        ident = K.ident[:, :].unsqueeze(1).to_broadcast([P, H, P])
        head = lambda i, hh: tok[:, i, (hh % 4) * P + (hh // 4) * HD:(hh % 4) * P + (hh // 4) * HD + HD]
        with nc.Block() as block:
            @block.sync
            def _(sp):
                K.load(sp, masks[:, :, :], A["k_rwkv"])
                K.load(sp, id2[:, :], A["k_id2"])

            @block.tensor
            def _(pe):
                pe.wait_ge(K.loads, loads0 + 32)
                for t in range(NT):
                    ts = slice(t * P, (t + 1) * P)

                    def pairs(bank, lhs, rhs):
                        for m in range(2):
                            for c in range(RW_T):
                                r = slice(m * HD, (m + 1) * HD)
                                ins = nc.tensor.matmul(ps[:, bank[m], c * P:(c + 1) * P], lhs[r, c, ts], rhs[r, c, ts],
                                                       start=True, stop=True)
                        return ins

                    if t:
                        pe.wait_ge(y_ready, t)
                    for i, src in enumerate((alpha, beta, kappa)):
                        for c in range(RW_T):
                            ins = nc.tensor.transpose(ps[:, i, c * P:(c + 1) * P], src[:, c, ts], K.ident[:, :])
                    ins.then_inc(tr, 1)
                    pairs((3, 4), beta, alpha)
                    pairs((5, 6), alpha, beta).then_inc(ab, 1)
                    pe.wait_ge(tok_ready, t + 1)
                    pairs((0, 1), kappa, alpha)
                    pairs((2, 7), kappa, rho).then_inc(ak, 1)
                    pe.wait_ge(ab_m, t + 1)
                    pairs((3, 4), beta, rho).then_inc(mb, 1)
                    pe.wait_ge(ak_m, t + 1)
                    pe.wait_ge(mb_m, t + 1)
                    for l in range(L):
                        n = t * L + l
                        pe.wait_ge(off_ready, n + 1)
                        pe.wait_ge(t_new, n + t + 1)
                        for hh in range(H):
                            ins = nc.tensor.matmul(ps[:, hh // 4, (hh % 4) * P:(hh % 4 + 1) * P], off[:, hh, :],
                                                   T[:, hh, :], start=True, stop=True)
                        ins.then_inc(xd, 1)
                        pe.wait_ge(x_ready, n + 1)
                        for hh in range(H):
                            nc.tensor.matmul(ps[:, 3 + hh // 4, (hh % 4) * P:(hh % 4 + 1) * P], X[:, hh, :],
                                             TT[:, hh, :], start=True, stop=True)
                            ins = nc.tensor.matmul(ps[:, 5 + hh // 4, (hh % 4) * P:(hh % 4 + 1) * P], TT[:, hh, :],
                                                   X[:, hh, :], start=True, stop=True)
                        ins.then_inc(tx, 1)
                    for hh in range(H):
                        ins = nc.tensor.matmul(ps[:, 0, hh * HD:(hh + 1) * HD], akT[:, hh, :],
                                               vtok[:, t, (hh % 4) * P + (hh // 4) * HD:(hh % 4) * P + (hh // 4) * HD + HD],
                                               start=True, stop=True)
                    ins.then_inc(zd, 1)
                    pe.wait_ge(r_ready, t + 1)
                    pe.wait_ge(t_new, (t + 1) * (L + 1))
                    for hh in range(H):
                        ins = nc.tensor.matmul(ps[:, 5 + hh // 4, (hh % 4) * P:(hh % 4 + 1) * P], TT[:, hh, :],
                                               R[:, hh, :], start=True, stop=True)
                    ins.then_inc(ud, 1)
                    pe.wait_ge(u_ready, t + 1)
                    for hh in range(H):
                        m, c = hh // 4, hh % 4
                        nc.tensor.matmul(ps[m * HD:(m + 1) * HD, 1, c * P:(c + 1) * P], at[:, hh, :], mbT[:, hh, :],
                                         start=True, stop=True)
                    for hh in range(H):
                        vh = vtok[:, t, (hh % 4) * P + (hh // 4) * HD:(hh % 4) * P + (hh // 4) * HD + HD]
                        nc.tensor.matmul(ps[:, 7, hh * HD:(hh + 1) * HD], mkT[:, hh, :], vh, start=True, stop=False)
                        ins = nc.tensor.matmul(ps[:, 7, hh * HD:(hh + 1) * HD], mbT[:, hh, :], un[:, hh, :],
                                               start=False, stop=True)
                    ins.then_inc(p6, 1)
                    for cc in range(CT):
                        q = slice(cc * RWKV_C, (cc + 1) * RWKV_C)
                        for hh in range(H):
                            m, c = hh // 4, hh % 4
                            o = slice(m * HD, (m + 1) * HD)
                            ch0 = c * P + m * HD
                            nc.tensor.matmul(ps[o, 2 + cc, c * HD:(c + 1) * HD], at[q, hh, :], tok[q, 1, ch0:ch0 + HD],
                                             start=True, stop=True)
                            hout = ps[o, 2 + cc, 256 + c * HD:256 + (c + 1) * HD]
                            nc.tensor.matmul(hout, tok[q, 2, ch0:ch0 + HD], vtok[q, t, ch0:ch0 + HD], start=True,
                                             stop=False)
                            ins = nc.tensor.matmul(hout, tok[q, 1, ch0:ch0 + HD], un[q, hh, :], start=False, stop=True)
                    ins.then_inc(ghd, 1)
                    pe.wait_ge(gh_ready, t + 1)
                    pe.wait_ge(rho_ready, t + 1)
                    for cc in range(CT):
                        n = t * CT + cc
                        pe.wait_ge(s_ready, n + t + 1)
                        for hh in range(H):
                            m, c = hh // 4, hh % 4
                            o = slice(m * HD, (m + 1) * HD)
                            ins = nc.tensor.matmul(ps[o, cc % 2, c * HD:(c + 1) * HD], G[o, cc, c, :], st[o, cc, c, :],
                                                   start=True, stop=True)
                        ins.then_inc(ch, 1)
                    pe.wait_ge(y0_ready, t + 1)
                    for cc in range(CT):
                        for m in range(2):
                            for c in range(RW_T):
                                o = slice(m * HD, (m + 1) * HD)
                                ins = nc.tensor.matmul(ps[cc * RWKV_C:(cc + 1) * RWKV_C, 6 + m, c * HD:(c + 1) * HD],
                                                       rt[o, c, cc * RWKV_C:(cc + 1) * RWKV_C], st[o, cc, c, :],
                                                       start=True, stop=True)
                    ins.then_inc(yd, 1)

            @block.scalar
            def _(sc):
                for t in range(NT):
                    sc.wait_ge(tr, t + 1)
                    nc.scalar.activation(tok[:, :, :], ps[:, 0:3, :], ACT.Copy).then_inc(tok_ready, 1)
                    for l in range(L):
                        n = t * L + l
                        sc.wait_ge(xd, n + 1)
                        nc.scalar.activation(X[:, :, :], two(0), ACT.Copy).then_inc(x_ready, 1)
                    sc.wait_ge(p6, t + 1)
                    nc.scalar.activation(y0[:, :, :], ps[:, 7, :].rearrange("p (h d) -> p h d", d=HD), ACT.Copy)\
                        .then_inc(y0_ready, 1)

            @block.vector
            def _(ve):
                ve.wait_ge(K.loads, loads0 + 32)
                nc.vector.memset(st[:, 0, :, :], 0.0).then_inc(s_ready, 1)
                for t in range(NT):
                    ve.wait_ge(ab, t + 1)
                    K.dve_link(nc.vector.tensor_tensor(abT[:, :, :], two(3), mask(1), ALU.mult))
                    K.dve_link(nc.vector.tensor_tensor(T[:, :, :], two(5), mask(0), ALU.mult))
                    K.dve_link(nc.vector.tensor_tensor(TT[:, :, :], abT[:, :, :], mask(3 + L), ALU.mult))
                    K.dve_link(nc.vector.tensor_tensor(TT[:, :, :], ident, TT[:, :, :], ALU.subtract))
                    nc.vector.tensor_tensor(T[:, :, :], ident, T[:, :, :], ALU.subtract).then_inc(t_new, 1)
                    ve.wait_ge(t_new, t * (L + 1) + 1)
                    nc.vector.tensor_copy(st[:, 0, :, :], st[:, 0, :, :]).then_inc(ab_m, 1)
                    ve.wait_ge(ak, t + 1)
                    nc.vector.tensor_tensor(akT[:, :, :], two(0), mask(1), ALU.mult)
                    for m, bank in enumerate((2, 7)):
                        ins = nc.vector.tensor_tensor(mkT[:, 4 * m:4 * m + 4, :],
                                                      ps[:, bank, :].rearrange("p (c n) -> p c n", n=P),
                                                      masks[:, 2, :].unsqueeze(1).to_broadcast([P, 4, P]), ALU.mult)
                    ins.then_inc(ak_m, 1)
                    ve.wait_ge(mb, t + 1)
                    nc.vector.tensor_tensor(mbT[:, :, :], two(3), mask(2), ALU.mult).then_inc(mb_m, 1)
                    for l in range(L):
                        n = t * L + l
                        if l or t:
                            ve.wait_ge(xd, n)
                        nc.vector.tensor_tensor(off[:, :, :], abT[:, :, :], mask(3 + l), ALU.mult)\
                            .then_inc(off_ready, 1)
                        ve.wait_ge(tx, n + 1)
                        if l < L - 1:
                            K.dve_link(nc.vector.tensor_tensor(T[:, :, :], T[:, :, :], two(5), ALU.subtract))
                        nc.vector.tensor_tensor(TT[:, :, :], TT[:, :, :], two(3), ALU.subtract).then_inc(t_new, 1)
                        ve.wait_ge(t_new, n + t + 2)
                    ve.wait_ge(zd, t + 1)
                    nc.vector.tensor_copy(R[:, :, HD:], ps[:, 0, :].rearrange("p (h d) -> p h d", d=HD))
                    nc.vector.tensor_copy(R[:, :, 0:HD].rearrange("p (m c) d -> p m c d", m=2),
                                          tok[:, 0, :].rearrange("p (c m d) -> p m c d", m=2, d=HD)).then_inc(r_ready, 1)
                    ve.wait_ge(ud, t + 1)
                    nc.vector.tensor_copy(at[:, :, :], two(5)[:, :, 0:HD])
                    nc.vector.tensor_scalar(un[:, :, :], two(5)[:, :, HD:], -1.0, None, ALU.mult).then_inc(u_ready, 1)
                    ve.wait_ge(p6, t + 1)
                    nc.vector.tensor_tensor(rt[:, :, :], rho[:, :, t * P:(t + 1) * P],
                                            ps[:, 1, :].rearrange("p (c n) -> p c n", n=P), ALU.subtract)\
                        .then_inc(rho_ready, 1)
                    ve.wait_ge(ghd, t + 1)
                    gh = ps[:, 2:6, :].rearrange("p c (g n d) -> p c g n d", g=2, d=HD)
                    W = decay_end[:, :, t * CT:(t + 1) * CT]
                    for cc in range(CT):
                        nc.vector.tensor_tensor(G[:, cc, :, :], id2[:, :].unsqueeze(1).to_broadcast([P, RW_T, HD]),
                                                gh[:, cc, 0, :, :], ALU.subtract)
                        ins = nc.vector.tensor_tensor(Hn[:, cc, :, :], gh[:, cc, 1, :, :],
                                                      W[:, :, cc:cc + 1].to_broadcast([P, RW_T, HD]), ALU.mult)
                    K.dve_link(ins)
                    nc.vector.tensor_copy(st[:, CT, 0, 0:1], st[:, 0, 0, 0:1]).then_inc(gh_ready, 1)
                    for cc in range(CT):
                        n = t * CT + cc
                        ve.wait_ge(ch, n + 1)
                        K.dve_link(nc.vector.tensor_tensor(st[:, cc + 1, :, :],
                                                           ps[:, cc % 2, 0:256].rearrange("p (c d) -> p c d", d=HD),
                                                           W[:, :, cc:cc + 1].to_broadcast([P, RW_T, HD]), ALU.mult))
                        nc.vector.tensor_tensor(st[:, cc + 1, :, :], st[:, cc + 1, :, :], Hn[:, cc, :, :], ALU.add)\
                            .then_inc(s_ready, 1)
                        ve.wait_ge(s_ready, n + t + 2)
                    ve.wait_ge(yd, t + 1)
                    ve.wait_ge(y0_ready, t + 1)
                    nc.vector.tensor_tensor(y[:, t, :].rearrange("p (c m d) -> p m c d", m=2, d=HD),
                                            ps[:, 6:8, 0:256].rearrange("p m (c d) -> p m c d", d=HD),
                                            y0[:, :, :].rearrange("p (m c) d -> p m c d", m=2), ALU.add)\
                        .then_inc(y_ready, 1)
                    if t < NT - 1:
                        nc.vector.tensor_copy(st[:, 0, :, :], st[:, CT, :, :]).then_inc(s_ready, 1)


def rwkv_finish(K, y, sgT, vtok, bonus):
    nc, ps, A = K.nc, K.ps, K.A
    group_norm(K, "rw_gn", y[:, :, :].rearrange("p t (h d) -> p (t h) d", d=HD), NT * RW_H, HD, GN_EPS_3, centre=True)
    gated = K.sem("rf_gate")
    with ExitStack() as ctx:
        g2 = K.sb(ctx, "rf_g2", [P, 512])
        lw = K.sb(ctx, "rf_lw", [P, 2, 512])
        with nc.Block() as block:
            @block.sync
            def _(sp):
                K.load(sp, g2[:, :], A["rwkv_g2_3"][0])
                for i, key in enumerate(("rwkv_ln_w_3", "rwkv_ln_b_3")):
                    K.load(sp, lw[:, i, :], A[key][0].rearrange("(a n) -> a n", a=1).partition_broadcast(P))

            @block.tensor
            def _(pe):
                pe.wait_ge(K.loads, K.loads_n)
                for t in range(NT):
                    ins = nc.tensor.matmul(ps[:, t, :], sgT[:, t * P:(t + 1) * P], g2[:, :], start=True, stop=True)
                ins.then_inc(gated, 1)

            @block.vector
            def _(ve):
                ve.wait_ge(K.loads, K.loads_n)
                for i, op in enumerate((ALU.mult, ALU.add)):
                    K.dve_link(nc.vector.tensor_tensor(y[:, :, :], y[:, :, :],
                                                       lw[:, i, :].unsqueeze(1).to_broadcast([P, NT, 512]), op))
                heads = lambda a: a[:, :, :].rearrange("p t (h d) -> p (t h) d", d=HD)
                K.dve_link(nc.vector.tensor_tensor(heads(vtok), heads(vtok),
                                                   bonus[:, :].unsqueeze(2).to_broadcast([P, NT * RW_H, HD]), ALU.mult))
                K.dve_link(nc.vector.tensor_tensor(y[:, :, :], y[:, :, :], vtok[:, :, :], ALU.add))
                ve.wait_ge(gated, 1)
                K.dve_link(nc.vector.tensor_tensor(y[:, :, :], ps[:, 0:4, :], y[:, :, :], ALU.mult))


def conv_up(K, stage, cw, ffT):
    nc = K.nc
    first, last = K.stream.span[stage]
    units = FFN_T // 2
    copied, conv, sig, made = (K.sem(f"cu_{n}") for n in "copied conv sig made".split())
    with ExitStack() as ctx:
        u = K.sb(ctx, "cu_u", [P, 2, 4, S + 2])
        c = K.sb(ctx, "cu_c", [P, 4, S])
        sg = K.sb(ctx, "cu_sg", [P, 2, S])
        with nc.Block() as block:
            @block.vector
            def _(ve):
                nc.vector.memset(u[:, :, :, 0:2], 0.0)
        with nc.Block() as block:
            @block.sync
            def _(sp):
                K.refill(sp, first, last)

            @block.tensor
            def _(pe):
                for j in range(units):
                    if j >= 2:
                        pe.wait_ge(copied, j - 1)
                    b = 4 * (j % 2)
                    for i in range(2):
                        n = first + 2 * j + i
                        K.wait_chunk(pe, n)
                        K.use_T(pe, n, 256, 0, K.hT, K.ps[:, b + 2 * i, :], False)
                        K.use_T(pe, n, 256, 1, K.hT, K.ps[:, b + 2 * i + 1, :], True)

            @block.scalar
            def _(sc):
                for j in range(units):
                    sc.wait_ge(K.chunk_used, first + 2 * j + 2)
                    if j >= 2:
                        sc.wait_ge(conv, j - 1)
                    nc.scalar.activation(u[:, j % 2, :, 2:], K.ps[:, 4 * (j % 2):4 * (j % 2) + 4, :], ACT.Copy)\
                        .then_inc(copied, 1)
                    sc.wait_ge(conv, j + 1)
                    if j:
                        sc.wait_ge(made, j)
                    nc.scalar.activation(sg[:, :, :], c[:, 0:2, :], ACT.Sigmoid).then_inc(sig, 1)

            @block.vector
            def _(ve):
                steps = 0
                for j in range(units):
                    ve.wait_ge(copied, j + 1)
                    tiles = (2 * j, 2 * j + 1, FFN_T + 2 * j, FFN_T + 2 * j + 1)
                    for tap in (2, 1, 0):
                        for i, n in enumerate(tiles):
                            src = u[:, j % 2, i, tap:tap + S]
                            if tap == 2:
                                ins = nc.vector.tensor_scalar(c[:, i, :], src, cw(2)[:, n:n + 1], cw(3)[:, n:n + 1],
                                                              ALU.mult, ALU.add)
                            else:
                                ins = nc.vector.scalar_tensor_tensor(c[:, i, :], src, cw(tap)[:, n:n + 1], c[:, i, :],
                                                                     ALU.mult, ALU.add)
                            if i == 3 and tap:
                                K.dve_link(ins)
                    ins.then_inc(conv, 1)
                    ve.wait_ge(conv, j + 1)
                    K.dve_link(nc.vector.tensor_tensor(c[:, 2:4, :], c[:, 0:2, :], c[:, 2:4, :], ALU.mult))
                    ve.wait_ge(sig, j + 1)
                    nc.vector.tensor_tensor(ffT[:, 2 * j:2 * j + 2, :], sg[:, :, :], c[:, 2:4, :], ALU.mult)\
                        .then_inc(made, 1)
                    ve.wait_ge(made, j + 1)


def block3(K):
    nc, A = K.nc, K.A
    with ExitStack() as ctx:
        gates = K.sb(ctx, "b3_gates", [P, 2, D])
        mods = K.sb(ctx, "b3_mods", [P, 4, KD])
        names = [("c", "c_3"), ("g1", "norm_mix_3"), ("g2", "norm_ffn_3"), ("mu", "rwkv_mu_3"), ("w0", "rwkv_w0_3"),
                 ("a0", "rwkv_a0_3"), ("k_k", "rwkv_k_k_3"), ("k_a", "rwkv_k_a_3")]
        vectors = [(k, A[n][0]) for k, n in names] + [("r_k", A["rwkv_r_k_3"][0].rearrange("h d -> (h d)"))]
        cols, at = load_columns(K, "b3_cols", vectors, ctx)
        col = lambda key, n: cols[:, at[key]:at[key] + n]
        modulation(K, "mod3", col("c", KD), A["b_mod_3"][0], gates, mods[:, 0, :], mods[:, 1, :], mods[:, 2, :],
                   mods[:, 3, :], col("g1", KD), col("g2", KD))
        with nc.sbuf_tensor("b3_xn", [P, NT, D], F32) as xn:
            normalise(K, "b3_norm", xn, mods[:, 0, :], mods[:, 1, :], K.hT)
        with ExitStack() as mix:
            ya = K.sb(mix, "b3_ya", [P, NT, 512])
            with ExitStack() as att:
                qkT = K.sb(att, "b3_qkT", [P, 8, S])
                v = K.sb(att, "b3_v_", [P, 2, NT, 256])
                f = K.sb(att, "b3_f_", [P, NT, 4])
                nf = K.sb(att, "b3_negF", [P, 4, S])
                linear(K, "b3_qk", "T", K.hT, 1,
                       act=lambda j, b: nc.scalar.activation(qkT[:, 2 * j:2 * j + 2, :], b, ACT.Copy))
                linear(K, "b3_v", "N", K.hT, 1,
                       act=lambda j, b: nc.scalar.activation(v[:, j, :, :], b[:, :, 0:256], ACT.Copy))
                linear(K, "b3_f", "N", K.hT, 1,
                       act=lambda j, b: nc.scalar.activation(f[:, :, :], b[:, :, 0:4], ACT.Copy))
                forget_sums(K, f, nf[:, :, :])
                causal_attention(K, qkT, v, nf, ya)
            sgT = K.sb(mix, "b3_sgT", [P, S])
            bonus = K.sb(mix, "b3_bonus", [P, NT * RW_H])
            wend = K.sb(mix, "b3_wend", [P, RW_T, S // RWKV_C])
            vtok = K.sb(mix, "b3_vtok", [P, NT, 512])
            alpha = K.sb(mix, "b3_alpha", [P, RW_T, S])
            beta = K.sb(mix, "b3_beta", [P, RW_T, S])
            feat = K.sb(mix, "b3_feat", [P, 14, S])
            shifted_features(K, feat, col("mu", 14))
            rwkv_prepare(K, feat, col, alpha[:, :, :], beta[:, :, :], wend[:, :, :], sgT[:, :], vtok[:, :, :],
                         bonus[:, :])
            y = feat[:, 8:12, :]
            rwkv_scan(K, feat[:, 0:4, :], alpha, beta, feat[:, 4:8, :], wend[:, :, :], vtok, y, feat[:, 12:14, :])
            rwkv_finish(K, y, sgT, vtok, bonus)
            turn_tiles(K, "b3_yT",
                       [(lambda t, i=i: ya[:, t, i * P:(i + 1) * P]) for i in range(2)] +
                       [(lambda t, i=i: y[:, t, i * P:(i + 1) * P]) for i in range(4)] +
                       [(lambda t, i=i: ya[:, t, (2 + i) * P:(3 + i) * P]) for i in range(2)],
                       [K.hT[:, i, :] for i in range(8)])
        add_residual(K, "b3_out", K.hT, 2, gate=gates[:, 0, :])
        with nc.sbuf_tensor("b3_xn2", [P, NT, D], F32) as xn:
            normalise(K, "b3_norm2", xn, mods[:, 2, :], mods[:, 3, :], K.hT)
        with ExitStack() as ffn:
            ffT = K.sb(ffn, "b3_ffT", [P, FFN_T, S])
            cw01, _ = load_columns(K, "b3_cw01", [("0", A["conv_w_3"][0, 0]), ("1", A["conv_w_3"][0, 1])], ffn)
            cw2b, _ = load_columns(K, "b3_cw2b", [("2", A["conv_w_3"][0, 2]), ("b", A["conv_b_3"][0])], ffn)
            n = 2 * FFN_T
            conv_up(K, "b3_up", lambda j: (cw01, cw2b)[j // 2][:, (j % 2) * n:(j % 2 + 1) * n], ffT)
            add_residual(K, "b3_down", ffT, 6, gate=gates[:, 1, :])
    final_norm(K, "b3_final", A["norm_final_3"], True)


def t5_bucket(dist, max_dist):
    exact = 16
    d = np.maximum(dist, 1).astype(np.float32)
    large = exact + (np.log(d / np.float32(exact)) / np.float32(math.log(max_dist / exact)) * np.float32(16))\
        .astype(np.int32)
    return np.where(dist < exact, dist, np.minimum(large, 31))


def hot_rows(dist, valid, max_dist):
    out = np.zeros((33, len(dist)), np.float32)
    b = t5_bucket(np.maximum(dist, 0), max_dist)
    for i in range(len(dist)):
        out[b[i] if valid[i] else 32, i] = 1.0
    return out


def shape_constants():
    c = {"k_ident": np.eye(P, dtype=np.float32)}
    half = RDK // 2
    inv = np.float32(10000.0) ** (-np.arange(half, dtype=np.float32) / np.float32(half))
    ang = np.arange(S, dtype=np.float32)[None, :] * inv[:, None]
    c["k_cos"] = np.concatenate([np.cos(ang)] * 2).astype(np.float32)
    c["k_sin"] = np.concatenate([np.sin(ang)] * 2).astype(np.float32)
    rot = np.zeros((P, P), np.float32)
    rot[np.arange(half) + half, np.arange(half)] = -1.0
    rot[np.arange(half), np.arange(half) + half] = 1.0
    c["k_rot"] = rot
    log_g = np.log1p(-np.exp2(-5.0 - np.arange(RH, dtype=np.float64)))
    p, f = np.arange(P)[:, None], np.arange(P)[None, :]
    dist = np.stack([128 * t + f - p for t in range(NT)], 1)
    c["k_decay"] = np.stack([np.where(dist >= 0, np.exp(np.maximum(dist, 0) * g), 0.0) * RDK ** -0.5 for g in log_g],
                            1).astype(np.float32)
    q = np.arange(1024)
    hot = [hot_rows(511 - q, (511 - q >= 0) & (511 - q <= 128), 2048)]
    q = np.arange(256)
    hot.append(hot_rows(4 * (127 - q), 127 - q >= 0, 2048))
    hot.append(hot_rows(4 * (127 - q), (127 - q >= 0) & ((127 - q) % 4 == 0), 2048))
    c["k_hot1"] = np.concatenate(hot, 1)
    c["k_before"] = (p < f).astype(np.float32)
    spans = S // CAP - 1
    ids = np.stack([np.repeat(np.arange(EXPERTS), spans), np.tile(CAP * (1 + np.arange(spans)), EXPERTS)])
    c["k_spans"] = np.broadcast_to(ids.astype(np.float32), (P, 2, EXPERTS * spans)).copy()
    c["k_iota"] = np.broadcast_to(np.arange(CAP, dtype=np.float32), (P, CAP)).copy()
    q = np.arange(640)
    c["k_hot2"] = hot_rows(511 - q, 511 - q >= 0, 128)
    same = p // GC == f // GC
    c["k_gla_tri"] = np.stack([same & (p <= f), same], 1).astype(np.float32)
    c["k_gla_heads"] = (p // GDK == np.arange(GH * GDV)[None, :] // GDV).astype(np.float32)
    bands = []
    for win in WINDOWS:
        inside = (f - p >= 0) & (f - p < win)
        eye = (p == f).astype(np.float32)
        head = inside / np.minimum(f + 1, win).astype(np.float32) - eye
        before = ((f + P - p) < win) / np.float32(win)
        bands.append(np.stack([head, inside / np.float32(win) - eye, before], 1))
    c["k_pool"] = np.stack(bands, 1).astype(np.float32)
    c["k_upto"] = (p <= f).astype(np.float32)
    c["k_future"] = np.where(f > p, np.float32(NEG), np.float32(0.0)).astype(np.float32)
    c["k_same_head"] = (p // HD == f // HD).astype(np.float32)
    c["k_head_sel"] = (p // HD == np.arange(2)[None, :]).astype(np.float32)
    c["k_reset"] = np.broadcast_to((np.arange(S) % RWKV_C != 0).astype(np.float32), (P, S)).copy()
    c["k_id2"] = (p % HD == np.arange(HD)[None, :]).astype(np.float32)
    chunk = p // RWKV_C == f // RWKV_C

    def joins(n):
        return (p // (2 * n) == f // (2 * n)) & (p % (2 * n) >= n) & (f % (2 * n) < n)

    c["k_rwkv"] = np.stack([joins(1), chunk & (p < f), chunk & (p <= f)] + [joins(n).T for n in LEVELS] + [joins(1).T],
                           1).astype(np.float32)
    return c


def build(nc, A, out):
    stream = Stream()
    for plan in PLANS:
        plan(stream, A)
    with ExitStack() as ctx:
        K = Kit(nc, ctx, A, out, stream)
        with nc.Block() as block:
            @block.sync
            def _(sp):
                K.load(sp, K.ident[:, :], A["k_ident"])
                K.load(sp, K.x[:, :, :], A["x"][0].rearrange("(t p) d -> p t d", p=P))
                for n in range(RING):
                    K.issue(sp, n)
                sp.wait_ge(K.loads, K.loads_n)

            @block.vector
            def _(ve):
                nc.vector.memset(K.ones[:, :], 1.0)
        for run in RUNS:
            K.scope(run)


_OUT = (1, S, D)


def kernel(**inputs):
    import concourse.bacc as _bacc
    from concourse.bass_utils import run_bass_kernel_spmd as _run

    nc = _bacc.Bacc("TRN2", target_bir_lowering=False, num_devices=1)
    arrays, A = {}, {}
    for name, a in {**{k: inputs[k] for k in INPUTS}, **shape_constants()}.items():
        a = np.ascontiguousarray(a)
        arrays[f"in_{name}"] = a
        A[name] = nc.dram_tensor(f"in_{name}", a.shape, mybir.dt.from_np(a.dtype), kind="ExternalInput").ap()
    out = nc.dram_tensor("out_0", _OUT, F32, kind="ExternalOutput").ap()
    build(nc, A, out)
    r = _run(nc, [arrays], core_ids=[0])
    return r.results[0]["out_0"]


INPUTS = ["x", "c", "w_ada", "b_ada", "g_mix", "w_in", "rel_bias", "w_ret_o", "w_att_o", "w_o", "g_ffn",
          "w_router", "b_router", "w_mlp1", "b_mlp1", "w_mlp2", "b_mlp2", "g_final", "attn_norm_g_2", "w_in_2",
          "q_norm_g_2", "k_norm_g_2", "lambda_vecs_2", "da_subln_g_2", "rel_bias_2", "gla_gate_w_2",
          "gla_gate_b_2", "gla_norm_g_2", "pool_w_2", "pool_scale_2", "w_out_2", "ffn_norm_g_2", "w_gate_2",
          "w_up_2", "w_down_2", "c_3", "w_mod_3", "b_mod_3", "norm_mix_3", "w_in_3", "fox_f_bias_3",
          "rwkv_mu_3", "rwkv_w0_3", "rwkv_w2_3", "rwkv_a0_3", "rwkv_a2_3", "rwkv_g2_3", "rwkv_k_k_3",
          "rwkv_k_a_3", "rwkv_r_k_3", "rwkv_ln_w_3", "rwkv_ln_b_3", "w_out_3", "norm_ffn_3", "w_up_3",
          "conv_w_3", "conv_b_3", "w_down_3", "norm_final_3"]
PLANS = [plan_block1, plan_block2, plan_block3]
RUNS = [block1, block2, block3]
```

```python
import math
from contextlib import ExitStack

import numpy as np
import concourse.bass as bass
from concourse import mybir

F32 = mybir.dt.float32
F32R = mybir.dt.float32r
I32 = mybir.dt.int32
ALU = mybir.AluOpType
ACT = mybir.ActivationFunctionType
AX = mybir.AxisListType.X

P = 128
D = 1024
S = 512
NT = S // P
KD = D // P
RING = 6
SLOT = 2048
NEG = -1.0e30
EPS = 1e-6
GN_EPS = 1e-5
EXPERTS = 32
TOPK = 4
CAP = 128
SPILLS = S * TOPK // CAP - 1
FFN = 2816
FFN_T = FFN // P
RWKV_C = 32


class Stream:

    def __init__(self):
        self.chunks, self.span, self.slot_loads, self.landed_at = [], {}, [0] * RING, []

    def add(self, stage, chunk):
        n = len(self.chunks)
        first, _ = self.span.get(stage, (n, n))
        self.span[stage] = (first, n + 1)
        self.chunks.append(chunk)
        self.slot_loads[n % RING] += len(chunk)
        self.landed_at.append(16 * self.slot_loads[n % RING])


    def further_loads(self, per_slot):
        self.slot_loads = [n + per_slot for n in self.slot_loads]


def columns(w, *spans):
    width = sum(n for _, n in spans)
    parts, at = [], 0
    for c0, n in spans:
        parts.append((width, at, n, w[:, c0:c0 + n].rearrange("(k p) n -> p k n", p=P)))
        at += n
    return parts


def rows(w, k0, nk, c0, n=512):
    return [(n, 0, n, w[k0 * P:(k0 + nk) * P, c0:c0 + n].rearrange("(k p) n -> p k n", p=P))]


class Kit:

    def __init__(self, nc, ctx, A, out, stream):
        self.nc, self.ctx, self.A, self.out, self.stream, self.scoped = nc, ctx, A, out, stream, []
        self.ring = self.sb(ctx, "ring", [P, RING, SLOT])
        self.x = self.sb(ctx, "x_res", [P, NT, D])
        self.hT = self.sb(ctx, "hT", [P, KD, S])
        self.ident = self.sb(ctx, "identity", [P, P])
        self.ones = self.sb(ctx, "ones", [P, P])
        self.ps = ctx.enter_context(nc.psum_tensor("psum", [P, 8, 512], F32))
        self.landed = [self.sem(f"slot{i}_landed") for i in range(RING)]
        self.chunk_used = self.sem("chunk_used")
        self.act_evac, self.act_evac_n = self.sem("act_evac"), 0
        self.dve_evac, self.dve_evac_n = self.sem("dve_evac"), 0
        self.act_order, self.act_order_n = self.sem("act_order"), 0
        self.dve_order, self.dve_order_n = self.sem("dve_order"), 0
        self.loads, self.loads_n = self.sem("loads"), 0
        self.stores, self.stores_n = self.sem("stores"), 0
        self.x_source, self.x_loaded = A["x"][0].rearrange("(t p) d -> p t d", p=P), self.sem("x_loaded")

    def sb(self, ctx, name, shape, dt=F32):
        return ctx.enter_context(self.nc.sbuf_tensor(name, shape, dt))

    def sem(self, name):
        sem = self.ctx.enter_context(self.nc.semaphore(name))
        self.scoped.append(sem)
        return sem

    def scope(self, run):
        self.scoped = []
        with ExitStack() as ctx:
            outer, self.ctx = self.ctx, ctx
            run(self)
            with self.nc.Block() as block:
                @block.sync
                def _(sp):
                    for sem in self.scoped:
                        sp.sem_clear(sem)
            self.ctx = outer

    def load(self, eng, dst, src, **kw):
        eng.dma_start(dst, src, **kw).then_inc(self.loads, 16)
        self.loads_n += 16

    def store(self, eng, dst, src, **kw):
        eng.dma_start(dst, src, **kw).then_inc(self.stores, 16)
        self.stores_n += 16

    def act_link(self, ins):
        self.act_order_n += 1
        ins.then_inc(self.act_order, 1)
        self.nc.scalar.wait_ge(self.act_order, self.act_order_n)

    def dve_link(self, ins):
        self.dve_order_n += 1
        ins.then_inc(self.dve_order, 1)
        self.nc.vector.wait_ge(self.dve_order, self.dve_order_n)

    def slot(self, n, width=512):
        return self.ring[:, n % RING, :].rearrange("p (k n) -> p k n", n=width)

    def issue(self, sp, n):
        for width, at, cols, src in self.stream.chunks[n]:
            nk = src.shape[1]
            dst = self.ring[:, n % RING, 0:nk * width].rearrange("p (k n) -> p k n", n=width)
            sp.dma_start(dst[:, :, at:at + cols], src).then_inc(self.landed[n % RING], 16)

    def refill(self, sp, first, last):
        for n in range(first, last):
            if n + RING < len(self.stream.chunks):
                sp.wait_ge(self.chunk_used, n + 1)
                self.issue(sp, n + RING)

    def wait_chunk(self, pe, n):
        pe.wait_ge(self.landed[n % RING], self.stream.landed_at[n])

    def use_T(self, pe, n, width, tile, src, out, last, m=P, sub=slice(None), nk=KD):
        w = self.slot(n, width)
        for k in range(nk):
            ins = self.nc.tensor.matmul(out, w[:, k, tile * P:tile * P + m], src[:, k, sub], start=(k == 0),
                                        stop=(k == nk - 1))
        if last:
            ins.then_inc(self.chunk_used, 1)
        return ins


def linear(K, stage, kind, src, per_unit, act=None, dve=None, act_runs_ahead=2):
    nc = K.nc
    first, last = K.stream.span[stage]
    units = (last - first) // per_unit
    assert units * per_unit == last - first
    banks = 2 * per_unit if kind == "T" else NT
    flight = 8 // banks
    freed, freed0 = (K.dve_evac, K.dve_evac_n) if dve else (K.act_evac, K.act_evac_n)
    act0, dve0 = K.act_evac_n, K.dve_evac_n

    def unit_banks(j):
        b = (j % flight) * banks
        return K.ps[:, b:b + banks, :]

    with nc.Block() as block:
        @block.sync
        def _(sp):
            K.refill(sp, first, last)

        @block.tensor
        def _(pe):
            for j in range(units):
                if j >= flight:
                    pe.wait_ge(freed, freed0 + j - flight + 1)
                out = unit_banks(j)
                k0 = 0
                total = sum(K.stream.chunks[first + j * per_unit + c][0][3].shape[1] for c in range(per_unit))
                for c in range(per_unit):
                    n = first + j * per_unit + c
                    K.wait_chunk(pe, n)
                    width = K.stream.chunks[n][0][0]
                    nk = K.stream.chunks[n][0][3].shape[1]
                    if kind == "T":
                        K.use_T(pe, n, width, 0, src, out[:, 2 * c, :], False)
                        K.use_T(pe, n, width, 1, src, out[:, 2 * c + 1, :], True)
                        continue
                    w = K.slot(n, width)
                    for t in range(NT):
                        for k in range(nk):
                            ins = nc.tensor.matmul(out[:, t, 0:width], src[:, k0 + k, t * P:(t + 1) * P], w[:, k, :],
                                                   start=(k0 + k == 0), stop=(k0 + k == total - 1))
                    ins.then_inc(K.chunk_used, 1)
                    k0 += nk

        if act:
            @block.scalar
            def _(sc):
                for j in range(units):
                    sc.wait_ge(K.chunk_used, first + (j + 1) * per_unit)
                    if dve and j >= act_runs_ahead:
                        sc.wait_ge(K.dve_evac, dve0 + j - act_runs_ahead + 1)
                    act(j, unit_banks(j)).then_inc(K.act_evac, 1)

        if dve:
            @block.vector
            def _(ve):
                for j in range(units):
                    if act:
                        ve.wait_ge(K.act_evac, act0 + j + 1)
                    ve.wait_ge(K.chunk_used, first + (j + 1) * per_unit)
                    dve(j, unit_banks(j)).then_inc(K.dve_evac, 1)
    if act:
        K.act_evac_n += units
    if dve:
        K.dve_evac_n += units


HALF = SLOT // 2


class SplitWeights:

    def __init__(self, K, ctx, stage):
        self.K, self.nc = K, K.nc
        self.first, self.last = K.stream.span[stage]
        self.w = K.sb(ctx, f"{stage}_w", [P, 2, 2, HALF], F32R)
        self.rounded, self.split = K.sem(f"{stage}_rounded"), K.sem(f"{stage}_split")
        self.first_used = K.sem(f"{stage}_first_used")
        self.halves = {}
        for n in range(self.first, self.last):
            nk = K.stream.chunks[n][0][3].shape[1]
            self.halves[n] = [(0, nk // 2, 0), (nk // 2, nk // 2, 1)]

    def number(self, n, place):
        return 2 * (n - self.first) + place + 1

    def wait_free(self, eng, n, place):
        if place == 0 and n > self.first:
            eng.wait_ge(self.first_used, n - self.first)
        if place == 1 and n > self.first:
            eng.wait_ge(self.K.chunk_used, n)

    def views(self, n, place):
        width = self.K.stream.chunks[n][0][0]
        r0, nr, _ = [h for h in self.halves[n] if h[2] == place][0]
        high, low = (self.w[:, place, part, 0:nr * width] for part in range(2))
        return self.K.ring[:, n % RING, r0 * width:(r0 + nr) * width], high, low

    def act_high(self, sc, n, place):
        raw, high, _ = self.views(n, place)
        self.K.wait_chunk(sc, n)
        self.wait_free(sc, n, place)
        self.nc.scalar.activation(high, raw, ACT.Copy).then_inc(self.rounded, 1)

    def pool(self, po):
        for n in range(self.first, self.last):
            for _, _, place in self.halves[n]:
                raw, high, low = self.views(n, place)
                po.wait_ge(self.rounded, self.number(n, place))
                self.nc.gpsimd.tensor_tensor(low, raw, high.bitcast(F32), ALU.subtract).then_inc(self.split, 1)

    def ready(self, pe, n, place):
        pe.wait_ge(self.split, self.number(n, place))
        width = self.K.stream.chunks[n][0][0]
        return self.w[:, place, :, :].rearrange("p s (k n) -> p s k n", n=width)

    def used(self, ins, place):
        ins.then_inc(self.K.chunk_used if place else self.first_used, 1)

    def rows(self, out, x, w, r0, nr, opens, closes):
        for k in range(nr):
            for a, b in ((0, 0), (1, 0), (0, 1)):
                ins = self.nc.tensor.matmul(out, x(a, r0 + k), w[:, b, k, :],
                                            start=(opens and r0 + k + a + b == 0),
                                            stop=(closes and r0 + k == KD - 1 and b == 1))
        return ins

    def tiles(self, pe, n, pair, out):
        nk = self.K.stream.chunks[n][0][3].shape[1]
        for r0, nr, place in self.halves[n]:
            w = self.ready(pe, n, place)
            for tile in range(2):
                cols = slice(tile * P, (tile + 1) * P)
                for k in range(nr):
                    for a, b in ((0, 0), (1, 0), (0, 1)):
                        ins = self.nc.tensor.matmul(out[:, tile, :], w[:, a, k, cols], pair[:, b, r0 + k, :],
                                                    start=(r0 + k + a + b == 0), stop=(r0 + k == nk - 1 and b == 1))
            self.used(ins, place)


def split_rows(K, name, src, pair):
    nc = K.nc
    rounded = K.sem(f"{name}_rounded")
    with nc.Block() as block:
        @block.scalar
        def _(sc):
            for k in range(0, KD, 2):
                nc.scalar.activation(pair[:, 0, k:k + 2, :], src[:, k:k + 2, :], ACT.Copy).then_inc(rounded, 1)

        @block.vector
        def _(ve):
            for k in range(0, KD, 2):
                ve.wait_ge(rounded, k // 2 + 1)
                nc.vector.tensor_tensor(pair[:, 1, k:k + 2, :], src[:, k:k + 2, :], pair[:, 0, k:k + 2, :].bitcast(F32),
                                        ALU.subtract)


def linear_split(K, stage, kind, src, per_unit, act=None, dve=None, act_runs_ahead=2, paired=True):
    nc = K.nc
    first, last = K.stream.span[stage]
    units = (last - first) // per_unit
    assert units * per_unit == last - first and (paired or kind == "N")
    banks = 2 * per_unit if kind == "T" else NT
    flight = 8 // banks
    freed, freed0 = (K.dve_evac, K.dve_evac_n) if dve else (K.act_evac, K.act_evac_n)
    act0, dve0 = K.act_evac_n, K.dve_evac_n

    def unit_banks(j):
        b = (j % flight) * banks
        return K.ps[:, b:b + banks, :]

    with ExitStack() as ctx:
        W = SplitWeights(K, ctx, stage)
        rows_of = {}
        for j in range(units):
            at = 0
            for c in range(per_unit):
                n = first + j * per_unit + c
                for r0, nr, place in W.halves[n]:
                    rows_of[n, place] = (at + r0, nr)
                at += K.stream.chunks[n][0][3].shape[1] if kind == "N" else 0
        total = at
        order = [(n, place) for n in range(first, last) for _, _, place in W.halves[n]]
        per = len(order) // units
        if not paired:
            parts = K.sb(ctx, f"{stage}_a", [P, 2, 2, 2, S], F32R)
            a_high, a_split = K.sem(f"{stage}_a_high"), K.sem(f"{stage}_a_split")

        def split_source(eng, i):
            n, place = order[i]
            r, nr = rows_of[n, place]
            high = parts[:, place, 0, 0:nr, :]
            if eng is nc.scalar:
                W.wait_free(eng, n, place)
                eng.activation(high, src[:, r:r + nr, :], ACT.Copy).then_inc(a_high, 1)
            else:
                eng.wait_ge(a_high, i + 1)
                eng.tensor_tensor(parts[:, place, 1, 0:nr, :], src[:, r:r + nr, :], high.bitcast(F32), ALU.subtract)\
                    .then_inc(a_split, 1)

        def take_units(eng, take):
            for j in range(units + 1):
                for i in range(per):
                    if j < units and eng is nc.scalar:
                        W.act_high(nc.scalar, *order[j * per + i])
                    if j < units and not paired:
                        split_source(eng, j * per + i)
                    if i == 1 and j and take:
                        take(j - 1)

        with nc.Block() as block:
            @block.sync
            def _(sp):
                K.refill(sp, first, last)

            @block.gpsimd
            def _(po):
                W.pool(po)

            @block.tensor
            def _(pe):
                for j in range(units):
                    if j >= flight:
                        pe.wait_ge(freed, freed0 + j - flight + 1)
                    out = unit_banks(j)
                    for i in range(j * per, (j + 1) * per):
                        n, place = order[i]
                        if kind == "T":
                            if i == 0 or order[i - 1][0] != n:
                                c = n - first - j * per_unit
                                W.tiles(pe, n, src, out[:, 2 * c:2 * c + 2, :])
                            continue
                        w = W.ready(pe, n, place)
                        width = K.stream.chunks[n][0][0]
                        r, nr = rows_of[n, place]
                        if paired:
                            x = src[:, :, r:r + nr, :]
                        else:
                            pe.wait_ge(a_split, i + 1)
                            x = parts[:, place, :, 0:nr, :]
                        for t in range(NT):
                            for k in range(nr):
                                for a, b in ((0, 0), (1, 0), (0, 1)):
                                    ins = nc.tensor.matmul(out[:, t, 0:width], x[:, a, k, t * P:(t + 1) * P],
                                                           w[:, b, k, :], start=(r + k + a + b == 0),
                                                           stop=(r + k == total - 1 and b == 1))
                        W.used(ins, place)

            @block.scalar
            def _(sc):
                def take(j):
                    sc.wait_ge(K.chunk_used, first + (j + 1) * per_unit)
                    if dve and j >= act_runs_ahead:
                        sc.wait_ge(K.dve_evac, dve0 + j - act_runs_ahead + 1)
                    act(j, unit_banks(j)).then_inc(K.act_evac, 1)
                take_units(nc.scalar, take if act else None)

            if dve or not paired:
                @block.vector
                def _(ve):
                    def take(j):
                        if act:
                            ve.wait_ge(K.act_evac, act0 + j + 1)
                        ve.wait_ge(K.chunk_used, first + (j + 1) * per_unit)
                        dve(j, unit_banks(j)).then_inc(K.dve_evac, 1)
                    take_units(nc.vector, take if dve else None)
    if act:
        K.act_evac_n += units
    if dve:
        K.dve_evac_n += units


def load_columns(K, name, vectors, ctx):
    nc = K.nc
    at, r = {}, 0
    for key, v in vectors:
        at[key] = r
        r += v.shape[0] // P
    assert r <= P
    cols = K.sb(ctx, name, [P, r])
    turned, copied = K.sem(f"{name}_turned"), K.sem(f"{name}_copied")
    with nc.sbuf_tensor(f"{name}_rows", [P, P], F32) as raw:
        with nc.Block() as block:
            @block.sync
            def _(sp):
                for key, v in vectors:
                    n = v.shape[0] // P
                    K.load(sp, raw[at[key]:at[key] + n, :], v.rearrange("(k p) -> k p", p=P))

            @block.tensor
            def _(pe):
                pe.wait_ge(K.loads, K.loads_n)
                nc.tensor.transpose(K.ps[:, 0, 0:r], raw[0:r, :], K.ident[0:r, 0:r]).then_inc(turned, 1)

            @block.vector
            def _(ve):
                ve.wait_ge(turned, 1)
                nc.vector.tensor_copy(cols[:, :], K.ps[:, 0, 0:r]).then_inc(copied, 1)
    return cols, at


def modulation(K, stage, c_cols, bias, gates, scale1, shift1, scale2, shift2, g1, g2):
    nc = K.nc
    first, last = K.stream.span[stage]
    sig_done, cs_done, evac = K.sem(f"{stage}_sig"), K.sem(f"{stage}_cs"), K.sem(f"{stage}_evac")
    with ExitStack() as ctx:
        sg = K.sb(ctx, f"{stage}_sg", [P, KD])
        cs = K.sb(ctx, f"{stage}_c", [P, KD, P])
        cv = K.sb(ctx, f"{stage}_cv", [P, KD])
        brow = K.sb(ctx, f"{stage}_b", [P, 512])
        sel = K.sb(ctx, f"{stage}_sel", [P, 12, P])
        diag = K.sb(ctx, f"{stage}_diag", [P, 4, P])
        cols = K.sb(ctx, f"{stage}_cols", [P, 6, KD])
        with nc.Block() as block:
            @block.sync
            def _(sp):
                K.load(sp, brow[0:12, :], bias.rearrange("(s n) -> s n", n=512))
                if K.x_source is not None:
                    for n in range(RING):
                        K.issue(sp, n)
                    sp.dma_start(K.x[:, :, :], K.x_source).then_inc(K.x_loaded, 16)
                K.refill(sp, first, last)
                if K.x_source is not None:
                    sp.wait_ge(K.x_loaded, 16)
                    K.x_source = None

            @block.scalar
            def _(sc):
                nc.scalar.activation(sg[:, :], c_cols, ACT.Sigmoid).then_inc(sig_done, 1)

            @block.tensor
            def _(pe):
                pe.wait_ge(cs_done, 1)
                pe.wait_ge(K.loads, K.loads_n)
                for s in range(12):
                    if s >= 8:
                        pe.wait_ge(evac, s - 7)
                    out = K.ps[:, s % 8, :]
                    nc.tensor.matmul(out, sel[0:12, s, :], brow[0:12, :], start=True, stop=False)
                    for c in range(2):
                        n = first + 2 * s + c
                        K.wait_chunk(pe, n)
                        for k in range(4):
                            ins = nc.tensor.matmul(out, cs[:, 4 * c + k, :], K.slot(n)[:, k, :], start=False,
                                                   stop=(c == 1 and k == 3))
                        ins.then_inc(K.chunk_used, 1)

            @block.vector
            def _(ve):
                ve.wait_ge(sig_done, 1)
                K.dve_link(nc.vector.tensor_tensor(cv[:, :], sg[:, :], c_cols, ALU.mult))
                nc.vector.tensor_copy(sel[:, :, :], K.ident[:, 0:12].unsqueeze(2).to_broadcast([P, 12, P]))
                nc.vector.tensor_copy(cs[:, :, :], cv[:, :].unsqueeze(2).to_broadcast([P, KD, P])).then_inc(cs_done, 1)
                for s in range(12):
                    ve.wait_ge(K.chunk_used, first + 2 * s + 2)
                    out, sec, half = K.ps[:, s % 8, :], s // 2, s % 2
                    if sec in (2, 5):
                        nc.vector.tensor_copy(gates[:, sec // 3, half * 512:(half + 1) * 512], out).then_inc(evac, 1)
                        continue
                    K.dve_link(nc.vector.tensor_tensor(diag[:, :, :], out.rearrange("p (k q) -> p k q", q=P),
                                                       K.ident[:, :].unsqueeze(1).to_broadcast([P, 4, P]), ALU.mult))
                    K.dve_link(nc.vector.tensor_reduce(cols[:, sec, half * 4:half * 4 + 4], diag[:, :, :], AX,
                                                       ALU.add))
                    nc.vector.tensor_copy(sg[:, 0:1], cols[:, sec, 0:1]).then_inc(evac, 1)
                for scale, shift, g, sec in ((scale1, shift1, g1, 0), (scale2, shift2, g2, 3)):
                    K.dve_link(nc.vector.tensor_copy(shift, cols[:, sec, :]))
                    K.dve_link(nc.vector.scalar_tensor_tensor(scale, cols[:, sec + 1, :], 1.0, g, ALU.add, ALU.mult))




def normalise(K, name, xn, scale, shift, dst):
    nc = K.nc
    squared, var, root, normed, turned = (K.sem(f"{name}_{s}") for s in ("squared", "var", "root", "normed", "turned"))
    with ExitStack() as ctx:
        ss = K.sb(ctx, f"{name}_ss", [P, NT])
        sd = K.sb(ctx, f"{name}_sd", [P, NT])
        with nc.Block() as block:
            @block.scalar
            def _(sc):
                for t in range(NT):
                    ins = nc.scalar.activation(xn[:, t, :], K.x[:, t, :], ACT.Square, accum_out=ss[:, t:t + 1])
                ins.then_inc(squared, 1)
                sc.wait_ge(var, 1)
                nc.scalar.activation(sd[:, :], ss[:, :], ACT.Sqrt).then_inc(root, 1)
                for k in range(0, KD, 2):
                    sc.wait_ge(turned, k + 1)
                    bias = shift[:, k:k + 1] if shift is not None else 0.0
                    nc.scalar.activation(dst[:, k, :], K.ps[:, k, :], ACT.Identity, scale=scale[:, k:k + 1], bias=bias)

            @block.vector
            def _(ve):
                ve.wait_ge(squared, 1)
                nc.vector.tensor_scalar(ss[:, :], ss[:, :], 1.0 / D, EPS, ALU.mult, ALU.add).then_inc(var, 1)
                ve.wait_ge(root, 1)
                K.dve_link(nc.vector.reciprocal(ss[:, :], sd[:, :]))
                for t in range(NT):
                    nc.vector.tensor_scalar(xn[:, t, :], K.x[:, t, :], ss[:, t:t + 1], None, ALU.mult)\
                        .then_inc(normed, 1)
                for k in range(1, KD, 2):
                    ve.wait_ge(turned, k + 1)
                    if shift is not None:
                        nc.vector.tensor_scalar(dst[:, k, :], K.ps[:, k, :], scale[:, k:k + 1], shift[:, k:k + 1],
                                                ALU.mult, ALU.add)
                    else:
                        nc.vector.tensor_scalar(dst[:, k, :], K.ps[:, k, :], scale[:, k:k + 1], None, ALU.mult)

            @block.tensor
            def _(pe):
                pe.wait_ge(normed, NT)
                for k in range(KD):
                    for t in range(NT):
                        ins = nc.tensor.transpose(K.ps[:, k, t * P:(t + 1) * P], xn[:, t, k * P:(k + 1) * P],
                                                  K.ident[:, :])
                    ins.then_inc(turned, 1)


def final_norm(K, name, gain, write_out):
    nc = K.nc
    squared, var, root, done = (K.sem(f"{name}_{s}") for s in ("squared", "var", "root", "done"))
    with ExitStack() as ctx:
        ss = K.sb(ctx, f"{name}_ss", [P, NT])
        sd = K.sb(ctx, f"{name}_sd", [P, NT])
        gb = K.sb(ctx, f"{name}_g", [P, D])
        junk = K.sb(ctx, f"{name}_junk", [P, D])
        with nc.Block() as block:
            @block.sync
            def _(sp):
                K.load(sp, gb[:, :], gain.rearrange("(a n) -> a n", a=1).partition_broadcast(P))
                if write_out:
                    for t in range(NT):
                        sp.wait_ge(done, t + 1)
                        K.store(sp, K.out[0, t * P:(t + 1) * P, :], K.x[:, t, :])
                    sp.wait_ge(K.stores, K.stores_n)

            @block.scalar
            def _(sc):
                for t in range(NT):
                    if t:
                        sc.wait_ge(squared, t)
                    nc.scalar.activation(junk[:, :], K.x[:, t, :], ACT.Square, accum_out=ss[:, t:t + 1])\
                        .then_inc(squared, 1)
                sc.wait_ge(var, 1)
                nc.scalar.activation(sd[:, :], ss[:, :], ACT.Sqrt).then_inc(root, 1)

            @block.vector
            def _(ve):
                ve.wait_ge(squared, NT)
                nc.vector.tensor_scalar(ss[:, :], ss[:, :], 1.0 / D, EPS, ALU.mult, ALU.add).then_inc(var, 1)
                ve.wait_ge(root, 1)
                ve.wait_ge(K.loads, K.loads_n)
                K.dve_link(nc.vector.reciprocal(ss[:, :], sd[:, :]))
                for t in range(NT):
                    nc.vector.scalar_tensor_tensor(K.x[:, t, :], K.x[:, t, :], ss[:, t:t + 1], gb[:, :],
                                                   ALU.mult, ALU.mult).then_inc(done, 1)


def add_residual(K, stage, src, per_unit, gate=None):
    nc = K.nc

    def dve(j, banks):
        x = K.x[:, :, j * 512:(j + 1) * 512]
        if gate is not None:
            g = gate[:, j * 512:(j + 1) * 512].unsqueeze(1).to_broadcast([P, NT, 512])
            K.dve_link(nc.vector.tensor_tensor(banks, banks, g, ALU.mult))
        return nc.vector.tensor_tensor(x, banks, x, ALU.add)

    linear_split(K, stage, "N", src, per_unit, dve=dve, paired=False)



RH, RDK, RDV = 4, 128, 256
AH, AG = 4, 3
RQ, RK_, RV, RG = 0, RH * RDK, 2 * RH * RDK, 2 * RH * RDK + RH * RDV
AQ = RG + RH * RDV
AK_ = AQ + AG * AH * P
AV = AK_ + AG * AH * P
GA = AV + AG * AH * P
GB = GA + D
T0W = 4 * P + 3
T12W = 2 * P


def plan_block1(st, A):
    w_ada, w_in = A["w_ada"][0], A["w_in"][0]
    for s in range(12):
        for c in range(2):
            st.add("mod1", rows(w_ada, 4 * c, 4, 512 * s))
    for h in range(RH):
        st.add("ret", columns(w_in, (RQ + h * RDK, RDK), (RK_ + h * RDK, RDK)))
        st.add("ret", columns(w_in, (RV + h * RDV, RDV)))
        st.add("ret", columns(w_in, (RG + h * RDV, RDV)))
    for i in range(4):
        st.add("gate_a", columns(w_in, (GA + 256 * i, 256)))
    for i in range(4):
        st.add("ret_o", columns(A["w_ret_o"][0], (256 * i, 256)))
    for h in range(AH):
        for g in range(AG):
            st.add("att", columns(w_in, (AQ + (g * AH + h) * P, P), (AK_ + (g * AH + h) * P, P)))
        st.add("att", columns(w_in, (AV + (AH + h) * P, P), (AV + (2 * AH + h) * P, P)))
        st.add("att", columns(w_in, (AV + h * P, P)))
    for i in range(4):
        st.add("gate_b", columns(w_in, (GB + 256 * i, 256)))
    for i in range(2):
        st.add("att_o", rows(A["w_att_o"][0], 0, 4, 512 * i))
    for j in range(2):
        for c in range(2):
            st.add("w_o", rows(A["w_o"][0], 4 * c, 4, 512 * j))
    for i in range(RING):
        st.add("moe", rows(A["w_mlp1"][0, 0], i % 2 * 4, 4, i // 2 * 512))
    st.further_loads(EXPERTS * 12 // RING - 1)


def retention(K, pair, retT):
    nc, A = K.nc, K.A
    first, _ = K.stream.span["ret"]
    raw_done, rot_done, turn_done = K.sem("ret_raw"), K.sem("ret_rot"), K.sem("ret_turned")
    sc_done, mask_done, y_done = K.sem("ret_scores"), K.sem("ret_masked"), K.sem("ret_y")
    var_done, sd_done, ret_done = K.sem("ret_var"), K.sem("ret_sd"), K.sem("ret_normed")
    tr_done, out_done, g_done = K.sem("ret_transposed"), K.sem("ret_copied"), K.sem("ret_gated")
    with ExitStack() as ctx:
        cos = K.sb(ctx, "rope_cos", [P, S])
        sin = K.sb(ctx, "rope_sin", [P, S])
        rot = K.sb(ctx, "rope_rot", [P, P])
        decay = K.sb(ctx, "decay", [P, RH, NT, P])
        raw, qk, t1 = K.hT[:, 0:2, :], K.hT[:, 2:4, :], K.hT[:, 4:6, :]
        y = K.hT[:, 6:8, :].rearrange("p a (t n) -> p (a t) n", n=RDV)
        W = SplitWeights(K, ctx, "ret")
        v = K.sb(ctx, "ret_v", [P, NT, RDV])
        sg = K.sb(ctx, "ret_sg", [P, NT, RDV])
        pt = K.sb(ctx, "ret_pt", [P, NT, S])
        stats = K.sb(ctx, "ret_stats", [P, NT, 6])
        mv = K.sb(ctx, "ret_mv", [P, NT, 2])
        sd = K.sb(ctx, "ret_sdv", [P, NT])
        ps = K.ps
        with nc.Block() as block:
            @block.sync
            def _(sp):
                for dst, key in ((cos, "k_cos"), (sin, "k_sin"), (rot, "k_rot")):
                    K.load(sp, dst[:, :], A[key])
                K.load(sp, decay[:, :, :, :], A["k_decay"])
                K.refill(sp, first, first + 3 * RH)

            @block.tensor
            def _(pe):
                pe.wait_ge(K.loads, K.loads_n)
                for h in range(RH):
                    n = first + 3 * h
                    if h:
                        pe.wait_ge(out_done, h)
                    W.tiles(pe, n, pair, ps[:, 0:2, :])
                    if h:
                        pe.wait_ge(ret_done, h)
                    for c in (1, 2):
                        for r0, nr, place in W.halves[n + c]:
                            w = W.ready(pe, n + c, place)
                            for t in range(NT):
                                out = ps[:, 2 + 2 * c + t // 2, (t % 2) * 256:(t % 2) * 256 + 256]
                                ins = W.rows(out, lambda a, k: pair[:, a, k, t * P:(t + 1) * P], w, r0, nr, t % 2 == 0, t % 2 == 1)
                            W.used(ins, place)
                    pe.wait_ge(raw_done, 2 * h + 1)
                    for i in range(2):
                        ins = nc.tensor.matmul(ps[:, 2 + i, :], rot[:, :], raw[:, i, :], start=True, stop=True)
                    ins.then_inc(turn_done, 1)
                    pe.wait_ge(rot_done, h + 1)
                    for j in range(NT):
                        ins = nc.tensor.matmul(ps[:, j, j * P:], qk[:, 1, j * P:(j + 1) * P], qk[:, 0, j * P:],
                                               start=True, stop=True)
                        ins.then_inc(sc_done, 1)
                    pe.wait_ge(raw_done, 2 * h + 2)
                    pe.wait_ge(mask_done, NT * (h + 1))
                    for i in range(NT):
                        for j in range(i + 1):
                            ins = nc.tensor.matmul(ps[:, 4 + i // 2, (i % 2) * 256:(i % 2) * 256 + 256],
                                                   pt[:, j, i * P:(i + 1) * P], v[:, j, :],
                                                   start=(j == 0), stop=(j == i))
                    ins.then_inc(y_done, 1)
                    pe.wait_ge(ret_done, h + 1)
                    for e in range(2):
                        for t in range(NT):
                            ins = nc.tensor.transpose(ps[:, e, t * P:(t + 1) * P], y[:, t, e * P:(e + 1) * P],
                                                      K.ident[:, :])
                    ins.then_inc(tr_done, 1)

            @block.gpsimd
            def _(po):
                W.pool(po)

            @block.scalar
            def _(sc):
                W.act_high(sc, first, 0)
                W.act_high(sc, first, 1)
                for h in range(RH):
                    W.act_high(sc, first + 3 * h + 1, 0)
                    W.act_high(sc, first + 3 * h + 1, 1)
                    sc.wait_ge(K.chunk_used, first + 3 * h + 1)
                    if h:
                        sc.wait_ge(rot_done, h)
                    nc.scalar.activation(raw[:, :, :], ps[:, 0:2, :], ACT.Copy).then_inc(raw_done, 1)
                    W.act_high(sc, first + 3 * h + 2, 0)
                    W.act_high(sc, first + 3 * h + 2, 1)
                    sc.wait_ge(K.chunk_used, first + 3 * h + 2)
                    if h:
                        sc.wait_ge(y_done, h)
                    nc.scalar.activation(v[:, :, :].rearrange("p t n -> p (t n)"),
                                         ps[:, 4:6, :].rearrange("p t n -> p (t n)"), ACT.Copy).then_inc(raw_done, 1)
                    sc.wait_ge(K.chunk_used, first + 3 * h + 3)
                    if h:
                        sc.wait_ge(ret_done, h)
                    nc.scalar.activation(sg[:, :, :].rearrange("p t n -> p (t n)"),
                                         ps[:, 6:8, :].rearrange("p t n -> p (t n)"), ACT.Sigmoid).then_inc(g_done, 1)
                    if h < RH - 1:
                        W.act_high(sc, first + 3 * h + 3, 0)
                        W.act_high(sc, first + 3 * h + 3, 1)
                    sc.wait_ge(var_done, h + 1)
                    nc.scalar.activation(sd[:, :], mv[:, :, 1], ACT.Sqrt).then_inc(sd_done, 1)
                    sc.wait_ge(tr_done, h + 1)
                    nc.scalar.activation(retT[:, 2 * h:2 * h + 2, :], ps[:, 0:2, :], ACT.Copy).then_inc(out_done, 1)

            @block.vector
            def _(ve):
                ve.wait_ge(K.loads, K.loads_n)
                for h in range(RH):
                    ve.wait_ge(raw_done, 2 * h + 1)
                    K.dve_link(nc.vector.tensor_tensor(t1[:, :, :], raw[:, :, :],
                                                       cos[:, :].unsqueeze(1).to_broadcast([P, 2, S]), ALU.mult))
                    ve.wait_ge(turn_done, h + 1)
                    if h:
                        ve.wait_ge(sc_done, NT * h)
                    K.dve_link(nc.vector.tensor_tensor(qk[:, :, :], ps[:, 2:4, :],
                                                       sin[:, :].unsqueeze(1).to_broadcast([P, 2, S]), ALU.mult))
                    nc.vector.tensor_tensor(qk[:, :, :], qk[:, :, :], t1[:, :, :], ALU.add).then_inc(rot_done, 1)
                    if h:
                        ve.wait_ge(y_done, h)
                    for j in range(NT):
                        ve.wait_ge(sc_done, NT * h + j + 1)
                        w = S - j * P
                        nc.vector.tensor_tensor(pt[:, j, j * P:], ps[:, j, j * P:],
                                                decay[:, h, :, :].rearrange("p a b -> p (a b)")[:, 0:w],
                                                ALU.mult).then_inc(mask_done, 1)
                    ve.wait_ge(g_done, h + 1)
                    K.dve_link(nc.vector.tensor_tensor(sg[:, :, :].rearrange("p t n -> p (t n)"),
                                                       sg[:, :, :].rearrange("p t n -> p (t n)"),
                                                       ps[:, 6:8, :].rearrange("p t n -> p (t n)"), ALU.mult))
                    ve.wait_ge(y_done, h + 1)
                    yp = ps[:, 4:6, :].rearrange("p t (a n) -> p (t a) n", n=RDV)
                    for t in range(NT):
                        K.dve_link(nc.vector.bn_stats(stats[:, t, :], yp[:, t, :]))
                        K.dve_link(nc.vector.bn_aggr(mv[:, t, :], stats[:, t, :]))
                    nc.vector.tensor_scalar(mv[:, :, 1], mv[:, :, 1], 1.0, GN_EPS, ALU.mult, ALU.add)\
                        .then_inc(var_done, 1)
                    ve.wait_ge(sd_done, h + 1)
                    K.dve_link(nc.vector.reciprocal(sd[:, :], sd[:, :]))
                    if h:
                        ve.wait_ge(tr_done, h)
                    for t in range(NT):
                        K.dve_link(nc.vector.tensor_scalar(y[:, t, :], yp[:, t, :], mv[:, t, 0:1], sd[:, t:t + 1],
                                                           ALU.subtract, ALU.mult))
                    nc.vector.tensor_tensor(y[:, :, :], y[:, :, :], sg[:, :, :], ALU.mult).then_inc(ret_done, 1)


def sigmoid_gate(K, stage, pair, dst):
    linear_split(K, stage, "T", pair, 1,
           act=lambda j, banks: K.nc.scalar.activation(dst[:, 2 * j:2 * j + 2, :], banks, ACT.Sigmoid))


def bias_tables(K, name, rel, hot_dram, jobs, heads):
    nc = K.nc
    row_done, ready, copied = K.sem(f"{name}_row"), K.sem(f"{name}_ready"), K.sem(f"{name}_copied")
    written, loads0 = [K.sem(f"{name}_written{i}") for i in range(2)], K.loads_n
    scratch = nc.dram_tensor(f"{name}_rows", (len(jobs), P * 1024), F32, kind="Internal").ap()
    with ExitStack() as ctx:
        rb = K.sb(ctx, f"{name}_rel", [33, heads])
        rbb = K.sb(ctx, f"{name}_relb", [33, heads, P])
        hot = K.sb(ctx, f"{name}_hot", [33, hot_dram.shape[1]])
        row = K.sb(ctx, f"{name}_rowb", [P, 2, 1024])
        with nc.Block() as block:
            @block.sync
            def _(sp):
                K.load(sp, rb[0:32, :], rel)
                K.load(sp, hot[:, :], hot_dram)
                for i, (_, _, w, _, _, _) in enumerate(jobs):
                    sp.wait_ge(copied, i + 1)
                    sp.dma_start(scratch[i, 0:P * w].rearrange("(p w) -> p w", w=w), row[:, i % 2, 0:w])\
                        .then_inc(written[i % 2], 16)
                for i, (_, _, w, step, base, table) in enumerate(jobs):
                    if i == 0:
                        for b in range(2):
                            sp.wait_ge(written[b], 16 * ((len(jobs) + 1 - b) // 2))
                    src = scratch[i, base:base + P * (w - step)].rearrange("(p w) -> p w", w=w - step)
                    K.load(sp, table, src[:, 0:table.shape[1]])
                sp.wait_ge(K.loads, K.loads_n)

            @block.vector
            def _(ve):
                nc.vector.memset(rb[32:33, :], NEG).then_inc(ready, 1)
                ve.wait_ge(ready, 1)
                ve.wait_ge(K.loads, loads0 + 32)
                nc.vector.tensor_copy(rbb[:, :, :], rb[:, :].unsqueeze(2).to_broadcast([33, heads, P]))\
                    .then_inc(ready, 1)
                for i, (_, _, w, _, _, _) in enumerate(jobs):
                    ve.wait_ge(row_done, i + 1)
                    if i >= 2:
                        ve.wait_ge(written[i % 2], 16 * (i // 2))
                    b = 2 * (i % 4)
                    nc.vector.tensor_copy(row[:, i % 2, 0:w],
                                          K.ps[:, b:b + 2, :].rearrange("p a n -> p (a n)")[:, 0:w]).then_inc(copied, 1)

            @block.tensor
            def _(pe):
                pe.wait_ge(ready, 2)
                for i, (head, q0, w, _, _, _) in enumerate(jobs):
                    if i >= 4:
                        pe.wait_ge(copied, i - 3)
                    for c in range(0, w, 512):
                        n = min(512, w - c)
                        ins = nc.tensor.matmul(K.ps[:, 2 * (i % 4) + c // 512, 0:n], rbb[:, head, :],
                                               hot[:, q0 + c:q0 + c + n], start=True, stop=True)
                    ins.then_inc(row_done, 1)


def dilated(K, pair, attT, T0, T12):
    nc = K.nc
    first, _ = K.stream.span["att"]
    names = "proj scores softmax transposed pT av norm oT copied summed maxed".split()
    proj, scores, softmax, transposed, p_ready, av, norm, o_turned, copied, biased, maxed = (
        K.sem(f"att_{n}") for n in names)
    scale = float(P) ** -0.5
    ps = K.ps
    with ExitStack() as ctx:
        qk = K.hT[:, 0:6, :]
        W = SplitWeights(K, ctx, "att")
        v = K.sb(ctx, "att_v", [P, AG, NT, P])
        s = K.sb(ctx, "att_s", [P, 2, 6 * P])
        pT = K.sb(ctx, "att_pT", [P, 6 * P])
        o = K.sb(ctx, "att_o_tok", [P, P])
        nm = K.sb(ctx, "att_negmax", [P, 2])
        l = K.sb(ctx, "att_sum", [P, 2])
        with nc.Block() as block:
            @block.sync
            def _(sp):
                K.refill(sp, first, first + 5 * AH)

            @block.tensor
            def _(pe):
                def score(u):
                    c = u % 4
                    if u >= 2:
                        pe.wait_ge(biased, 2 * (u - 1))
                    b = 2 * (u % 2)
                    nc.tensor.matmul(ps[:, b, :], qk[:, 0, c::4], qk[:, 1, :], start=True, stop=True)
                    nc.tensor.matmul(ps[:, b + 1, 0:P], qk[:, 2, c::4], qk[:, 3, c::4], start=True, stop=True)
                    nc.tensor.matmul(ps[:, b + 1, P:2 * P], qk[:, 4, c::4], qk[:, 5, c::4], start=True, stop=True)\
                        .then_inc(scores, 1)

                def turn_output(u):
                    pe.wait_ge(norm, u + 1)
                    if u:
                        pe.wait_ge(copied, u)
                    nc.tensor.transpose(ps[:, 7, 0:P], o[:, :], K.ident[:, :]).then_inc(o_turned, 1)

                for h in range(AH):
                    n = first + 5 * h
                    if h:
                        pe.wait_ge(copied, 4 * h)
                    for g in range(AG):
                        W.tiles(pe, n + g, pair, ps[:, 2 * g:2 * g + 2, :])
                    for r0, nr, place in W.halves[n + 3]:
                        w = W.ready(pe, n + 3, place)
                        for t in range(NT):
                            out = ps[:, 6 + t // 2, (t % 2) * 256:(t % 2) * 256 + 256]
                            ins = W.rows(out, lambda a, k: pair[:, a, k, t::4], w, r0, nr, t % 2 == 0, t % 2 == 1)
                        W.used(ins, place)
                    pe.wait_ge(proj, 5 * h + 1)
                    for r0, nr, place in W.halves[n + 4]:
                        w = W.ready(pe, n + 4, place)
                        for t in range(NT):
                            ins = W.rows(ps[:, 0, t * P:(t + 1) * P], lambda a, k: pair[:, a, k, t * P:(t + 1) * P],
                                         w, r0, nr, t == 0, t == NT - 1)
                        W.used(ins, place)
                    pe.wait_ge(proj, 5 * h + 5)
                    score(4 * h)
                    score(4 * h + 1)
                    for c in range(4):
                        u = 4 * h + c
                        pe.wait_ge(softmax, u + 1)
                        for j in range(6):
                            ins = nc.tensor.transpose(ps[:, 4 + j // 4, (j % 4) * P:(j % 4 + 1) * P],
                                                      s[:, u % 2, j * P:(j + 1) * P], K.ident[:, :])
                        ins.then_inc(transposed, 1)
                        if c < 2:
                            score(u + 2)
                        if c:
                            turn_output(u - 1)
                        pe.wait_ge(p_ready, u + 1)
                        for j in range(6):
                            rhs = v[:, 0, j, :] if j < 4 else v[:, j - 3, c, :]
                            ins = nc.tensor.matmul(ps[:, 6, 0:P], pT[:, j * P:(j + 1) * P], rhs, start=(j == 0),
                                                   stop=(j == 5))
                        ins.then_inc(av, 1)
                    turn_output(4 * h + 3)

            @block.gpsimd
            def _(po):
                W.pool(po)

            @block.scalar
            def _(sc):
                def highs(n):
                    for _, _, place in W.halves[n]:
                        W.act_high(sc, n, place)

                def take_output(u):
                    sc.wait_ge(o_turned, u + 1)
                    nc.scalar.activation(attT[:, u // 4, u % 4::4], ps[:, 7, 0:P], ACT.Copy).then_inc(copied, 1)

                highs(first)
                for h in range(AH):
                    n = first + 5 * h
                    for g in range(AG):
                        highs(n + g + 1)
                        sc.wait_ge(K.chunk_used, n + g + 1)
                        if h:
                            sc.wait_ge(scores, 4 * h)
                        nc.scalar.activation(qk[:, 2 * g:2 * g + 2, :], ps[:, 2 * g:2 * g + 2, :], ACT.Copy)\
                            .then_inc(proj, 1)
                    highs(n + 4)
                    sc.wait_ge(K.chunk_used, n + 4)
                    nc.scalar.activation(v[:, 1:3, :, :],
                                         ps[:, 6:8, :].rearrange("p a (b g n) -> p g (a b) n", g=2, n=P), ACT.Copy)\
                        .then_inc(proj, 1)
                    sc.wait_ge(K.chunk_used, n + 5)
                    nc.scalar.activation(v[:, 0, :, :].rearrange("p b c -> p (b c)"), ps[:, 0, :], ACT.Copy)\
                        .then_inc(proj, 1)
                    if h < AH - 1:
                        highs(n + 5)
                    for c in range(4):
                        u = 4 * h + c
                        sc.wait_ge(maxed, u + 1)
                        nc.scalar.activation(s[:, u % 2, :], s[:, u % 2, :], ACT.Exp, bias=nm[:, u % 2:u % 2 + 1],
                                             scale=1.0, accum_out=l[:, u % 2:u % 2 + 1]).then_inc(softmax, 1)
                        sc.wait_ge(transposed, u + 1)
                        if u:
                            sc.wait_ge(av, u)
                        nc.scalar.activation(pT[:, :], ps[:, 4:6, :].rearrange("p a n -> p (a n)")[:, 0:6 * P],
                                             ACT.Copy).then_inc(p_ready, 1)
                        if c:
                            take_output(u - 1)
                    take_output(4 * h + 3)

            @block.vector
            def _(ve):
                def soften(u):
                    h, c, b = u // 4, u % 4, 2 * (u % 2)
                    ve.wait_ge(scores, u + 1)
                    if u >= 2:
                        ve.wait_ge(transposed, u - 1)
                    nc.vector.scalar_tensor_tensor(s[:, u % 2, 0:S], ps[:, b, :], scale, T0[:, h, 3 - c:3 - c + S],
                                                   ALU.mult, ALU.add).then_inc(biased, 1)
                    nc.vector.scalar_tensor_tensor(s[:, u % 2, S:], ps[:, b + 1, 0:2 * P], scale, T12[:, h, :],
                                                   ALU.mult, ALU.add).then_inc(biased, 1)
                    ve.wait_ge(biased, 2 * (u + 1))
                    K.dve_link(nc.vector.tensor_reduce(nm[:, u % 2:u % 2 + 1], s[:, u % 2, :], AX, ALU.max))
                    nc.vector.tensor_scalar(nm[:, u % 2:u % 2 + 1], nm[:, u % 2:u % 2 + 1], -1.0, None, ALU.mult)\
                        .then_inc(maxed, 1)

                for h in range(AH):
                    soften(4 * h)
                    soften(4 * h + 1)
                    for c in range(4):
                        u = 4 * h + c
                        if c < 2:
                            soften(u + 2)
                        ve.wait_ge(softmax, u + 1)
                        K.dve_link(nc.vector.reciprocal(l[:, u % 2:u % 2 + 1], l[:, u % 2:u % 2 + 1]))
                        ve.wait_ge(av, u + 1)
                        if u:
                            ve.wait_ge(o_turned, u)
                        nc.vector.tensor_scalar(o[:, :], ps[:, 6, 0:P], l[:, u % 2:u % 2 + 1], None, ALU.mult)\
                            .then_inc(norm, 1)


def route(K, wr, br, posm, gate, extra):
    nc = K.nc
    A = K.A
    logit_done, masked, placed = K.sem("rt_logits"), K.sem("rt_masked"), K.sem("rt_placed")
    exp_in, exp_out, loads0, counted = K.sem("rt_expin"), K.sem("rt_expout"), K.loads_n, K.sem("rt_counted")
    E = EXPERTS
    with ExitStack() as ctx:
        w = K.sb(ctx, "rt_w", [P, KD, E])
        b = K.sb(ctx, "rt_b", [P, E])
        tri = K.sb(ctx, "rt_tri", [P, P])
        lg = K.sb(ctx, "rt_lg", [P, NT, E])
        m8 = K.sb(ctx, "rt_m8", [P, NT, 8])
        same = K.sb(ctx, "rt_same", [P, NT, E])
        mask = K.sb(ctx, "rt_mask", [P, NT, E])
        ssum = K.sb(ctx, "rt_sum", [P, NT])
        cnt = K.sb(ctx, "rt_cnt", [P, E])
        spans = S // CAP - 1
        held = K.sb(ctx, "rt_held", [P, E * spans])
        rank = K.sb(ctx, "rt_rank", [P, E * spans])
        code = K.sb(ctx, "rt_code", [P, 2, E * spans])
        number = K.sb(ctx, "rt_number", [P, SPILLS])
        hit = K.sb(ctx, "rt_hit", [P, SPILLS, E * spans])
        lst = K.sb(ctx, "rt_list", [P, SPILLS, E * spans])
        found = K.sb(ctx, "rt_found", [P, 2, SPILLS])
        with nc.Block() as block:
            @block.sync
            def _(sp):
                K.load(sp, w[:, :, :], wr.rearrange("(k p) e -> p k e", p=P))
                K.load(sp, b[:, :], br.rearrange("(a e) -> a e", a=1).partition_broadcast(P))
                K.load(sp, tri[:, :], A["k_before"])
                K.load(sp, code[:, :, :], A["k_spans"])
                K.load(sp, number[:, :], A["k_iota"][:, 0:SPILLS])

            @block.tensor
            def _(pe):
                pe.wait_ge(K.loads, loads0 + 80)
                for t in range(NT):
                    for k in range(KD):
                        ins = nc.tensor.matmul(K.ps[:, 0, t * E:(t + 1) * E], K.hT[:, k, t * P:(t + 1) * P],
                                               w[:, k, :], start=(k == 0), stop=(k == KD - 1))
                ins.then_inc(logit_done, 1)
                pe.wait_ge(masked, 1)
                for t in range(NT):
                    for j in range(t + 1):
                        ins = nc.tensor.matmul(K.ps[:, 1, t * E:(t + 1) * E], K.ones[:, :] if j < t else tri[:, :],
                                               mask[:, j, :], start=(j == 0), stop=(j == t))
                for j in range(NT):
                    ins = nc.tensor.matmul(K.ps[:, 2, 0:E], K.ones[:, :], mask[:, j, :], start=(j == 0),
                                           stop=(j == NT - 1))
                ins.then_inc(placed, 1)

            @block.scalar
            def _(sc):
                sc.wait_ge(exp_in, 1)
                nc.scalar.activation(gate[:, :, 0:E], lg[:, :, :], ACT.Exp).then_inc(exp_out, 1)

            @block.vector
            def _(ve):
                ve.wait_ge(K.loads, loads0 + 80)
                ve.wait_ge(logit_done, 1)
                K.dve_link(nc.vector.tensor_tensor(lg[:, :, :], K.ps[:, 0, 0:NT * E].rearrange("p (t e) -> p t e", e=E),
                                                   b[:, :].unsqueeze(1).to_broadcast([P, NT, E]), ALU.add))
                for t in range(NT):
                    nc.vector.max(m8[:, t, :], lg[:, t, :]).then_inc(counted, 1)
                ve.wait_ge(counted, NT)
                fourth = m8[:, :, 3:4].to_broadcast([P, NT, E])
                K.dve_link(nc.vector.tensor_tensor(mask[:, :, :], lg[:, :, :], fourth, ALU.is_gt))
                K.dve_link(nc.vector.tensor_tensor(same[:, :, :], lg[:, :, :], fourth, ALU.is_equal))
                K.dve_link(nc.vector.tensor_reduce(ssum[:, :], mask[:, :, :], AX, ALU.add))
                for t in range(NT):
                    K.dve_link(nc.vector.tensor_tensor_scan(cnt[:, :], K.ones[:, 0:E], same[:, t, :],
                                                            ssum[:, t:t + 1], ALU.mult, ALU.add))
                    K.dve_link(nc.vector.scalar_tensor_tensor(cnt[:, :], cnt[:, :], float(TOPK), same[:, t, :],
                                                              ALU.is_le, ALU.mult))
                    K.dve_link(nc.vector.tensor_tensor(mask[:, t, :], mask[:, t, :], cnt[:, :], ALU.add))
                nc.vector.tensor_tensor(lg[:, :, :], lg[:, :, :], m8[:, :, 0:1].to_broadcast([P, NT, E]),
                                        ALU.subtract).then_inc(masked, 1)
                ve.wait_ge(masked, 1)
                nc.vector.tensor_copy(same[:, :, :], mask[:, :, :]).then_inc(exp_in, 1)
                nc.vector.memset(gate[:, :, E:], 0.0)
                ve.wait_ge(exp_out, 1)
                g = gate[:, :, 0:E]
                K.dve_link(nc.vector.tensor_tensor(g, g, mask[:, :, :], ALU.mult))
                K.dve_link(nc.vector.tensor_reduce(ssum[:, :], g, AX, ALU.add))
                K.dve_link(nc.vector.reciprocal(ssum[:, :], ssum[:, :]))
                nc.vector.tensor_tensor(g, g, ssum[:, :].unsqueeze(2).to_broadcast([P, NT, E]), ALU.mult)
                ve.wait_ge(placed, 1)
                K.dve_link(nc.vector.memset(posm[:, :, E:], -1.0))
                K.dve_link(nc.vector.scalar_tensor_tensor(posm[:, :, 0:E],
                                                          K.ps[:, 1, 0:NT * E].rearrange("p (t e) -> p t e", e=E),
                                                          1.0, mask[:, :, :], ALU.add, ALU.mult))
                K.dve_link(nc.vector.tensor_scalar(posm[:, :, 0:E], posm[:, :, 0:E], 1.0, None, ALU.subtract))
                extra_n, extra_e, extra_at = extra
                for far in range(spans):
                    h = held[:, :].rearrange("p (e b) -> p e b", b=spans)[:, :, far]
                    K.dve_link(nc.vector.tensor_scalar(h, K.ps[:, 2, 0:E], float(CAP * (far + 1)), None, ALU.is_gt))
                K.dve_link(nc.vector.tensor_tensor_scan(rank[:, :], K.ones[:, 0:E * spans], held[:, :], -1.0,
                                                        ALU.mult, ALU.add))
                K.dve_link(nc.vector.tensor_tensor(hit[:, :, :], number[:, :].unsqueeze(2).to_broadcast(
                    [P, SPILLS, E * spans]), rank[:, :].unsqueeze(1).to_broadcast([P, SPILLS, E * spans]), ALU.is_equal))
                K.dve_link(nc.vector.tensor_tensor(hit[:, :, :], hit[:, :, :], held[:, :].unsqueeze(1).to_broadcast(
                    [P, SPILLS, E * spans]), ALU.mult))
                for i in range(2):
                    K.dve_link(nc.vector.tensor_tensor(lst[:, :, :], hit[:, :, :], code[:, i, :].unsqueeze(1)
                                                       .to_broadcast([P, SPILLS, E * spans]), ALU.mult))
                    K.dve_link(nc.vector.tensor_reduce(found[:, i, :], lst[:, :, :], AX, ALU.add))
                K.dve_link(nc.vector.tensor_copy(extra_e[:, :], found[:, 0, :]))
                K.dve_link(nc.vector.tensor_copy(extra_at[:, :], found[:, 1, :]))
                K.dve_link(nc.vector.tensor_scalar(extra_n[:, :], rank[:, E * spans - 1:], 1.0, None, ALU.add))


HALVES = 6
PER = 2 * 12


class Experts:

    def __init__(self, K, name, bufs, iota, added0=0):
        self.K, self.nc, self.used, self.added0 = K, K.nc, K.sem(f"{name}_used"), added0
        self.B, self.iota = bufs, iota
        self.picked, self.gathered, self.xe_ready = (K.sem(f"{name}_{n}") for n in ("picked", "gathered", "xe"))
        self.high, self.low_dve, self.low_pool = (K.sem(f"{name}_{n}") for n in ("high", "low_dve", "low_pool"))
        self.pick_turned, self.scatter_ready = K.sem(f"{name}_pick_turned"), K.sem(f"{name}_scatter_ready")
        self.clamped, self.sig_done, self.act_done = (K.sem(f"{name}_{n}") for n in ("clamped", "sig", "act"))
        self.a_turned, self.aT_high, self.aT_ready = (K.sem(f"{name}_{n}") for n in ("a_turned", "aT_high", "aT"))
        self.ye_high, self.ye_ready = K.sem(f"{name}_ye_high"), K.sem(f"{name}_ye")
        self.scattered, self.added = K.sem(f"{name}_scattered"), K.sem(f"{name}_added")

    def act_high(self, sc, u, j, fresh=False):
        self.B["wait_raw"](sc, u, j)
        if j >= HALVES or not fresh:
            sc.wait_ge(self.used, u * PER + (j - HALVES + 1))
        self.nc.scalar.activation(self.B["high"][:, j % HALVES, :], self.B["raw"](j), ACT.Copy).then_inc(self.high, 1)

    def make_low(self, eng, sem, u, j):
        eng.wait_ge(self.high, u * PER + (j + 1))
        eng.tensor_tensor(self.B["low"][:, j % HALVES, :], self.B["raw"](j),
                          self.B["high"][:, j % HALVES, :].bitcast(F32), ALU.subtract).then_inc(sem, 1)

    def wait_low(self, eng, u, j):
        if j % 6 in (4, 5):
            eng.wait_ge(self.low_pool, u * (PER // 3) + (j // 6 * 2 + j % 6 - 3))
        else:
            eng.wait_ge(self.low_dve, u * (PER // 3 * 2) + (j // 6 * 4 + j % 6 + 1))

    def dve_low(self, ve, u, j):
        if j % 6 < 4:
            self.make_low(ve, self.low_dve, u, j)

    def split(self, part, eng, u, js, ahead):
        for j in js:
            if j < PER:
                part(eng, u, j)
            elif ahead:
                part(eng, u + 1, j - PER)

    def dve_pick(self, ve, e, par):
        nc, B = self.nc, self.B
        nc.vector.tensor_copy(B["esel"][:, par, :], self.K.ident[0:EXPERTS, bass.ds(e, 1)].to_broadcast([EXPERTS, CAP]))
        nc.vector.tensor_copy(B["gcol"][:, par, :], B["gate"][:, :, bass.ds(e, 1)].rearrange("p t a -> p (t a)"))
        nc.vector.tensor_tensor(B["pick"][:, par, :, :], self.iota.unsqueeze(1).to_broadcast([P, NT, CAP]),
                                B["posm"][:, :, bass.ds(e, 1)].to_broadcast([P, NT, CAP]), ALU.is_equal)\
            .then_inc(self.picked, 1)

    def dve_add(self, ve, u, par, i):
        m, t = i // NT, i % NT
        ve.wait_ge(self.scattered, u * 8 + (i + 1))
        acc = self.B["acc"][:, t, m * 512:(m + 1) * 512]
        self.nc.vector.scalar_tensor_tensor(acc, self.K.ps[:, 6 + i % 2, :], self.B["gcol"][:, par, t:t + 1], acc,
                                            ALU.mult, ALU.add).then_inc(self.added, 1)

    def dve_expert(self, ve, u, e_next, par, fresh, ahead=True):
        nc, B = self.nc, self.B

        def low_of_turned(c):
            ve.wait_ge(self.aT_high, u * 4 + (c + 1))
            out = B["aT"][:, :, 2 * c:2 * c + 2, :]
            nc.vector.tensor_tensor(out[:, 1, :, :].rearrange("p a b -> p (a b)"), self.K.ps[:, 3, 0:256],
                                    out[:, 0, :, :].rearrange("p a b -> p (a b)").bitcast(F32), ALU.subtract)\
                .then_inc(self.aT_ready, 1)

        for c in range(4):
            if c == 0 and not fresh:
                for i in (4, 5):
                    self.dve_add(ve, u - 1, 1 - par, i)
            self.split(self.dve_low, ve, u, range(4 * c + 6, 4 * c + 9), ahead)
            up = self.K.ps[:, c % 2, :].rearrange("p (n two) -> p n two", two=2)
            glu, lin = B["glu"][:, c % 2, :], B["lin"][:, c % 2, :]
            ve.wait_ge(self.used, u * PER + (4 * c + 4))
            nc.vector.tensor_scalar(glu, up[:, :, 0], 7.0, None, ALU.min)
            nc.vector.tensor_scalar(lin, up[:, :, 1], 7.0, -7.0, ALU.min, ALU.max).then_inc(self.clamped, 1)
            ve.wait_ge(self.clamped, u * 8 + (2 * c + 1))
            nc.vector.scalar_tensor_tensor(lin, lin, 1.0, glu, ALU.add, ALU.mult).then_inc(self.clamped, 1)
            ve.wait_ge(self.clamped, u * 8 + (2 * c + 2))
            ve.wait_ge(self.sig_done, u * 4 + (c + 1))
            if c > 1 or not fresh:
                ve.wait_ge(self.a_turned, u * 4 + max(c - 1, 0))
            nc.vector.tensor_tensor(B["a"][:, c % 2, :], lin, B["sig"][:, c % 2, :], ALU.mult).then_inc(self.act_done, 1)
            if c:
                low_of_turned(c - 1)
            else:
                if not fresh:
                    for i in (6, 7):
                        self.dve_add(ve, u - 1, 1 - par, i)
                if ahead:
                    if not fresh:
                        ve.wait_ge(self.added, u * 8)
                    self.dve_pick(ve, e_next, 1 - par)
            self.split(self.dve_low, ve, u, (4 * c + 9,), ahead)
        low_of_turned(3)
        for m in range(2):
            self.split(self.dve_low, ve, u, range(4 * m + 22, 4 * m + 25), ahead)
            ve.wait_ge(self.ye_high, u * 2 + (m + 1))
            nc.vector.tensor_tensor(B["ye"][:, m, 1, :], self.K.ps[:, m, :], B["ye"][:, m, 0, :].bitcast(F32),
                                    ALU.subtract).then_inc(self.ye_ready, 1)
            if m:
                for i in (2, 3):
                    self.dve_add(ve, u, par, i)
            self.split(self.dve_low, ve, u, (4 * m + 25,), ahead)
            if not m:
                for i in (0, 1):
                    self.dve_add(ve, u, par, i)
        if not ahead:
            for i in range(4, 8):
                self.dve_add(ve, u, par, i)

    def pool_expert(self, po, u):
        for j in range(PER):
            if j % 6 >= 4:
                self.make_low(po, self.low_pool, u, j)

    def act_xe(self, sc, u, part):
        sc.wait_ge(self.gathered, u * 2 + (part + 1))
        self.nc.scalar.activation(self.B["xe"][:, part, :, :].rearrange("p k n -> p (k n)"),
                                  self.K.ps[:, 4:6, :].rearrange("p a n -> p (a n)"), ACT.Copy)\
            .then_inc(self.xe_ready, 1)

    def act_expert(self, sc, u, fresh, ahead=True):
        nc, B = self.nc, self.B

        def turn(c):
            sc.wait_ge(self.a_turned, u * 4 + (c + 1))
            nc.scalar.activation(B["aT"][:, 0, 2 * c:2 * c + 2, :].rearrange("p a b -> p (a b)"),
                                 self.K.ps[:, 3, 0:256], ACT.Copy).then_inc(self.aT_high, 1)

        for c in range(4):
            self.split(self.act_high, sc, u, range(4 * c + 6, 4 * c + 9), ahead)
            if c == 3 and ahead:
                sc.wait_ge(self.used, u * PER + 16)
                self.act_xe(sc, u + 1, 0)
            sc.wait_ge(self.clamped, u * 8 + (2 * c + 1))
            if c > 1 or not fresh:
                sc.wait_ge(self.act_done, u * 4 + max(c - 1, 0))
            nc.scalar.activation(B["sig"][:, c % 2, :], B["glu"][:, c % 2, :], ACT.Sigmoid, scale=1.702)\
                .then_inc(self.sig_done, 1)
            if c:
                turn(c - 1)
            self.split(self.act_high, sc, u, (4 * c + 9,), ahead)
        sc.wait_ge(self.pick_turned, u + 1)
        nc.scalar.activation(B["scat"][:, :], self.K.ps[:, 2, :], ACT.Copy).then_inc(self.scatter_ready, 1)
        turn(3)
        if ahead:
            self.act_xe(sc, u + 1, 1)
        for m in range(2):
            self.split(self.act_high, sc, u, range(4 * m + 22, 4 * m + 25), ahead)
            sc.wait_ge(self.used, u * PER + (16 + 4 * m + 4))
            nc.scalar.activation(B["ye"][:, m, 0, :], self.K.ps[:, m, :], ACT.Copy).then_inc(self.ye_high, 1)
            self.split(self.act_high, sc, u, (4 * m + 25,), ahead)

    def pe_gather(self, pe, u, par, part, ks=range(KD)):
        if part == 0:
            pe.wait_ge(self.picked, u + 1)
        else:
            pe.wait_ge(self.xe_ready, u * 2 + 1)
        for k in ks:
            for t in range(NT):
                ins = self.nc.tensor.matmul(self.K.ps[:, 4 + k // 4, (k % 4) * CAP:(k % 4 + 1) * CAP],
                                            self.B["h"][:, part, t, k * P:(k + 1) * P], self.B["pick"][:, par, t, :],
                                            start=(t == 0), stop=(t == NT - 1))
        if KD - 1 in ks:
            ins.then_inc(self.gathered, 1)

    def pe_scatter(self, pe, u, tiles, fresh):
        B = self.B
        for i in tiles:
            m, t = i // NT, i % NT
            if t == 0:
                pe.wait_ge(self.ye_ready, u * 2 + (m + 1))
            if i > 1 or not fresh:
                pe.wait_ge(self.added, u * 8 + (self.added0 + i - 1))
            for part in range(2):
                ins = self.nc.tensor.matmul(self.K.ps[:, 6 + i % 2, :], B["scat"][:, t * P:(t + 1) * P],
                                            B["ye"][:, m, part, :], start=(part == 0), stop=(part == 1))
            ins.then_inc(self.scattered, 1)

    def pe_expert(self, pe, u, par, fresh, ahead=True):
        nc, ps, B = self.nc, self.K.ps, self.B

        def turn(c):
            pe.wait_ge(self.act_done, u * 4 + (c + 1))
            if c or not fresh:
                pe.wait_ge(self.aT_ready, u * 4 + c)
            for i in range(2):
                ins = nc.tensor.transpose(ps[:, 3, i * P:(i + 1) * P], B["a"][:, c % 2, i * P:(i + 1) * P],
                                          self.K.ident[:, :])
            ins.then_inc(self.a_turned, 1)

        def product(out, lhs, j, started):
            pe.wait_ge(self.high, u * PER + (j + 1))
            high, low = (B[n][:, j % HALVES, :].rearrange("p (k n) -> p k n", n=512) for n in ("high", "low"))
            k0 = 2 * (j % 4)
            for part in range(2):
                for k in range(2):
                    nc.tensor.matmul(out, lhs[:, part, k0 + k, :], high[:, k, :],
                                     start=(k0 + k + part == 0 and not started), stop=False)
            self.wait_low(pe, u, j)
            for k in range(2):
                ins = nc.tensor.matmul(out, lhs[:, 0, k0 + k, :], low[:, k, :], start=False, stop=(k0 + k == KD - 1))
            ins.then_inc(self.used, 1)

        pe.wait_ge(self.xe_ready, u * 2 + 2)
        for c in range(4):
            if c < 2 and not fresh:
                pe.wait_ge(self.ye_ready, u * 2 - 1 + c)
            elif c > 1:
                pe.wait_ge(self.clamped, u * 8 + 2 * (c - 2) + 1)
            nc.tensor.matmul(ps[:, c % 2, :], B["esel"][:, par, :], B["b1"][:, c * 512:(c + 1) * 512], start=True,
                             stop=False)
            for i in range(4):
                product(ps[:, c % 2, :], B["xe"], 4 * c + i, True)
                if c == 0 and i % 2 and not fresh:
                    self.pe_scatter(pe, u - 1, (3 + i, 4 + i), False)
            if c:
                turn(c - 1)
            if c == 1 and ahead:
                self.pe_gather(pe, u + 1, 1 - par, 0)
        if not fresh:
            pe.wait_ge(self.scatter_ready, u)
        for t in range(NT):
            ins = nc.tensor.transpose(ps[:, 2, t * P:(t + 1) * P], B["pick"][:, par, t, :].bitcast(F32),
                                      self.K.ident[:, :])
        ins.then_inc(self.pick_turned, 1)
        if ahead:
            self.pe_gather(pe, u + 1, 1 - par, 1, range(4))
        turn(3)
        if ahead:
            self.pe_gather(pe, u + 1, 1 - par, 1, range(4, KD))
        pe.wait_ge(self.aT_ready, u * 4 + 4)
        for j in range(16, 20):
            product(ps[:, 0, :], B["aT"], j, False)
        pe.wait_ge(self.scatter_ready, u + 1)
        for j in range(20, 24):
            product(ps[:, 1, :], B["aT"], j, False)
            if j % 2:
                self.pe_scatter(pe, u, (j - 21, j - 20), fresh)
        if not ahead:
            self.pe_scatter(pe, u, (4, 5, 6, 7), fresh)


def expert_source(A, e, j):
    w = A["w_mlp1"] if j < 8 else A["w_mlp2"]
    col, k0 = ((j % 8) // 2) * 512, (j % 2) * 4
    return w[0, bass.ds(e, 1), k0 * P:(k0 + 4) * P, col:col + 512].rearrange("e (k p) n -> p (e k) n", p=P)


def token_halves(K, h):
    nc = K.nc
    turned, highs = K.sem("th_turned"), K.sem("th_high")
    two = lambda t: K.ps[:, 2 * t:2 * t + 2, :].rearrange("p a n -> p (a n)")
    with nc.Block() as block:
        @block.tensor
        def _(pe):
            for t in range(NT):
                for k in range(KD):
                    ins = nc.tensor.transpose(K.ps[:, 2 * t + k // 4, (k % 4) * P:(k % 4 + 1) * P],
                                              K.hT[:, k, t * P:(t + 1) * P], K.ident[:, :])
                ins.then_inc(turned, 1)

        @block.scalar
        def _(sc):
            for t in range(NT):
                sc.wait_ge(turned, t + 1)
                nc.scalar.activation(h[:, 0, t, :], two(t), ACT.Copy).then_inc(highs, 1)

        @block.vector
        def _(ve):
            for t in range(NT):
                ve.wait_ge(highs, t + 1)
                nc.vector.tensor_tensor(h[:, 1, t, :], two(t), h[:, 0, t, :].bitcast(F32), ALU.subtract)


def mixture(K, posm, gate, extra):
    nc, A, ring = K.nc, K.A, K.stream
    first, last = ring.span["moe"]
    extra_n, extra_e, extra_at = extra
    PAIRS = EXPERTS // 2
    LOADS = 16 * 12 // RING
    assert last - first == RING and 12 % RING == 0 and PER % HALVES == 0 and PER % 6 == 0
    loads0 = K.loads_n
    saved = K.x_saved = nc.dram_tensor("x_saved", (P, NT * D), F32, kind="Internal").ap()
    acc = K.x
    flat_x = K.x[:, :, :].rearrange("p t d -> p (t d)")
    with ExitStack() as ctx:
        h = K.sb(ctx, "moe_h", [P, 2, NT, D], F32R)
        token_halves(K, h)
        iota = K.sb(ctx, "moe_iota", [P, CAP])
        places = K.sb(ctx, "spill_places", [P, CAP])
        lane = lambda i: K.hT[:, i, :].rearrange("p (b n) -> p b n", b=2)
        B = {"h": h, "posm": posm, "gate": gate, "acc": acc,
             "b1": K.hT[0:EXPERTS, 0:4, :].rearrange("p a n -> p (a n)"),
             "sig": lane(4), "glu": lane(5), "lin": lane(6), "a": lane(7),
             "pick": K.sb(ctx, "moe_pick", [P, 2, NT, CAP], F32R), "esel": K.sb(ctx, "moe_esel", [EXPERTS, 2, CAP]),
             "gcol": K.sb(ctx, "moe_gcol", [P, 2, NT]), "xe": K.sb(ctx, "moe_xe", [P, 2, KD, CAP], F32R),
             "aT": K.sb(ctx, "moe_aT", [P, 2, KD, CAP], F32R), "ye": K.sb(ctx, "moe_ye", [P, 2, 2, 512], F32R),
             "scat": K.sb(ctx, "moe_scat", [P, NT * P], F32R), "high": K.sb(ctx, "moe_high", [P, HALVES, HALF], F32R),
             "low": K.sb(ctx, "moe_low", [P, HALVES, HALF], F32R)}

        slot = lambda chunk: (first + chunk) % RING
        half = lambda ring_slot, j: K.ring[:, ring_slot, (j % 2) * HALF:(j % 2 + 1) * HALF]
        B["raw"] = lambda j: half(slot(j // 2), j)
        B["wait_raw"] = lambda eng, u, j: eng.wait_ge(
            K.landed[slot(j // 2)], u * LOADS + (ring.landed_at[first + j // 2 % RING] + 16 * (j // 2 // RING)))
        X = Experts(K, "moe", B, iota[:, :])
        landed, shifted = [K.sem(f"spill_landed{i}") for i in range(RING)], K.sem("spill_iota")
        C = dict(B)
        C["raw"] = lambda j: half(j // 2 % RING, j)
        C["wait_raw"] = lambda eng, u, j: eng.wait_ge(landed[j // 2 % RING], u * LOADS + 16 * (j // 2 // RING + 1))
        Y = Experts(K, "spill", C, places[:, :], added0=1)
        ready, kept = K.sem("moe_ready"), K.sem("x_kept")
        with nc.Block() as block:
            @block.sync
            def _(sp):
                sp.dma_start(saved, flat_x).then_inc(kept, 16)
                K.load(sp, B["b1"], A["b_mlp1"][0])
                K.load(sp, iota[:, :], A["k_iota"])

                def refill(u, chunk):
                    X.wait_low(sp, u, 2 * chunk + 1)
                    n = chunk + RING
                    sp.dma_start(K.slot(first + chunk), expert_source(A, u + n // 12, n % 12))\
                        .then_inc(K.landed[slot(chunk)], 16)

                for chunk in range(12):
                    refill(0, chunk)
                with sp.Fori(1, EXPERTS - 1) as u:
                    for chunk in range(12):
                        refill(u, chunk)
                for chunk in range(12 - RING):
                    refill(EXPERTS - 1, chunk)

            @block.vector
            def _(ve):
                nc.vector.memset(places[:, :], 0.0).then_inc(Y.added, 1)
                ve.wait_ge(kept, 16)
                nc.vector.memset(acc[:, :, :], 0.0).then_inc(ready, 1)
                ve.wait_ge(ready, 1)
                ve.wait_ge(K.loads, loads0 + 32)
                X.dve_pick(ve, 0, 0)
                for j in range(HALVES):
                    X.dve_low(ve, 0, j)
                for par in range(2):
                    X.dve_expert(ve, par, par + 1, par, fresh=par == 0)
                with ve.Fori(1, PAIRS - 1) as i:
                    for par in range(2):
                        X.dve_expert(ve, i * 2 + par, i * 2 + (par + 1), par, fresh=False)
                for u in (EXPERTS - 2, EXPERTS - 1):
                    X.dve_expert(ve, u, u + 1, u % 2, fresh=False, ahead=u < EXPERTS - 1)

            @block.gpsimd
            def _(po):
                X.pool_expert(po, 0)
                with po.Fori(1, EXPERTS) as u:
                    X.pool_expert(po, u)

            @block.scalar
            def _(sc):
                for j in range(HALVES):
                    X.act_high(sc, 0, j, True)
                X.act_xe(sc, 0, 0)
                X.act_xe(sc, 0, 1)
                for par in range(2):
                    X.act_expert(sc, par, fresh=par == 0)
                with sc.Fori(1, PAIRS - 1) as i:
                    for par in range(2):
                        X.act_expert(sc, i * 2 + par, fresh=False)
                for u in (EXPERTS - 2, EXPERTS - 1):
                    X.act_expert(sc, u, fresh=False, ahead=u < EXPERTS - 1)

            @block.tensor
            def _(pe):
                pe.wait_ge(K.loads, loads0 + 32)
                for part in range(2):
                    X.pe_gather(pe, 0, 0, part)
                for par in range(2):
                    X.pe_expert(pe, par, par, fresh=par == 0)
                with pe.Fori(1, PAIRS - 1) as i:
                    for par in range(2):
                        X.pe_expert(pe, i * 2 + par, par, fresh=False)
                for u in (EXPERTS - 2, EXPERTS - 1):
                    X.pe_expert(pe, u, u % 2, fresh=False, ahead=u < EXPERTS - 1)

        def each(eng, body):
            n = eng.value_load(extra_n[0:1, 0:1], min_val=0, max_val=SPILLS)
            with eng.If(n > 0):
                with eng.Fori(0, n) as i:
                    e = eng.value_load(extra_e[0:1, bass.ds(i, 1)], min_val=0, max_val=EXPERTS - 1)
                    eng.wait_ge(Y.added, i * 8 + 1)
                    body(i, e)

        with nc.Block() as block:
            @block.sync
            def _(sp):
                def body(i, e):
                    for n in range(12):
                        if n >= RING:
                            Y.wait_low(sp, i, 2 * (n - RING) + 1)
                        sp.dma_start(K.slot(n), expert_source(A, e, n)).then_inc(landed[n % RING], 16)
                each(sp, body)

            @block.vector
            def _(ve):
                def body(i, e):
                    nc.vector.tensor_scalar(places[:, :], iota[:, :], extra_at[:, bass.ds(i, 1)], None, ALU.add)\
                        .then_inc(shifted, 1)
                    ve.wait_ge(shifted, i + 1)
                    Y.dve_pick(ve, e, 0)
                    for j in range(HALVES):
                        Y.dve_low(ve, i, j)
                    Y.dve_expert(ve, i, None, 0, fresh=True, ahead=False)
                each(ve, body)

            @block.gpsimd
            def _(po):
                each(po, lambda i, e: Y.pool_expert(po, i))

            @block.scalar
            def _(sc):
                def body(i, e):
                    for j in range(HALVES):
                        Y.act_high(sc, i, j, True)
                    Y.act_xe(sc, i, 0)
                    Y.act_xe(sc, i, 1)
                    Y.act_expert(sc, i, fresh=True, ahead=False)
                each(sc, body)

            @block.tensor
            def _(pe):
                def body(i, e):
                    for part in range(2):
                        Y.pe_gather(pe, i, 0, part)
                    Y.pe_expert(pe, i, 0, fresh=True, ahead=False)
                each(pe, body)


def finish_mixture(K, gate, gates_f):
    nc, A = K.nc, K.A
    ring = K.stream
    _, last = ring.span["moe"]
    turned, copied, product, loads0 = K.sem("fm_turned"), K.sem("fm_copied"), K.sem("fm_product"), K.loads_n
    with ExitStack() as ctx:
        b2 = K.sb(ctx, "moe_b2", [EXPERTS, D])
        gT = K.sb(ctx, "moe_gT", [EXPERTS, S])
        with nc.Block() as block:
            @block.sync
            def _(sp):
                K.load(sp, b2[:, :], A["b_mlp2"][0])
                K.load(sp, K.hT[:, :, :].rearrange("p k n -> p (k n)"), K.x_saved)
                for n in range(last, min(last + RING, len(ring.chunks))):
                    K.issue(sp, n)

            @block.tensor
            def _(pe):
                for t in range(NT):
                    ins = nc.tensor.transpose(K.ps[0:EXPERTS, 0, t * P:(t + 1) * P], gate[:, t, 0:EXPERTS],
                                              K.ident[:, :])
                ins.then_inc(turned, 1)
                pe.wait_ge(copied, 1)
                pe.wait_ge(K.loads, loads0 + 32)
                pe.nop().then_inc(K.chunk_used, RING)
                for t in range(NT):
                    for m in range(2):
                        ins = nc.tensor.matmul(K.ps[:, 2 * t + m, :], gT[:, t * P:(t + 1) * P],
                                               b2[:, m * 512:(m + 1) * 512], start=True, stop=True)
                ins.then_inc(product, 1)

            @block.vector
            def _(ve):
                ve.wait_ge(turned, 1)
                nc.vector.tensor_copy(gT[:, :], K.ps[0:EXPERTS, 0, :]).then_inc(copied, 1)
                ve.wait_ge(product, 1)
                flat = lambda a: a[:, :, :].rearrange("p a n -> p (a n)")
                K.dve_link(nc.vector.tensor_tensor(flat(K.x), flat(K.ps), flat(K.x), ALU.add))
                K.dve_link(nc.vector.tensor_tensor(K.x[:, :, :], K.x[:, :, :],
                                                   gates_f.unsqueeze(1).to_broadcast([P, NT, D]), ALU.mult))
                ve.wait_ge(K.loads, loads0 + 32)
                K.dve_link(nc.vector.tensor_tensor(flat(K.x), flat(K.x), flat(K.hT), ALU.add))


def block1(K):
    nc, A = K.nc, K.A
    with ExitStack() as ctx:
        gates = K.sb(ctx, "b1_gates", [P, 2, D])
        mods = K.sb(ctx, "b1_mods", [P, 4, KD])
        cols, at = load_columns(K, "b1_cols", [("c", A["c"][0]), ("g_mix", A["g_mix"][0]), ("g_ffn", A["g_ffn"][0])], ctx)
        col = lambda key, n: cols[:, at[key]:at[key] + n]
        modulation(K, "mod1", col("c", KD), A["b_ada"][0], gates, mods[:, 0, :], mods[:, 1, :], mods[:, 2, :],
                   mods[:, 3, :], col("g_mix", KD), col("g_ffn", KD))
        with nc.sbuf_tensor("b1_xn", [P, NT, D], F32) as xn:
            normalise(K, "b1_norm", xn, mods[:, 0, :], mods[:, 1, :], K.hT)
        with nc.sbuf_tensor("b1_merged", [P, KD, S], F32) as merged:
            with nc.sbuf_tensor("b1_pair", [P, 2, KD, S], F32R) as pair:
                split_rows(K, "b1_pair", K.hT, pair)
                with nc.sbuf_tensor("b1_retT", [P, KD, S], F32) as retT:
                    retention(K, pair, retT)
                    sigmoid_gate(K, "gate_a", pair, merged)
                    with nc.sbuf_tensor("b1_retpair", [P, 2, KD, S], F32R) as retpair:
                        split_rows(K, "b1_retpair", retT, retpair)
                        linear_split(K, "ret_o", "T", retpair, 1,
                                     dve=lambda j, b: nc.vector.tensor_tensor(
                                         merged[:, 2 * j:2 * j + 2, :], b, merged[:, 2 * j:2 * j + 2, :], ALU.mult))
                with nc.sbuf_tensor("b1_attT", [P, AH, S], F32) as attT:
                    with ExitStack() as tables:
                        T0, T12 = K.sb(tables, "b1_T0", [P, AH, T0W]), K.sb(tables, "b1_T12", [P, AH, T12W])
                        jobs = [(h, 0, 1024, 4, 508, T0[:, h, :]) for h in range(AH)]
                        for g in range(1, AG):
                            jobs += [(g * AH + h, 768 + 256 * g, 256, 1, 127, T12[:, h, (g - 1) * P:g * P])
                                     for h in range(AH)]
                        bias_tables(K, "b1_bias", A["rel_bias"], A["k_hot1"], jobs, AG * AH)
                        dilated(K, pair, attT, T0, T12)
                    with nc.sbuf_tensor("b1_gate_b", [P, KD, S], F32) as gb:
                        sigmoid_gate(K, "gate_b", pair, gb)

                        def merge(j, banks):
                            K.dve_link(nc.vector.tensor_tensor(gb[:, 4 * j:4 * j + 4, :], banks,
                                                               gb[:, 4 * j:4 * j + 4, :], ALU.mult))
                            return nc.vector.tensor_tensor(merged[:, 4 * j:4 * j + 4, :], merged[:, 4 * j:4 * j + 4, :],
                                                           gb[:, 4 * j:4 * j + 4, :], ALU.add)
                        attention_out(K, attT, merge)
            add_residual(K, "w_o", merged, 2, gate=gates[:, 0, :])
        with ExitStack() as mctx:
            posm = K.sb(mctx, "moe_posm", [P, NT, EXPERTS + 1])
            gate = K.sb(mctx, "moe_gate", [P, NT, EXPERTS + 1])
            extra = (K.sb(mctx, "extra_n", [P, 1], I32), K.sb(mctx, "extra_e", [P, SPILLS], I32),
                     K.sb(mctx, "extra_at", [P, SPILLS]))
            with nc.sbuf_tensor("b1_xn2", [P, NT, D], F32) as xn:
                normalise(K, "b1_norm2", xn, mods[:, 2, :], mods[:, 3, :], K.hT)
            route(K, A["w_router"][0], A["b_router"][0], posm, gate, extra)
            mixture(K, posm, gate, extra)
            finish_mixture(K, gate, gates[:, 1, :])
        final_norm(K, "b1_out", A["g_final"], False)


def attention_out(K, attT, merge):
    nc = K.nc
    first, last = K.stream.span["att_o"]
    evac0 = K.dve_evac_n
    with nc.Block() as block:
        @block.sync
        def _(sp):
            K.refill(sp, first, last)

        @block.tensor
        def _(pe):
            for j in range(2):
                K.wait_chunk(pe, first + j)
                w = K.slot(first + j)
                for i in range(4):
                    for k in range(AH):
                        ins = nc.tensor.matmul(K.ps[:, 4 * j + i, :], w[:, k, i * P:(i + 1) * P], attT[:, k, :],
                                               start=(k == 0), stop=(k == AH - 1))
                ins.then_inc(K.chunk_used, 1)

        @block.vector
        def _(ve):
            for j in range(2):
                ve.wait_ge(K.chunk_used, first + j + 1)
                merge(j, K.ps[:, 4 * j:4 * j + 4, :]).then_inc(K.dve_evac, 1)
    K.dve_evac_n += 2



DH, DQK, DV = 4, 64, 128
GH, GDK, GDV, GC = 4, 32, 64, 64
C2_Q, C2_K, C2_V = 0, 512, 1024
C2_GQK, C2_GV, C2_GLR, C2_GR, C2_POOL = 1536, 1792, 2048, 2064, 2320
LAM_INIT = 0.8 - 0.6 * math.exp(0.0)
WINDOWS = (2, 4, 8, 16)


def plan_ffn(st, name, w_gate, gate0, w_up, up0, w_down):
    for i in range(FFN_T // 2):
        st.add(f"{name}_up", columns(w_gate, (gate0 + 256 * i, 256)))
        st.add(f"{name}_up", columns(w_up, (up0 + 256 * i, 256)))
    for j in range(2):
        for k in range(0, FFN_T, 4):
            st.add(f"{name}_down", rows(w_down, k, min(4, FFN_T - k), 512 * j))


def plan_block2(st, A):
    w = A["w_in_2"][0]
    for c0 in (C2_Q, C2_K, C2_V):
        for c in range(2):
            st.add("b2_qkv", rows(w, 4 * c, 4, c0))
    for c0 in (C2_GQK, C2_GV, C2_GR, C2_POOL):
        st.add("b2_rest", columns(w, (c0, 256)))
    st.add("b2_lr", columns(w, (C2_GLR, 16)))
    for j in range(2):
        for c in range(2):
            st.add("b2_out", rows(A["w_out_2"][0], 4 * c, 4, 512 * j))
    plan_ffn(st, "b2", A["w_gate_2"][0], 0, A["w_up_2"][0], 0, A["w_down_2"][0])


def group_norm(K, name, view, groups, width, eps, centre=False):
    nc = K.nc
    var, root = K.sem(f"{name}_var"), K.sem(f"{name}_root")
    with ExitStack() as ctx:
        sq = K.sb(ctx, f"{name}_sq", [P, groups, width])
        ms = K.sb(ctx, f"{name}_ms", [P, groups])
        sd = K.sb(ctx, f"{name}_sd", [P, groups])
        spread = ms[:, :].unsqueeze(2).to_broadcast([P, groups, width])
        with nc.Block() as block:
            @block.vector
            def _(ve):
                if centre:
                    K.dve_link(nc.vector.tensor_reduce(ms[:, :], view, AX, ALU.add))
                    K.dve_link(nc.vector.tensor_scalar(ms[:, :], ms[:, :], 1.0 / width, None, ALU.mult))
                    K.dve_link(nc.vector.tensor_tensor(view, view, spread, ALU.subtract))
                K.dve_link(nc.vector.tensor_tensor(sq[:, :, :], view, view, ALU.mult))
                K.dve_link(nc.vector.tensor_reduce(ms[:, :], sq[:, :, :], AX, ALU.add))
                nc.vector.tensor_scalar(ms[:, :], ms[:, :], 1.0 / width, eps, ALU.mult, ALU.add).then_inc(var, 1)
                ve.wait_ge(root, 1)
                K.dve_link(nc.vector.reciprocal(ms[:, :], sd[:, :]))
                K.dve_link(nc.vector.tensor_tensor(view, view, spread, ALU.mult))

            @block.scalar
            def _(sc):
                sc.wait_ge(var, 1)
                nc.scalar.activation(sd[:, :], ms[:, :], ACT.Sqrt).then_inc(root, 1)


def turn_tiles(K, name, sources, dests, scale=None):
    nc = K.nc
    turned, copied = K.sem(f"{name}_turned"), K.sem(f"{name}_copied")
    with nc.Block() as block:
        @block.tensor
        def _(pe):
            for i, src in enumerate(sources):
                if i >= 8:
                    pe.wait_ge(copied, i - 7)
                for t in range(NT):
                    ins = nc.tensor.transpose(K.ps[:, i % 8, t * P:(t + 1) * P], src(t), K.ident[:, :])
                ins.then_inc(turned, 1)

        @block.scalar
        def _(sc):
            for i, dst in enumerate(dests):
                sc.wait_ge(turned, i + 1)
                s = scale(i) if scale else None
                nc.scalar.activation(dst, K.ps[:, i % 8, :], ACT.Identity, scale=s if s is not None else 1.0, bias=0.0)\
                    .then_inc(copied, 1)


def diff_attention(K, name, qT, kT, v, TB, neg_lam, a_out):
    nc, ps = K.nc, K.ps
    scores, biased, maxed, softmax, mixed, turned, pT_ready, av, stored = (
        K.sem(f"{name}_{n}") for n in "scores biased maxed softmax mixed turned pT av stored".split())
    U = DH * NT
    with ExitStack() as ctx:
        s = K.sb(ctx, f"{name}_s", [P, 2, 2, S])
        w = K.sb(ctx, f"{name}_w", [P, 2, S])
        pT = K.sb(ctx, f"{name}_pTs", [P, S])
        nm = K.sb(ctx, f"{name}_nm", [P, 2, 2])
        l = K.sb(ctx, f"{name}_l", [P, 2, 2])
        with nc.Block() as block:
            @block.tensor
            def _(pe):
                def score(u):
                    h, i = u // NT, u % NT
                    if u >= 2:
                        pe.wait_ge(biased, u - 1)
                    for m in range(2):
                        r = slice(m * DQK, (m + 1) * DQK)
                        ins = nc.tensor.matmul(ps[:, 2 * (u % 2) + m, 0:(i + 1) * P], qT[r, h, i * P:(i + 1) * P],
                                               kT[r, h, 0:(i + 1) * P], start=True, stop=True)
                    ins.then_inc(scores, 1)

                score(0)
                for u in range(U):
                    h, i = u // NT, u % NT
                    if u + 1 < U:
                        score(u + 1)
                    pe.wait_ge(mixed, u + 1)
                    if u:
                        pe.wait_ge(pT_ready, u)
                    for j in range(i + 1):
                        ins = nc.tensor.transpose(ps[:, 4, j * P:(j + 1) * P], w[:, u % 2, j * P:(j + 1) * P],
                                                  K.ident[:, :])
                    ins.then_inc(turned, 1)
                    pe.wait_ge(pT_ready, u + 1)
                    if u >= 2:
                        pe.wait_ge(stored, u - 1)
                    for j in range(i + 1):
                        ins = nc.tensor.matmul(ps[:, 5 + u % 2, 0:DV], pT[:, j * P:(j + 1) * P],
                                               v[:, j, h * DV:(h + 1) * DV], start=(j == 0), stop=(j == i))
                    ins.then_inc(av, 1)

            @block.scalar
            def _(sc):
                for u in range(U):
                    h, i = u // NT, u % NT
                    n, b = (i + 1) * P, u % 2
                    sc.wait_ge(maxed, u + 1)
                    for m in range(2):
                        nc.scalar.activation(s[:, b, m, 0:n], s[:, b, m, 0:n], ACT.Exp, bias=nm[:, b, m:m + 1],
                                             scale=1.0, accum_out=l[:, b, m:m + 1]).then_inc(softmax, 1)
                    sc.wait_ge(turned, u + 1)
                    if u:
                        sc.wait_ge(av, u)
                    nc.scalar.activation(pT[:, 0:n], ps[:, 4, 0:n], ACT.Copy).then_inc(pT_ready, 1)
                    sc.wait_ge(av, u + 1)
                    nc.scalar.activation(a_out[:, i, h * DV:(h + 1) * DV], ps[:, 5 + u % 2, 0:DV], ACT.Copy)\
                        .then_inc(stored, 1)

            @block.vector
            def _(ve):
                def soften(u):
                    h, i = u // NT, u % NT
                    n, b = (i + 1) * P, u % 2
                    ve.wait_ge(scores, u + 1)
                    if u >= 2:
                        ve.wait_ge(mixed, u - 1)
                    nc.vector.tensor_tensor(s[:, b, :, 0:n], ps[:, 2 * b:2 * b + 2, 0:n],
                                            TB[:, h, (3 - i) * P:].unsqueeze(1).to_broadcast([P, 2, n]), ALU.add)\
                        .then_inc(biased, 1)
                    ve.wait_ge(biased, u + 1)
                    K.dve_link(nc.vector.tensor_reduce(nm[:, b, :], s[:, b, :, 0:n], AX, ALU.max))
                    nc.vector.tensor_scalar(nm[:, b, :], nm[:, b, :], -1.0, None, ALU.mult).then_inc(maxed, 1)

                soften(0)
                for u in range(U):
                    n, b = (u % NT + 1) * P, u % 2
                    if u + 1 < U:
                        soften(u + 1)
                    ve.wait_ge(softmax, 2 * u + 2)
                    K.dve_link(nc.vector.reciprocal(l[:, b, :], l[:, b, :]))
                    K.dve_link(nc.vector.tensor_tensor(l[:, b, 1:2], l[:, b, 1:2], neg_lam, ALU.mult))
                    if u >= 2:
                        ve.wait_ge(turned, u - 1)
                    K.dve_link(nc.vector.tensor_scalar(w[:, b, 0:n], s[:, b, 0, 0:n], l[:, b, 0:1], None, ALU.mult))
                    nc.vector.scalar_tensor_tensor(w[:, b, 0:n], s[:, b, 1, 0:n], l[:, b, 1:2], w[:, b, 0:n],
                                                   ALU.mult, ALU.add).then_inc(mixed, 1)


def gla(K, glrT, gqk, gv, gr, b_out):
    nc, ps, A = K.nc, K.ps, K.A
    zdone, absd, ln_in, lndone, la_ready, cum, sub, expd, decd, qk_ready, turned, qkT_ready, scored, masked = (
        K.sem(f"gla_{n}") for n in "z abs ln_in ln la cum sub exp dec qk turned qkT scored masked".split())
    kv_done, kv_used, state_ready, o_done = (K.sem(f"gla_{n}") for n in "kv kv_used state o".split())
    loads0 = K.loads_n
    W = GH * GDK
    with ExitStack() as ctx:
        gw = K.sb(ctx, "gla_w", [16, W])
        gb = K.sb(ctx, "gla_b", [P, W])
        tri = K.sb(ctx, "gla_tri", [P, 2, P])
        hm = K.sb(ctx, "gla_hm", [P, GH * GDV])
        z = K.sb(ctx, "gla_zb", [P, NT, W])
        az = K.sb(ctx, "gla_az", [P, NT, W])
        la = K.sb(ctx, "gla_lab", [P, NT, W])
        eb = K.sb(ctx, "gla_eb", [P, NT, W])
        en = K.sb(ctx, "gla_en", [P, NT, W])
        el = K.sb(ctx, "gla_el", [P, NT, W])
        qT = K.sb(ctx, "gla_qT", [P, S])
        kT = K.sb(ctx, "gla_kT", [P, S])
        at = K.sb(ctx, "gla_at", [P, NT, GH, P])
        dec = K.sb(ctx, "gla_decb", [P, 8])
        st = K.sb(ctx, "gla_st", [P, 8, GH * GDV])
        kvm = K.sb(ctx, "gla_kvm", [P, GH * GDV])
        flat = lambda a: a[:, :, :].rearrange("p t n -> p (t n)")
        with nc.Block() as block:
            @block.sync
            def _(sp):
                K.load(sp, gw[:, :], A["gla_gate_w_2"][0])
                K.load(sp, gb[:, :], A["gla_gate_b_2"][0].rearrange("(a n) -> a n", a=1).partition_broadcast(P))
                K.load(sp, tri[:, :, :], A["k_gla_tri"])
                K.load(sp, hm[:, :], A["k_gla_heads"])

            @block.tensor
            def _(pe):
                pe.wait_ge(K.loads, loads0 + 64)
                for t in range(NT):
                    ins = nc.tensor.matmul(ps[:, 0, t * W:(t + 1) * W], glrT[:, t * P:(t + 1) * P], gw[:, :],
                                           start=True, stop=True)
                ins.then_inc(zdone, 1)
                pe.wait_ge(la_ready, 1)
                for t in range(NT):
                    nc.tensor.matmul(ps[:, 1, t * W:(t + 1) * W], tri[:, 0, :], la[:, t, :], start=True, stop=True)
                    nc.tensor.matmul(ps[:, 2, t * W:(t + 1) * W], tri[:, 1, :], la[:, t, :], start=True, stop=True)
                    ins = nc.tensor.matmul(ps[:, 3, 2 * t:2 * t + 2], la[:, t, :], tri[:, 1, 0:P:GC], start=True,
                                           stop=True)
                ins.then_inc(cum, 1)
                pe.wait_ge(qk_ready, 1)
                for t in range(NT):
                    nc.tensor.transpose(ps[:, 4, t * P:(t + 1) * P], eb[:, t, :], K.ident[:, :])
                    ins = nc.tensor.transpose(ps[:, 5, t * P:(t + 1) * P], en[:, t, :], K.ident[:, :])
                ins.then_inc(turned, 1)
                pe.wait_ge(qkT_ready, 1)
                for h in range(GH):
                    r = slice(h * GDK, (h + 1) * GDK)
                    for t in range(NT):
                        ins = nc.tensor.matmul(ps[:, 4 + h, t * P:(t + 1) * P], kT[r, t * P:(t + 1) * P],
                                               qT[r, t * P:(t + 1) * P], start=True, stop=True)
                    ins.then_inc(scored, 1)
                pe.wait_ge(qk_ready, 2)
                for n in range(7):
                    t, r = n // 2, slice((n % 2) * GC, (n % 2 + 1) * GC)
                    if n >= 2:
                        pe.wait_ge(kv_used, n - 1)
                    nc.tensor.matmul(ps[:, n % 2, 0:GH * GDV], el[r, t, :], gv[r, t, :], start=True, stop=True)\
                        .then_inc(kv_done, 1)
                pe.wait_ge(masked, GH)
                pe.wait_ge(qkT_ready, 1)
                for t in range(NT):
                    for h in range(GH):
                        c = slice(h * GDV, (h + 1) * GDV)
                        ins = nc.tensor.matmul(ps[:, 2 + t // 2, (t % 2) * 256 + h * GDV:(t % 2) * 256 + (h + 1) * GDV],
                                               at[:, t, h, :], gv[:, t, c], start=True, stop=True)
                pe.wait_ge(state_ready, 8)
                for n in range(8):
                    t, r = n // 2, slice((n % 2) * GC, (n % 2 + 1) * GC)
                    ins = nc.tensor.matmul(ps[r, 4 + t // 2, (t % 2) * 256:(t % 2) * 256 + 256],
                                           qT[:, n * GC:(n + 1) * GC], st[:, n, :], start=True, stop=True)
                ins.then_inc(o_done, 1)

            @block.scalar
            def _(sc):
                sc.wait_ge(absd, 1)
                nc.scalar.activation(flat(az), flat(az), ACT.Exp, scale=-1.0).then_inc(ln_in, 1)
                sc.wait_ge(ln_in, 1)
                nc.scalar.activation(flat(az), flat(az), ACT.Ln, bias=1.0).then_inc(lndone, 1)
                sc.wait_ge(cum, 1)
                nc.scalar.activation(flat(eb), ps[:, 1, :], ACT.Exp).then_inc(expd, 1)
                nc.scalar.activation(flat(en), ps[:, 1, :], ACT.Exp, scale=-1.0).then_inc(expd, 1)
                nc.scalar.activation(dec[:, :], ps[:, 3, 0:8], ACT.Exp).then_inc(decd, 1)
                sc.wait_ge(sub, 1)
                nc.scalar.activation(flat(el), flat(el), ACT.Exp).then_inc(expd, 1)
                sc.wait_ge(turned, 1)
                nc.scalar.activation(qT[:, :], ps[:, 4, :], ACT.Copy)
                nc.scalar.activation(kT[:, :], ps[:, 5, :], ACT.Copy).then_inc(qkT_ready, 1)

            @block.vector
            def _(ve):
                ve.wait_ge(zdone, 1)
                ve.wait_ge(K.loads, loads0 + 64)
                K.dve_link(nc.vector.tensor_tensor(z[:, :, :], ps[:, 0, :].rearrange("p (t n) -> p t n", n=W),
                                                   gb[:, :].unsqueeze(1).to_broadcast([P, NT, W]), ALU.add))
                nc.vector.scalar_tensor_tensor(flat(az), flat(z), -1.0, flat(z), ALU.mult, ALU.max).then_inc(absd, 1)
                K.dve_link(nc.vector.tensor_scalar(flat(z), flat(z), 0.0, None, ALU.min))
                ve.wait_ge(lndone, 1)
                K.dve_link(nc.vector.tensor_tensor(flat(la), flat(z), flat(az), ALU.subtract))
                nc.vector.tensor_scalar(flat(la), flat(la), 1.0 / 16.0, None, ALU.mult).then_inc(la_ready, 1)
                ve.wait_ge(expd, 2)
                K.dve_link(nc.vector.tensor_copy(flat(z), ps[:, 1, :]))
                nc.vector.tensor_tensor(flat(el), ps[:, 2, :], flat(z), ALU.subtract).then_inc(sub, 1)
                ve.wait_ge(decd, 1)
                K.dve_link(nc.vector.scalar_tensor_tensor(eb[:, :, :], gqk[:, :, 0:W], float(GDK) ** -0.5, eb[:, :, :],
                                                          ALU.mult, ALU.mult))
                nc.vector.tensor_tensor(en[:, :, :], gqk[:, :, W:], en[:, :, :], ALU.mult).then_inc(qk_ready, 1)
                ve.wait_ge(expd, 3)
                nc.vector.tensor_tensor(el[:, :, :], gqk[:, :, W:], el[:, :, :], ALU.mult).then_inc(qk_ready, 1)
                for h in range(GH):
                    ve.wait_ge(scored, h + 1)
                    nc.vector.tensor_tensor(at[:, :, h, :], ps[:, 4 + h, :].rearrange("p (t n) -> p t n", n=P),
                                            tri[:, 0, :].unsqueeze(1).to_broadcast([P, NT, P]), ALU.mult)\
                        .then_inc(masked, 1)
                nc.vector.memset(st[:, 0, :], 0.0).then_inc(state_ready, 1)
                for n in range(7):
                    ve.wait_ge(kv_done, n + 1)
                    ve.wait_ge(state_ready, n + 1)
                    nc.vector.tensor_tensor(kvm[:, :], ps[:, n % 2, 0:GH * GDV], hm[:, :], ALU.mult)\
                        .then_inc(kv_used, 1)
                    ve.wait_ge(kv_used, n + 1)
                    nc.vector.scalar_tensor_tensor(st[:, n + 1, :], st[:, n, :], dec[:, n:n + 1], kvm[:, :], ALU.mult,
                                                   ALU.add).then_inc(state_ready, 1)
                ve.wait_ge(o_done, 1)
                two = lambda b: ps[:, b:b + 2, :].rearrange("p a n -> p (a n)")
                K.dve_link(nc.vector.tensor_copy(flat(b_out), two(2)))
                K.dve_link(nc.vector.tensor_tensor(flat(b_out), two(4), flat(b_out), ALU.add))
        group_norm(K, "gla_norm", b_out[:, :, :].rearrange("p t (h d) -> p (t h) d", d=GDV), NT * GH, GDV, EPS)
        gated = K.sem("gla_gated")
        gn = K.sb(ctx, "gla_gn", [P, GDV])
        with nc.Block() as block:
            @block.sync
            def _(sp):
                K.load(sp, gn[:, :], A["gla_norm_g_2"][0].rearrange("(a n) -> a n", a=1).partition_broadcast(P))

            @block.scalar
            def _(sc):
                nc.scalar.activation(flat(z), gr[:, :, 0:W], ACT.Sigmoid)
                nc.scalar.activation(flat(az), gr[:, :, W:], ACT.Sigmoid).then_inc(gated, 1)

            @block.vector
            def _(ve):
                ve.wait_ge(K.loads, K.loads_n)
                o = b_out[:, :, :].rearrange("p t (h d) -> p (t h) d", d=GDV)
                K.dve_link(nc.vector.tensor_tensor(o, o, gn[:, :].unsqueeze(1).to_broadcast([P, NT * GH, GDV]), ALU.mult))
                K.dve_link(nc.vector.tensor_tensor(b_out[:, :, :], b_out[:, :, :], gr[:, :, :], ALU.mult))
                ve.wait_ge(gated, 1)
                K.dve_link(nc.vector.tensor_tensor(b_out[:, :, 0:W], b_out[:, :, 0:W], z[:, :, :], ALU.mult))
                K.dve_link(nc.vector.tensor_tensor(b_out[:, :, W:], b_out[:, :, W:], az[:, :, :], ALU.mult))


def pooling(K, u, scale_cols, mixedT):
    nc, ps, A = K.nc, K.ps, K.A
    pooled, copied, mixed = K.sem("pool_pooled"), K.sem("pool_copied"), K.sem("pool_mixed")
    with ExitStack() as ctx:
        band = K.sb(ctx, "pool_band", [P, 4, 3, P])
        pw = K.sb(ctx, "pool_w", [P, 2, GDV])
        pT = K.sb(ctx, "pool_T", [P, 2, S])
        with nc.Block() as block:
            @block.sync
            def _(sp):
                K.load(sp, band[:, :, :, :], A["k_pool"])
                for g in range(4):
                    K.load(sp, pw[(g % 2) * 64:(g % 2) * 64 + 64, g // 2, :], A["pool_w_2"][0, g])

            @block.tensor
            def _(pe):
                pe.wait_ge(K.loads, K.loads_n)
                for g in range(4):
                    r = slice((g % 2) * 64, (g % 2) * 64 + 64)
                    for i in range(NT):
                        out = ps[r, g // 2, i * P:(i + 1) * P]
                        ins = nc.tensor.matmul(out, u[:, i, g * 64:(g + 1) * 64], band[:, g, 0 if i == 0 else 1, :],
                                               start=True, stop=(i == 0))
                        if i:
                            ins = nc.tensor.matmul(out, u[:, i - 1, g * 64:(g + 1) * 64], band[:, g, 2, :],
                                                   start=False, stop=True)
                ins.then_inc(pooled, 1)
                pe.wait_ge(copied, 1)
                for g in range(4):
                    r = slice((g % 2) * 64, (g % 2) * 64 + 64)
                    ins = nc.tensor.matmul(ps[r, 2 + g // 2, :], pw[r, g // 2, :], pT[r, g // 2, :], start=True,
                                           stop=True)
                ins.then_inc(mixed, 1)

            @block.vector
            def _(ve):
                ve.wait_ge(pooled, 1)
                nc.vector.tensor_copy(pT[:, :, :], ps[:, 0:2, :]).then_inc(copied, 1)
                ve.wait_ge(mixed, 1)
                for i in range(2):
                    nc.vector.tensor_scalar(mixedT[:, 6 + i, :], ps[:, 2 + i, :], scale_cols[:, i:i + 1], None, ALU.mult)


def swiglu_up(K, stage, pair, ffT):
    nc = K.nc
    with nc.sbuf_tensor(f"{stage}_sig", [P, 2, 2, S], F32) as sg:
        def act(j, banks):
            return nc.scalar.activation(sg[:, j % 2, :, :], banks[:, 0:2, :], ACT.Sigmoid)

        def dve(j, banks):
            K.dve_link(nc.vector.tensor_tensor(sg[:, j % 2, :, :], sg[:, j % 2, :, :], banks[:, 0:2, :], ALU.mult))
            return nc.vector.tensor_tensor(ffT[:, 2 * j:2 * j + 2, :], sg[:, j % 2, :, :], banks[:, 2:4, :], ALU.mult)

        linear_split(K, stage, "T", pair, 2, act=act, dve=dve)


def block2(K):
    nc, A = K.nc, K.A
    with ExitStack() as ctx:
        cols, at = load_columns(K, "b2_cols", [("g1", A["attn_norm_g_2"][0]), ("g2", A["ffn_norm_g_2"][0]),
                                               ("pool", A["pool_scale_2"][0])], ctx)
        with nc.sbuf_tensor("b2_xn", [P, NT, D], F32) as xn:
            normalise(K, "b2_norm", xn, cols[:, at["g1"]:at["g1"] + KD], None, K.hT)
        with ExitStack() as mix:
            mixedT = K.sb(mix, "b2_mixedT", [P, KD, S])
            qk = K.sb(mix, "b2_qk", [P, 2, NT, 512])
            v = K.sb(mix, "b2_v", [P, NT, 512])
            rest = K.sb(mix, "b2_rest", [P, 4, NT, 256])
            glrT = K.sb(mix, "b2_glrT", [16, S])
            dests = [qk[:, 0, :, :], qk[:, 1, :, :], v[:, :, :]]
            with nc.sbuf_tensor("b2_xpair", [P, 2, KD, S], F32R) as pair:
                split_rows(K, "b2_xpair", K.hT, pair)
                linear_split(K, "b2_qkv", "N", pair, 2,
                             act=lambda j, b: nc.scalar.activation(dests[j], b, ACT.Copy))
                linear_split(K, "b2_rest", "N", pair, 1,
                             act=lambda j, b: nc.scalar.activation(rest[:, j, :, :], b[:, :, 0:256], ACT.Copy))
            first, last = K.stream.span["b2_lr"]
            lr_done = K.sem("b2_lr_done")
            with nc.Block() as block:
                @block.sync
                def _(sp):
                    K.refill(sp, first, last)

                @block.tensor
                def _(pe):
                    K.wait_chunk(pe, first)
                    K.use_T(pe, first, 16, 0, K.hT, K.ps[0:16, 0, :], True, m=16)

                @block.vector
                def _(ve):
                    ve.wait_ge(K.chunk_used, first + 1)
                    nc.vector.tensor_copy(glrT[:, :], K.ps[0:16, 0, :])
            with ExitStack() as da:
                group_norm(K, "b2_qkn", qk[:, :, :, :].rearrange("p a t (h d) -> p (a t h) d", d=DQK), 64, DQK, EPS)
                gq = K.sb(da, "b2_gq", [P, 2])
                lv = K.sb(da, "b2_lv", [P, 4, DQK])
                lp = K.sb(da, "b2_lp", [P, 2, DQK])
                ls = K.sb(da, "b2_ls", [P, 2])
                neg_lam = K.sb(da, "b2_neg_lam", [P, 1])
                lsum, lexp = K.sem("b2_lam_sum"), K.sem("b2_lam_exp")
                with nc.Block() as block:
                    @block.sync
                    def _(sp):
                        for i, key in enumerate(("q_norm_g_2", "k_norm_g_2")):
                            for m in range(2):
                                K.load(sp, gq[m * DQK:(m + 1) * DQK, i:i + 1],
                                       A[key][0].rearrange("(p a) -> p a", a=1))
                        K.load(sp, lv[:, :, :].rearrange("p a n -> p (a n)"),
                               A["lambda_vecs_2"].rearrange("o a n -> o (a n)").partition_broadcast(P))

                    @block.vector
                    def _(ve):
                        ve.wait_ge(K.loads, K.loads_n)
                        K.dve_link(nc.vector.scalar_tensor_tensor(gq[:, 0:1], gq[:, 0:1], float(DQK) ** -0.5,
                                                                  gq[:, 1:2], ALU.mult, ALU.mult))
                        K.dve_link(nc.vector.tensor_tensor(lp[:, :, :], lv[:, 0:4:2, :], lv[:, 1:4:2, :], ALU.mult))
                        nc.vector.tensor_reduce(ls[:, :], lp[:, :, :], AX, ALU.add).then_inc(lsum, 1)
                        ve.wait_ge(lexp, 1)
                        K.dve_link(nc.vector.tensor_tensor(neg_lam[:, :], ls[:, 1:2], ls[:, 0:1], ALU.subtract))
                        K.dve_link(nc.vector.tensor_scalar(neg_lam[:, :], neg_lam[:, :], LAM_INIT, None, ALU.subtract))

                    @block.scalar
                    def _(sc):
                        sc.wait_ge(lsum, 1)
                        nc.scalar.activation(ls[:, :], ls[:, :], ACT.Exp).then_inc(lexp, 1)
                TB = K.sb(da, "b2_TB", [P, DH, S])
                bias_tables(K, "b2_bias", A["rel_bias_2"], A["k_hot2"],
                            [(h, 0, 640, 1, 127, TB[:, h, :]) for h in range(DH)], DH)
                qkT = K.sb(da, "b2_qkT", [P, 2, DH, S])
                turn_tiles(K, "b2_qkT",
                           [(lambda t, i=i: qk[:, i // DH, t, (i % DH) * P:(i % DH + 1) * P]) for i in range(2 * DH)],
                           [qkT[:, i // DH, i % DH, :] for i in range(2 * DH)],
                           scale=lambda i: gq[:, 0:1] if i < DH else None)
                diff_attention(K, "da", qkT[:, 0, :, :], qkT[:, 1, :, :], v, TB, neg_lam[:, :], qk[:, 0, :, :])
            a_out = qk[:, 0, :, :]
            group_norm(K, "b2_subln", a_out.rearrange("p t (h d) -> p (t h) d", d=DV), NT * DH, DV, EPS)
            with nc.sbuf_tensor("b2_sg", [P, DV], F32) as sg:
                with nc.Block() as block:
                    @block.sync
                    def _(sp):
                        K.load(sp, sg[:, :], A["da_subln_g_2"][0].rearrange("(a n) -> a n", a=1).partition_broadcast(P))

                    @block.vector
                    def _(ve):
                        ve.wait_ge(K.loads, K.loads_n)
                        K.dve_link(nc.vector.tensor_scalar(sg[:, :], sg[:, :], 1.0 - LAM_INIT, None, ALU.mult))
                        o = a_out.rearrange("p t (h d) -> p (t h) d", d=DV)
                        K.dve_link(nc.vector.tensor_tensor(o, o, sg[:, :].unsqueeze(1).to_broadcast([P, NT * DH, DV]),
                                                           ALU.mult))
            with nc.sbuf_tensor("b2_bout", [P, NT, 256], F32) as b_out:
                gla(K, glrT, rest[:, 0, :, :], rest[:, 1, :, :], rest[:, 2, :, :], b_out)
                turn_tiles(K, "b2_mixT",
                           [(lambda t, i=i: a_out[:, t, i * P:(i + 1) * P]) for i in range(4)] +
                           [(lambda t, i=i: b_out[:, t, i * P:(i + 1) * P]) for i in range(2)],
                           [mixedT[:, i, :] for i in range(6)])
            pooling(K, rest[:, 3, :, :], cols[:, at["pool"]:at["pool"] + 2], mixedT)
            add_residual(K, "b2_out", mixedT, 2)
        with nc.sbuf_tensor("b2_xn2", [P, NT, D], F32) as xn:
            normalise(K, "b2_norm2", xn, cols[:, at["g2"]:at["g2"] + KD], None, K.hT)
        with nc.sbuf_tensor("b2_ffT", [P, FFN_T, S], F32) as ffT:
            with nc.sbuf_tensor("b2_hpair", [P, 2, KD, S], F32R) as pair:
                split_rows(K, "b2_hpair", K.hT, pair)
                swiglu_up(K, "b2_up", pair, ffT)
            add_residual(K, "b2_down", ffT, 6)



HD = 64
C3_FQ, C3_FK, C3_FV, C3_FF = 0, 256, 512, 768
C3_RW = 772
C3_MQ, C3_MK, C3_MV = 2564, 2820, 3076
RW_T = 4
RW_H = 8
CT = P // RWKV_C
DECAY_SCALE = -math.exp(-0.5)
GN_EPS_3 = 64e-5
LEVELS = (2, 4, 8, 16)


def plan_block3(st, A):
    w = A["w_in_3"][0]
    for s in range(12):
        for c in range(2):
            st.add("mod3", rows(A["w_mod_3"][0], 4 * c, 4, 512 * s))
    for c0 in (C3_FQ, C3_FK, C3_MQ, C3_MK):
        st.add("b3_qk", columns(w, (c0, 256)))
    for c0 in (C3_FV, C3_MV):
        st.add("b3_v", columns(w, (c0, 256)))
    st.add("b3_f", columns(w, (C3_FF, 4)))
    for i in range(7):
        st.add("b3_rw", columns(w, (C3_RW + 256 * i, 256)))
    for j in range(2):
        for c in range(2):
            st.add("b3_out", rows(A["w_out_3"][0], 4 * c, 4, 512 * j))
    plan_ffn(st, "b3", A["w_up_3"][0], 0, A["w_up_3"][0], FFN, A["w_down_3"][0])


def forget_sums(K, fcols, neg_f):
    nc, ps, A = K.nc, K.ps, K.A
    absd, expd, lnd, spread, summed = (K.sem(f"ff_{n}") for n in "abs exp ln spread sum".split())
    with ExitStack() as ctx:
        fb = K.sb(ctx, "ff_b", [P, 4])
        tri = K.sb(ctx, "ff_tri", [P, P])
        az = K.sb(ctx, "ff_az", [P, NT, 4])
        lfb = K.sb(ctx, "ff_lfb", [P, NT, 4, P])
        with nc.Block() as block:
            @block.sync
            def _(sp):
                K.load(sp, fb[:, :], A["fox_f_bias_3"][0].rearrange("(a n) -> a n", a=1).partition_broadcast(P))
                K.load(sp, tri[:, :], A["k_upto"])

            @block.vector
            def _(ve):
                ve.wait_ge(K.loads, K.loads_n)
                K.dve_link(nc.vector.tensor_tensor(fcols[:, :, :], fcols[:, :, :],
                                                   fb[:, :].unsqueeze(1).to_broadcast([P, NT, 4]), ALU.add))
                nc.vector.scalar_tensor_tensor(az[:, :, :], fcols[:, :, :], -1.0, fcols[:, :, :], ALU.mult, ALU.max)\
                    .then_inc(absd, 1)
                K.dve_link(nc.vector.tensor_scalar(fcols[:, :, :], fcols[:, :, :], 0.0, None, ALU.min))
                ve.wait_ge(lnd, 1)
                K.dve_link(nc.vector.tensor_tensor(fcols[:, :, :], az[:, :, :], fcols[:, :, :], ALU.subtract))
                nc.vector.tensor_copy(lfb[:, :, :, :].rearrange("p t h n -> p (t h) n"),
                                      fcols[:, :, :].rearrange("p t h -> p (t h)").unsqueeze(2)
                                      .to_broadcast([P, NT * 4, P])).then_inc(spread, 1)
                ve.wait_ge(summed, 1)
                nc.vector.tensor_copy(neg_f, ps[:, 0:4, :])

            @block.scalar
            def _(sc):
                sc.wait_ge(absd, 1)
                nc.scalar.activation(az[:, :, :], az[:, :, :], ACT.Exp, scale=-1.0).then_inc(expd, 1)
                sc.wait_ge(expd, 1)
                nc.scalar.activation(az[:, :, :], az[:, :, :], ACT.Ln, bias=1.0).then_inc(lnd, 1)

            @block.tensor
            def _(pe):
                pe.wait_ge(spread, 1)
                for h in range(4):
                    for s in range(NT):
                        for t in range(s + 1):
                            ins = nc.tensor.matmul(ps[:, h, s * P:(s + 1) * P], lfb[:, t, h, :],
                                                   tri[:, :] if t == s else K.ones[:, :], start=(t == 0), stop=(t == s))
                ins.then_inc(summed, 1)


def causal_attention(K, qkT, v, neg_f, y):
    nc, ps, A = K.nc, K.ps, K.A
    scores, biased, diag, maxed, softmax, turned, pT_ready, av, stored = (
        K.sem(f"ca_{n}") for n in "scores biased diag maxed softmax turned pT av stored".split())
    U = 4 * NT
    with ExitStack() as ctx:
        s = K.sb(ctx, "ca_s", [P, 2, 2, S])
        pT = K.sb(ctx, "ca_pTs", [P, 2, S])
        nm = K.sb(ctx, "ca_nm", [P, 2, 2])
        l = K.sb(ctx, "ca_l", [P, 2, 2])
        mask = K.sb(ctx, "ca_mask", [P, P])
        with nc.Block() as block:
            @block.sync
            def _(sp):
                K.load(sp, mask[:, :], A["k_future"])

            @block.tensor
            def _(pe):
                def score(u):
                    g, i = u // NT, u % NT
                    q, k = 4 * (g // 2) + g % 2, 4 * (g // 2) + 2 + g % 2
                    if u >= 2:
                        pe.wait_ge(biased, u - 1)
                    for m in range(2):
                        r = slice(m * HD, (m + 1) * HD)
                        ins = nc.tensor.matmul(ps[:, 2 * (u % 2) + m, 0:(i + 1) * P], qkT[r, q, i * P:(i + 1) * P],
                                               qkT[r, k, 0:(i + 1) * P], start=True, stop=True)
                    ins.then_inc(scores, 1)

                score(0)
                for u in range(U):
                    g, i = u // NT, u % NT
                    if u + 1 < U:
                        score(u + 1)
                    pe.wait_ge(softmax, 2 * u + 2)
                    if u:
                        pe.wait_ge(pT_ready, u)
                    for m in range(2):
                        for j in range(i + 1):
                            ins = nc.tensor.transpose(ps[:, 4 + m, j * P:(j + 1) * P],
                                                      s[:, u % 2, m, j * P:(j + 1) * P], K.ident[:, :])
                    ins.then_inc(turned, 1)
                    pe.wait_ge(pT_ready, u + 1)
                    if u >= 2:
                        pe.wait_ge(stored, u - 1)
                    for m in range(2):
                        for j in range(i + 1):
                            c = (g % 2) * 128 + m * HD
                            ins = nc.tensor.matmul(ps[:, 6 + u % 2, m * HD:(m + 1) * HD], pT[:, m, j * P:(j + 1) * P],
                                                   v[:, g // 2, j, c:c + HD], start=(j == 0), stop=(j == i))
                    ins.then_inc(av, 1)

            @block.scalar
            def _(sc):
                for u in range(U):
                    n, b = (u % NT + 1) * P, u % 2
                    sc.wait_ge(maxed, u + 1)
                    for m in range(2):
                        nc.scalar.activation(s[:, b, m, 0:n], s[:, b, m, 0:n], ACT.Exp, bias=nm[:, b, m:m + 1],
                                             scale=1.0, accum_out=l[:, b, m:m + 1]).then_inc(softmax, 1)
                    sc.wait_ge(turned, u + 1)
                    if u:
                        sc.wait_ge(av, u)
                    nc.scalar.activation(pT[:, :, 0:n], ps[:, 4:6, 0:n], ACT.Copy).then_inc(pT_ready, 1)

            @block.vector
            def _(ve):
                def soften(u):
                    g, i = u // NT, u % NT
                    n, b = (i + 1) * P, u % 2
                    ve.wait_ge(scores, u + 1)
                    if u >= 2:
                        ve.wait_ge(turned, u - 1)
                    bank = ps[:, 2 * b:2 * b + 2, 0:n]
                    if g < 2:
                        nc.vector.scalar_tensor_tensor(s[:, b, :, 0:n], bank, float(HD) ** -0.5,
                                                       neg_f[:, 2 * g:2 * g + 2, 0:n], ALU.mult, ALU.add)\
                            .then_inc(biased, 1)
                    else:
                        nc.vector.tensor_scalar(s[:, b, :, 0:n], bank, float(HD) ** -0.5, None, ALU.mult)\
                            .then_inc(biased, 1)
                    ve.wait_ge(biased, u + 1)
                    nc.vector.tensor_tensor(s[:, b, :, i * P:n], s[:, b, :, i * P:n],
                                            mask[:, :].unsqueeze(1).to_broadcast([P, 2, P]), ALU.add).then_inc(diag, 1)
                    ve.wait_ge(diag, u + 1)
                    K.dve_link(nc.vector.tensor_reduce(nm[:, b, :], s[:, b, :, 0:n], AX, ALU.max))
                    nc.vector.tensor_scalar(nm[:, b, :], nm[:, b, :], -1.0, None, ALU.mult).then_inc(maxed, 1)

                ve.wait_ge(K.loads, K.loads_n)
                soften(0)
                for u in range(U):
                    g, i, b = u // NT, u % NT, u % 2
                    if u + 1 < U:
                        soften(u + 1)
                    ve.wait_ge(softmax, 2 * u + 2)
                    K.dve_link(nc.vector.reciprocal(l[:, b, :], l[:, b, :]))
                    ve.wait_ge(av, u + 1)
                    nc.vector.tensor_tensor(y[:, i, g * P:(g + 1) * P].rearrange("p (m d) -> p m d", d=HD),
                                            ps[:, 6 + b, 0:P].rearrange("p (m d) -> p m d", d=HD),
                                            l[:, b, :].unsqueeze(2).to_broadcast([P, 2, HD]), ALU.mult)\
                        .then_inc(stored, 1)


def shifted_features(K, pair, feat, mu):
    nc = K.nc
    with nc.sbuf_tensor("rw_prev", [P, 2, 2, S + 1], F32) as prev:
        with nc.Block() as block:
            @block.vector
            def _(ve):
                nc.vector.memset(prev[:, :, :, 0:1], 0.0)

        def act(j, banks):
            return nc.scalar.activation(prev[:, j % 2, :, 1:], banks, ACT.Copy)

        def dve(j, banks):
            f = feat[:, 2 * j:2 * j + 2, :]
            K.dve_link(nc.vector.tensor_tensor(f, prev[:, j % 2, :, 0:S], banks, ALU.subtract))
            for i in range(2):
                n = 2 * j + i
                ins = nc.vector.scalar_tensor_tensor(feat[:, n, :], feat[:, n, :], mu[:, n:n + 1],
                                                     prev[:, j % 2, i, 1:], ALU.mult, ALU.add)
                if i == 0:
                    K.dve_link(ins)
            return ins

        linear_split(K, "b3_rw", "T", pair, 1, act=act, dve=dve)


def rwkv_prepare(K, feat, col, alpha, beta, decay_end, sgT, vtok, bonus):
    nc, ps, A = K.nc, K.ps, K.A
    n_ = lambda s: K.sem(f"rp_{s}")
    tanhd, wdone, sigw, adone, siga, sqd, nsum, nclamp, nroot, bsum, exps, prod, bonusd, vt, vc = (
        n_(s) for s in "tanh w sigw a siga sq nsum nclamp nroot bsum exp prod bonus vt vc".split())
    loads0 = K.loads_n
    r, k, v = feat[:, 0:4, :], feat[:, 4:8, :], feat[:, 8:12, :]
    cb = lambda key: col(key, RW_T).unsqueeze(2).to_broadcast([P, RW_T, S])
    with ExitStack() as ctx:
        w2 = K.sb(ctx, "rp_w2", [P, 512])
        same = K.sb(ctx, "rp_same", [P, P])
        hsel = K.sb(ctx, "rp_hsel", [P, 2])
        reset = K.sb(ctx, "rp_reset", [P, S])
        omk = K.sb(ctx, "rp_omk", [P, RW_T])
        ld = K.sb(ctx, "rp_ld", [P, RW_T, S])
        a = K.sb(ctx, "rp_a_", [P, RW_T, S])
        b = K.sb(ctx, "rp_b", [P, RW_T, S])
        e = K.sb(ctx, "rp_e", [P, RW_T, S])
        with nc.Block() as block:
            @block.sync
            def _(sp):
                K.load(sp, w2[0:64, :], A["rwkv_w2_3"][0])
                K.load(sp, w2[64:128, :], A["rwkv_a2_3"][0])
                K.load(sp, same[:, :], A["k_same_head"])
                K.load(sp, hsel[:, :], A["k_head_sel"])
                K.load(sp, reset[:, :], A["k_reset"])

            @block.tensor
            def _(pe):
                pe.wait_ge(K.loads, loads0 + 80)
                for t in range(NT):
                    for c in range(RW_T):
                        ins = nc.tensor.transpose(ps[:, t, c * P:(c + 1) * P], feat[:, 8 + c, t * P:(t + 1) * P],
                                                  K.ident[:, :])
                ins.then_inc(vt, 1)
                pe.wait_ge(tanhd, 1)
                for c in range(RW_T):
                    ins = nc.tensor.matmul(ps[:, 4 + c, :], w2[0:64, c * P:(c + 1) * P], feat[0:64, 12, :], start=True,
                                           stop=True)
                ins.then_inc(wdone, 1)
                pe.wait_ge(vc, 1)
                for c in range(RW_T):
                    ins = nc.tensor.matmul(ps[:, c, :], w2[64:128, c * P:(c + 1) * P], feat[64:128, 12, :], start=True,
                                           stop=True)
                ins.then_inc(adone, 1)
                pe.wait_ge(sqd, 1)
                pe.wait_ge(sigw, 1)
                for c in range(RW_T):
                    ins = nc.tensor.matmul(ps[:, 4 + c, :], same[:, :], e[:, c, :], start=True, stop=True)
                ins.then_inc(nsum, 1)
                pe.wait_ge(prod, 1)
                pe.wait_ge(siga, 1)
                for t in range(NT):
                    for c in range(RW_T):
                        ins = nc.tensor.matmul(ps[:, 0, t * 8 + 2 * c:t * 8 + 2 * c + 2], e[:, c, t * P:(t + 1) * P],
                                               hsel[:, :], start=True, stop=True)
                ins.then_inc(bonusd, 1)

            @block.scalar
            def _(sc):
                nc.scalar.activation(feat[0:64, 12, :], feat[0:64, 12, :], ACT.Tanh).then_inc(tanhd, 1)
                nc.scalar.activation(sgT, feat[:, 13, :], ACT.Sigmoid)
                sc.wait_ge(vt, 1)
                nc.scalar.activation(vtok, ps[:, 0:4, :], ACT.Copy).then_inc(vc, 1)
                sc.wait_ge(wdone, 1)
                for c in range(RW_T):
                    ins = nc.scalar.activation(ld[:, c, :], ps[:, 4 + c, :], ACT.Sigmoid, bias=col("w0", RW_T)[:, c:c + 1])
                ins.then_inc(sigw, 1)
                sc.wait_ge(adone, 1)
                for c in range(RW_T):
                    ins = nc.scalar.activation(a[:, c, :], ps[:, c, :], ACT.Sigmoid, bias=col("a0", RW_T)[:, c:c + 1])
                ins.then_inc(siga, 1)
                sc.wait_ge(nclamp, 1)
                nc.scalar.activation(beta, beta, ACT.Sqrt).then_inc(nroot, 1)
                sc.wait_ge(bsum, 1)
                nc.scalar.activation(ld[:, :, :], ld[:, :, :], ACT.Exp).then_inc(exps, 1)
                sc.wait_ge(bonusd, 1)
                nc.scalar.activation(e[:, :, :], b[:, :, :], ACT.Exp).then_inc(exps, 1)
                nc.scalar.activation(b[:, :, :], b[:, :, :], ACT.Exp, scale=-1.0).then_inc(exps, 1)

            @block.vector
            def _(ve):
                ve.wait_ge(K.loads, loads0 + 80)
                K.dve_link(nc.vector.tensor_tensor(alpha, k, cb("k_k"), ALU.mult))
                nc.vector.tensor_tensor(e[:, :, :], alpha, alpha, ALU.mult).then_inc(sqd, 1)
                ve.wait_ge(nsum, 1)
                nc.vector.tensor_scalar(beta, ps[:, 4:8, :], 1e-24, None, ALU.max).then_inc(nclamp, 1)
                ve.wait_ge(nroot, 1)
                K.dve_link(nc.vector.reciprocal(beta, beta))
                K.dve_link(nc.vector.tensor_tensor(alpha, alpha, beta, ALU.mult))
                K.dve_link(nc.vector.tensor_scalar(omk[:, :], col("k_a", RW_T), -1.0, 1.0, ALU.mult, ALU.add))
                ve.wait_ge(siga, 1)
                for c in range(RW_T):
                    K.dve_link(nc.vector.tensor_scalar(beta[:, c, :], a[:, c, :], col("k_a", RW_T)[:, c:c + 1],
                                                       omk[:, c:c + 1], ALU.mult, ALU.add))
                K.dve_link(nc.vector.tensor_tensor(k, k, beta, ALU.mult))
                K.dve_link(nc.vector.tensor_tensor(beta, r, k, ALU.mult))
                nc.vector.tensor_tensor(e[:, :, :], beta, cb("r_k"), ALU.mult).then_inc(prod, 1)
                ve.wait_ge(prod, 1)
                K.dve_link(nc.vector.tensor_tensor(beta, alpha, a[:, :, :], ALU.mult))
                ve.wait_ge(sigw, 1)
                K.dve_link(nc.vector.tensor_scalar(ld[:, :, :], ld[:, :, :], DECAY_SCALE, None, ALU.mult))
                for c in range(RW_T):
                    K.dve_link(nc.vector.tensor_tensor_scan(b[:, c, :], reset[:, :], ld[:, c, :], 0.0, ALU.mult, ALU.add))
                nc.vector.tensor_tensor(ld[:, :, :], b[:, :, :], ld[:, :, :], ALU.subtract).then_inc(bsum, 1)
                ve.wait_ge(bonusd, 1)
                nc.vector.tensor_copy(bonus, ps[:, 0, 0:NT * 8])
                ve.wait_ge(exps, 3)
                K.dve_link(nc.vector.tensor_tensor(alpha, alpha, ld[:, :, :], ALU.mult))
                K.dve_link(nc.vector.tensor_tensor(beta, beta, b[:, :, :], ALU.mult))
                K.dve_link(nc.vector.tensor_tensor(k, k, b[:, :, :], ALU.mult))
                K.dve_link(nc.vector.tensor_tensor(r, r, e[:, :, :], ALU.mult))
                K.dve_link(nc.vector.tensor_copy(decay_end, e[:, :, RWKV_C - 1::RWKV_C]))


def rwkv_scan(K, rho, alpha, beta, kappa, decay_end, vtok, y, spare):
    nc, ps, A = K.nc, K.ps, K.A
    n_ = lambda s: K.sem(f"rs_{s}")
    tr, tok_ready, ab, ak, mb, ab_m, ak_m, mb_m, t_ready, off_ready, xd, x_ready, tx, t_new = (
        n_(s) for s in "tr tok ab ak mb abm akm mbm t off x xready tx tnew".split())
    zd, r_ready, ud, u_ready, p6, rho_ready, y0_ready, ghd, gh_ready, ch, s_ready, yd, y_ready = (
        n_(s) for s in "z rready u uready p6 rho y0 gh ghready chain state y yready".split())
    loads0 = K.loads_n
    H = RW_H
    L = len(LEVELS)
    with ExitStack() as ctx:
        masks = K.sb(ctx, "rs_masks", [P, 4 + L, P])
        id2 = K.sb(ctx, "rs_id2", [P, HD])
        tok = K.sb(ctx, "rs_tokb", [P, 3, 512])
        abT = K.sb(ctx, "rs_abT", [P, H, P])
        akT = K.sb(ctx, "rs_akT", [P, H, P])
        mkT = K.sb(ctx, "rs_mkT", [P, H, P])
        mbT = K.sb(ctx, "rs_mbT", [P, H, P])
        by_head = lambda a: a.rearrange("p a (c n) -> p (a c) n", n=P)
        T, TT, X = by_head(K.hT[:, 4:6, :]), by_head(K.hT[:, 6:8, :]), by_head(spare)
        off = K.sb(ctx, "rs_offb", [P, H, P])
        halves = akT[:, :, :].rearrange("p (a b) n -> p a (b n)", a=2)
        at, un = (halves[:, i, :].rearrange("p (h d) -> p h d", d=HD) for i in range(2))
        rt = K.sb(ctx, "rs_rt", [P, RW_T, P])
        y0 = K.sb(ctx, "rs_y0b", [P, H, HD])
        st = K.sb(ctx, "rs_st", [P, CT + 1, RW_T, HD])
        G = K.hT[:, 0:2, :].rearrange("p a (b c d) -> p (a b) c d", c=RW_T, d=HD)
        Hn = K.hT[:, 2:4, :].rearrange("p a (b c d) -> p (a b) c d", c=RW_T, d=HD)
        R = off
        two = lambda b: ps[:, b:b + 2, :].rearrange("p m (c n) -> p (m c) n", n=P)
        mask = lambda i: masks[:, i, :].unsqueeze(1).to_broadcast([P, H, P])
        ident = K.ident[:, :].unsqueeze(1).to_broadcast([P, H, P])
        head = lambda i, hh: tok[:, i, (hh % 4) * P + (hh // 4) * HD:(hh % 4) * P + (hh // 4) * HD + HD]
        with nc.Block() as block:
            @block.sync
            def _(sp):
                K.load(sp, masks[:, :, :], A["k_rwkv"])
                K.load(sp, id2[:, :], A["k_id2"])

            @block.tensor
            def _(pe):
                pe.wait_ge(K.loads, loads0 + 32)
                for t in range(NT):
                    ts = slice(t * P, (t + 1) * P)

                    def pairs(bank, lhs, rhs):
                        for m in range(2):
                            for c in range(RW_T):
                                r = slice(m * HD, (m + 1) * HD)
                                ins = nc.tensor.matmul(ps[:, bank[m], c * P:(c + 1) * P], lhs[r, c, ts], rhs[r, c, ts],
                                                       start=True, stop=True)
                        return ins

                    if t:
                        pe.wait_ge(y_ready, t)
                    for i, src in enumerate((alpha, beta, kappa)):
                        for c in range(RW_T):
                            ins = nc.tensor.transpose(ps[:, i, c * P:(c + 1) * P], src[:, c, ts], K.ident[:, :])
                    ins.then_inc(tr, 1)
                    pairs((3, 4), beta, alpha)
                    pairs((5, 6), alpha, beta).then_inc(ab, 1)
                    pe.wait_ge(tok_ready, t + 1)
                    pairs((0, 1), kappa, alpha)
                    pairs((2, 7), kappa, rho).then_inc(ak, 1)
                    pe.wait_ge(ab_m, t + 1)
                    pairs((3, 4), beta, rho).then_inc(mb, 1)
                    pe.wait_ge(ak_m, t + 1)
                    pe.wait_ge(mb_m, t + 1)
                    for l in range(L):
                        for m in range(2):
                            n = 2 * (t * L + l) + m
                            pe.wait_ge(off_ready, n + 1)
                            pe.wait_ge(t_new, t * (2 * L + 1) + (2 * l + m if l else 1))
                            for c in range(4):
                                ins = nc.tensor.matmul(ps[:, m, c * P:(c + 1) * P], off[:, 4 * m + c, :],
                                                       T[:, 4 * m + c, :], start=True, stop=True)
                            ins.then_inc(xd, 1)
                        for m in range(2):
                            pe.wait_ge(x_ready, 2 * (t * L + l) + m + 1)
                            for c in range(4):
                                hh, cols = 4 * m + c, slice(c * P, (c + 1) * P)
                                ins = nc.tensor.matmul(ps[:, 3 + m, cols], X[:, hh, :], TT[:, hh, :], start=True,
                                                       stop=True)
                                if l < L - 1:
                                    ins = nc.tensor.matmul(ps[:, 5 + m, cols], TT[:, hh, :], X[:, hh, :], start=True,
                                                           stop=True)
                            ins.then_inc(tx, 1)
                    for hh in range(H):
                        ins = nc.tensor.matmul(ps[:, 0, hh * HD:(hh + 1) * HD], akT[:, hh, :],
                                               vtok[:, t, (hh % 4) * P + (hh // 4) * HD:(hh % 4) * P + (hh // 4) * HD + HD],
                                               start=True, stop=True)
                    ins.then_inc(zd, 1)
                    pe.wait_ge(r_ready, t + 1)
                    pe.wait_ge(t_new, (t + 1) * (2 * L + 1))
                    for hh in range(H):
                        ins = nc.tensor.matmul(ps[:, 5 + hh // 4, (hh % 4) * P:(hh % 4 + 1) * P], TT[:, hh, :],
                                               R[:, hh, :], start=True, stop=True)
                    ins.then_inc(ud, 1)
                    pe.wait_ge(u_ready, t + 1)
                    for hh in range(H):
                        m, c = hh // 4, hh % 4
                        nc.tensor.matmul(ps[m * HD:(m + 1) * HD, 1, c * P:(c + 1) * P], at[:, hh, :], mbT[:, hh, :],
                                         start=True, stop=True)
                    for hh in range(H):
                        vh = vtok[:, t, (hh % 4) * P + (hh // 4) * HD:(hh % 4) * P + (hh // 4) * HD + HD]
                        nc.tensor.matmul(ps[:, 7, hh * HD:(hh + 1) * HD], mkT[:, hh, :], vh, start=True, stop=False)
                        ins = nc.tensor.matmul(ps[:, 7, hh * HD:(hh + 1) * HD], mbT[:, hh, :], un[:, hh, :],
                                               start=False, stop=True)
                    ins.then_inc(p6, 1)
                    for cc in range(CT):
                        q = slice(cc * RWKV_C, (cc + 1) * RWKV_C)
                        for hh in range(H):
                            m, c = hh // 4, hh % 4
                            o = slice(m * HD, (m + 1) * HD)
                            ch0 = c * P + m * HD
                            nc.tensor.matmul(ps[o, 2 + cc, c * HD:(c + 1) * HD], at[q, hh, :], tok[q, 1, ch0:ch0 + HD],
                                             start=True, stop=True)
                            hout = ps[o, 2 + cc, 256 + c * HD:256 + (c + 1) * HD]
                            nc.tensor.matmul(hout, tok[q, 2, ch0:ch0 + HD], vtok[q, t, ch0:ch0 + HD], start=True,
                                             stop=False)
                            ins = nc.tensor.matmul(hout, tok[q, 1, ch0:ch0 + HD], un[q, hh, :], start=False, stop=True)
                    ins.then_inc(ghd, 1)
                    pe.wait_ge(gh_ready, t + 1)
                    pe.wait_ge(rho_ready, t + 1)
                    for cc in range(CT):
                        n = t * CT + cc
                        pe.wait_ge(s_ready, n + t + 1)
                        for hh in range(H):
                            m, c = hh // 4, hh % 4
                            o = slice(m * HD, (m + 1) * HD)
                            ins = nc.tensor.matmul(ps[o, cc % 2, c * HD:(c + 1) * HD], G[o, cc, c, :], st[o, cc, c, :],
                                                   start=True, stop=True)
                        ins.then_inc(ch, 1)
                    pe.wait_ge(y0_ready, t + 1)
                    for cc in range(CT):
                        for m in range(2):
                            for c in range(RW_T):
                                o = slice(m * HD, (m + 1) * HD)
                                ins = nc.tensor.matmul(ps[cc * RWKV_C:(cc + 1) * RWKV_C, 6 + m, c * HD:(c + 1) * HD],
                                                       rt[o, c, cc * RWKV_C:(cc + 1) * RWKV_C], st[o, cc, c, :],
                                                       start=True, stop=True)
                    ins.then_inc(yd, 1)

            @block.scalar
            def _(sc):
                for t in range(NT):
                    sc.wait_ge(tr, t + 1)
                    nc.scalar.activation(tok[:, :, :], ps[:, 0:3, :], ACT.Copy).then_inc(tok_ready, 1)
                    for l in range(L):
                        for m in range(2):
                            sc.wait_ge(xd, 2 * (t * L + l) + m + 1)
                            nc.scalar.activation(X[:, 4 * m:4 * m + 4, :],
                                                 ps[:, m, :].rearrange("p (c n) -> p c n", n=P), ACT.Copy)\
                                .then_inc(x_ready, 1)
                    sc.wait_ge(p6, t + 1)
                    nc.scalar.activation(y0[:, :, :], ps[:, 7, :].rearrange("p (h d) -> p h d", d=HD), ACT.Copy)\
                        .then_inc(y0_ready, 1)

            @block.vector
            def _(ve):
                ve.wait_ge(K.loads, loads0 + 32)
                nc.vector.memset(st[:, 0, :, :], 0.0).then_inc(s_ready, 1)
                for t in range(NT):
                    ve.wait_ge(ab, t + 1)
                    K.dve_link(nc.vector.tensor_tensor(abT[:, :, :], two(3), mask(1), ALU.mult))
                    K.dve_link(nc.vector.tensor_tensor(T[:, :, :], two(5), mask(0), ALU.mult))
                    K.dve_link(nc.vector.tensor_tensor(TT[:, :, :], abT[:, :, :], mask(3 + L), ALU.mult))
                    K.dve_link(nc.vector.tensor_tensor(TT[:, :, :], ident, TT[:, :, :], ALU.subtract))
                    nc.vector.tensor_tensor(T[:, :, :], ident, T[:, :, :], ALU.subtract).then_inc(t_new, 1)
                    ve.wait_ge(t_new, t * (2 * L + 1) + 1)
                    nc.vector.tensor_copy(st[:, 0, :, :], st[:, 0, :, :]).then_inc(ab_m, 1)
                    ve.wait_ge(ak, t + 1)
                    nc.vector.tensor_tensor(akT[:, :, :], two(0), mask(1), ALU.mult)
                    for m, bank in enumerate((2, 7)):
                        ins = nc.vector.tensor_tensor(mkT[:, 4 * m:4 * m + 4, :],
                                                      ps[:, bank, :].rearrange("p (c n) -> p c n", n=P),
                                                      masks[:, 2, :].unsqueeze(1).to_broadcast([P, 4, P]), ALU.mult)
                    ins.then_inc(ak_m, 1)
                    ve.wait_ge(mb, t + 1)
                    nc.vector.tensor_tensor(mbT[:, :, :], two(3), mask(2), ALU.mult).then_inc(mb_m, 1)

                    def make_off(l, m):
                        hs = slice(4 * m, 4 * m + 4)
                        n = 2 * (t * L + l) + m
                        if n > 1:
                            ve.wait_ge(xd, n - 1)
                        nc.vector.tensor_tensor(off[:, hs, :], abT[:, hs, :], mask(3 + l)[:, hs, :], ALU.mult)\
                            .then_inc(off_ready, 1)

                    for m in range(2):
                        make_off(0, m)
                    for l in range(L):
                        for m in range(2):
                            hs = slice(4 * m, 4 * m + 4)
                            half = lambda bank: ps[:, bank, :].rearrange("p (c n) -> p c n", n=P)
                            if l < L - 1:
                                make_off(l + 1, m)
                            ve.wait_ge(tx, 2 * (t * L + l) + m + 1)
                            if l < L - 1:
                                K.dve_link(nc.vector.tensor_tensor(T[:, hs, :], T[:, hs, :], half(5 + m),
                                                                   ALU.subtract))
                            nc.vector.tensor_tensor(TT[:, hs, :], TT[:, hs, :], half(3 + m), ALU.subtract)\
                                .then_inc(t_new, 1)
                            ve.wait_ge(t_new, t * (2 * L + 1) + 2 * l + m + 2)
                    ve.wait_ge(zd, t + 1)
                    nc.vector.tensor_copy(R[:, :, HD:], ps[:, 0, :].rearrange("p (h d) -> p h d", d=HD))
                    nc.vector.tensor_copy(R[:, :, 0:HD].rearrange("p (m c) d -> p m c d", m=2),
                                          tok[:, 0, :].rearrange("p (c m d) -> p m c d", m=2, d=HD)).then_inc(r_ready, 1)
                    ve.wait_ge(ud, t + 1)
                    nc.vector.tensor_copy(at[:, :, :], two(5)[:, :, 0:HD])
                    nc.vector.tensor_scalar(un[:, :, :], two(5)[:, :, HD:], -1.0, None, ALU.mult).then_inc(u_ready, 1)
                    ve.wait_ge(p6, t + 1)
                    nc.vector.tensor_tensor(rt[:, :, :], rho[:, :, t * P:(t + 1) * P],
                                            ps[:, 1, :].rearrange("p (c n) -> p c n", n=P), ALU.subtract)\
                        .then_inc(rho_ready, 1)
                    ve.wait_ge(ghd, t + 1)
                    gh = ps[:, 2:6, :].rearrange("p c (g n d) -> p c g n d", g=2, d=HD)
                    W = decay_end[:, :, t * CT:(t + 1) * CT]
                    for cc in range(CT):
                        nc.vector.tensor_tensor(G[:, cc, :, :], id2[:, :].unsqueeze(1).to_broadcast([P, RW_T, HD]),
                                                gh[:, cc, 0, :, :], ALU.subtract)
                        ins = nc.vector.tensor_tensor(Hn[:, cc, :, :], gh[:, cc, 1, :, :],
                                                      W[:, :, cc:cc + 1].to_broadcast([P, RW_T, HD]), ALU.mult)
                    K.dve_link(ins)
                    nc.vector.tensor_copy(st[:, CT, 0, 0:1], st[:, 0, 0, 0:1]).then_inc(gh_ready, 1)
                    for cc in range(CT):
                        n = t * CT + cc
                        ve.wait_ge(ch, n + 1)
                        K.dve_link(nc.vector.tensor_tensor(st[:, cc + 1, :, :],
                                                           ps[:, cc % 2, 0:256].rearrange("p (c d) -> p c d", d=HD),
                                                           W[:, :, cc:cc + 1].to_broadcast([P, RW_T, HD]), ALU.mult))
                        nc.vector.tensor_tensor(st[:, cc + 1, :, :], st[:, cc + 1, :, :], Hn[:, cc, :, :], ALU.add)\
                            .then_inc(s_ready, 1)
                        ve.wait_ge(s_ready, n + t + 2)
                    ve.wait_ge(yd, t + 1)
                    ve.wait_ge(y0_ready, t + 1)
                    nc.vector.tensor_tensor(y[:, t, :].rearrange("p (c m d) -> p m c d", m=2, d=HD),
                                            ps[:, 6:8, 0:256].rearrange("p m (c d) -> p m c d", d=HD),
                                            y0[:, :, :].rearrange("p (m c) d -> p m c d", m=2), ALU.add)\
                        .then_inc(y_ready, 1)
                    if t < NT - 1:
                        nc.vector.tensor_copy(st[:, 0, :, :], st[:, CT, :, :]).then_inc(s_ready, 1)


def rwkv_finish(K, y, sgT, vtok, bonus):
    nc, ps, A = K.nc, K.ps, K.A
    group_norm(K, "rw_gn", y[:, :, :].rearrange("p t (h d) -> p (t h) d", d=HD), NT * RW_H, HD, GN_EPS_3, centre=True)
    gated = K.sem("rf_gate")
    with ExitStack() as ctx:
        g2 = K.sb(ctx, "rf_g2", [P, 512])
        lw = K.sb(ctx, "rf_lw", [P, 2, 512])
        with nc.Block() as block:
            @block.sync
            def _(sp):
                K.load(sp, g2[:, :], A["rwkv_g2_3"][0])
                for i, key in enumerate(("rwkv_ln_w_3", "rwkv_ln_b_3")):
                    K.load(sp, lw[:, i, :], A[key][0].rearrange("(a n) -> a n", a=1).partition_broadcast(P))

            @block.tensor
            def _(pe):
                pe.wait_ge(K.loads, K.loads_n)
                for t in range(NT):
                    ins = nc.tensor.matmul(ps[:, t, :], sgT[:, t * P:(t + 1) * P], g2[:, :], start=True, stop=True)
                ins.then_inc(gated, 1)

            @block.vector
            def _(ve):
                ve.wait_ge(K.loads, K.loads_n)
                for i, op in enumerate((ALU.mult, ALU.add)):
                    K.dve_link(nc.vector.tensor_tensor(y[:, :, :], y[:, :, :],
                                                       lw[:, i, :].unsqueeze(1).to_broadcast([P, NT, 512]), op))
                heads = lambda a: a[:, :, :].rearrange("p t (h d) -> p (t h) d", d=HD)
                K.dve_link(nc.vector.tensor_tensor(heads(vtok), heads(vtok),
                                                   bonus[:, :].unsqueeze(2).to_broadcast([P, NT * RW_H, HD]), ALU.mult))
                K.dve_link(nc.vector.tensor_tensor(y[:, :, :], y[:, :, :], vtok[:, :, :], ALU.add))
                ve.wait_ge(gated, 1)
                K.dve_link(nc.vector.tensor_tensor(y[:, :, :], ps[:, 0:4, :], y[:, :, :], ALU.mult))


def conv_up(K, stage, pair, cw, ffT):
    nc = K.nc
    first, last = K.stream.span[stage]
    units = FFN_T // 2
    copied, conv, sig, made = (K.sem(f"cu_{n}") for n in "copied conv sig made".split())
    with ExitStack() as ctx:
        u = K.sb(ctx, "cu_u", [P, 2, 4, S + 2])
        c, sg = K.hT[:, 0:4, :], K.hT[:, 4:6, :]
        W = SplitWeights(K, ctx, stage)
        with nc.Block() as block:
            @block.vector
            def _(ve):
                nc.vector.memset(u[:, :, :, 0:2], 0.0)
        with nc.Block() as block:
            @block.sync
            def _(sp):
                K.refill(sp, first, last)

            @block.tensor
            def _(pe):
                for j in range(units):
                    if j >= 2:
                        pe.wait_ge(copied, j - 1)
                    b = 4 * (j % 2)
                    for i in range(2):
                        W.tiles(pe, first + 2 * j + i, pair, K.ps[:, b + 2 * i:b + 2 * i + 2, :])

            @block.gpsimd
            def _(po):
                W.pool(po)

            @block.scalar
            def _(sc):
                for j in range(units + 1):
                    for i in range(4):
                        if j < units:
                            W.act_high(sc, first + 2 * j + i // 2, i % 2)
                        if j and i == 1:
                            sc.wait_ge(K.chunk_used, first + 2 * j)
                            if j >= 3:
                                sc.wait_ge(conv, j - 2)
                            nc.scalar.activation(u[:, (j - 1) % 2, :, 2:],
                                                 K.ps[:, 4 * ((j - 1) % 2):4 * ((j - 1) % 2) + 4, :], ACT.Copy)\
                                .then_inc(copied, 1)
                        if j and i == 3:
                            sc.wait_ge(conv, j)
                            if j > 1:
                                sc.wait_ge(made, j - 1)
                            nc.scalar.activation(sg, c[:, 0:2, :], ACT.Sigmoid).then_inc(sig, 1)

            @block.vector
            def _(ve):
                steps = 0
                for j in range(units):
                    ve.wait_ge(copied, j + 1)
                    tiles = (2 * j, 2 * j + 1, FFN_T + 2 * j, FFN_T + 2 * j + 1)
                    for tap in (2, 1, 0):
                        for i, n in enumerate(tiles):
                            src = u[:, j % 2, i, tap:tap + S]
                            if tap == 2:
                                ins = nc.vector.tensor_scalar(c[:, i, :], src, cw(2)[:, n:n + 1], cw(3)[:, n:n + 1],
                                                              ALU.mult, ALU.add)
                            else:
                                ins = nc.vector.scalar_tensor_tensor(c[:, i, :], src, cw(tap)[:, n:n + 1], c[:, i, :],
                                                                     ALU.mult, ALU.add)
                            if i == 3 and tap:
                                K.dve_link(ins)
                    ins.then_inc(conv, 1)
                    ve.wait_ge(conv, j + 1)
                    K.dve_link(nc.vector.tensor_tensor(c[:, 2:4, :], c[:, 0:2, :], c[:, 2:4, :], ALU.mult))
                    ve.wait_ge(sig, j + 1)
                    nc.vector.tensor_tensor(ffT[:, 2 * j:2 * j + 2, :], sg, c[:, 2:4, :], ALU.mult)\
                        .then_inc(made, 1)
                    ve.wait_ge(made, j + 1)


def block3(K):
    nc, A = K.nc, K.A
    with ExitStack() as ctx:
        gates = K.sb(ctx, "b3_gates", [P, 2, D])
        mods = K.sb(ctx, "b3_mods", [P, 4, KD])
        names = [("c", "c_3"), ("g1", "norm_mix_3"), ("g2", "norm_ffn_3"), ("mu", "rwkv_mu_3"), ("w0", "rwkv_w0_3"),
                 ("a0", "rwkv_a0_3"), ("k_k", "rwkv_k_k_3"), ("k_a", "rwkv_k_a_3")]
        vectors = [(k, A[n][0]) for k, n in names] + [("r_k", A["rwkv_r_k_3"][0].rearrange("h d -> (h d)"))]
        cols, at = load_columns(K, "b3_cols", vectors, ctx)
        col = lambda key, n: cols[:, at[key]:at[key] + n]
        modulation(K, "mod3", col("c", KD), A["b_mod_3"][0], gates, mods[:, 0, :], mods[:, 1, :], mods[:, 2, :],
                   mods[:, 3, :], col("g1", KD), col("g2", KD))
        with nc.sbuf_tensor("b3_xn", [P, NT, D], F32) as xn:
            normalise(K, "b3_norm", xn, mods[:, 0, :], mods[:, 1, :], K.hT)
        with ExitStack() as mix:
            ya = K.sb(mix, "b3_ya", [P, NT, 512])
            with ExitStack() as att:
                qkT = K.sb(att, "b3_qkT", [P, 8, S])
                v = K.sb(att, "b3_v_", [P, 2, NT, 256])
                f = K.sb(att, "b3_f_", [P, NT, 4])
                nf = K.sb(att, "b3_negF", [P, 4, S])
                with nc.sbuf_tensor("b3_xpair", [P, 2, KD, S], F32R) as pair:
                    split_rows(K, "b3_xpair", K.hT, pair)
                    linear_split(K, "b3_qk", "T", pair, 1,
                                 act=lambda j, b: nc.scalar.activation(qkT[:, 2 * j:2 * j + 2, :], b, ACT.Copy))
                    linear_split(K, "b3_v", "N", pair, 1,
                                 act=lambda j, b: nc.scalar.activation(v[:, j, :, :], b[:, :, 0:256], ACT.Copy))
                linear(K, "b3_f", "N", K.hT, 1,
                       act=lambda j, b: nc.scalar.activation(f[:, :, :], b[:, :, 0:4], ACT.Copy))
                forget_sums(K, f, nf[:, :, :])
                causal_attention(K, qkT, v, nf, ya)
            sgT = K.sb(mix, "b3_sgT", [P, S])
            bonus = K.sb(mix, "b3_bonus", [P, NT * RW_H])
            wend = K.sb(mix, "b3_wend", [P, RW_T, S // RWKV_C])
            vtok = K.sb(mix, "b3_vtok", [P, NT, 512])
            feat = K.sb(mix, "b3_feat", [P, 14, S])
            with nc.sbuf_tensor("b3_rpair", [P, 2, KD, S], F32R) as pair:
                split_rows(K, "b3_rpair", K.hT, pair)
                shifted_features(K, pair, feat, col("mu", 14))
            alpha = K.sb(mix, "b3_alpha", [P, RW_T, S])
            beta = K.sb(mix, "b3_beta", [P, RW_T, S])
            rwkv_prepare(K, feat, col, alpha[:, :, :], beta[:, :, :], wend[:, :, :], sgT[:, :], vtok[:, :, :],
                         bonus[:, :])
            y = feat[:, 8:12, :]
            rwkv_scan(K, feat[:, 0:4, :], alpha, beta, feat[:, 4:8, :], wend[:, :, :], vtok, y, feat[:, 12:14, :])
            rwkv_finish(K, y, sgT, vtok, bonus)
            turn_tiles(K, "b3_yT",
                       [(lambda t, i=i: ya[:, t, i * P:(i + 1) * P]) for i in range(2)] +
                       [(lambda t, i=i: y[:, t, i * P:(i + 1) * P]) for i in range(4)] +
                       [(lambda t, i=i: ya[:, t, (2 + i) * P:(3 + i) * P]) for i in range(2)],
                       [K.hT[:, i, :] for i in range(8)])
        add_residual(K, "b3_out", K.hT, 2, gate=gates[:, 0, :])
        with nc.sbuf_tensor("b3_xn2", [P, NT, D], F32) as xn:
            normalise(K, "b3_norm2", xn, mods[:, 2, :], mods[:, 3, :], K.hT)
        with ExitStack() as ffn:
            ffT = K.sb(ffn, "b3_ffT", [P, FFN_T, S])
            cw01, _ = load_columns(K, "b3_cw01", [("0", A["conv_w_3"][0, 0]), ("1", A["conv_w_3"][0, 1])], ffn)
            cw2b, _ = load_columns(K, "b3_cw2b", [("2", A["conv_w_3"][0, 2]), ("b", A["conv_b_3"][0])], ffn)
            n = 2 * FFN_T
            with nc.sbuf_tensor("b3_hpair", [P, 2, KD, S], F32R) as pair:
                split_rows(K, "b3_hpair", K.hT, pair)
                conv_up(K, "b3_up", pair, lambda j: (cw01, cw2b)[j // 2][:, (j % 2) * n:(j % 2 + 1) * n], ffT)
            add_residual(K, "b3_down", ffT, 6, gate=gates[:, 1, :])
    final_norm(K, "b3_final", A["norm_final_3"], True)


def t5_bucket(dist, max_dist):
    exact = 16
    d = np.maximum(dist, 1).astype(np.float32)
    large = exact + (np.log(d / np.float32(exact)) / np.float32(math.log(max_dist / exact)) * np.float32(16))\
        .astype(np.int32)
    return np.where(dist < exact, dist, np.minimum(large, 31))


def hot_rows(dist, valid, max_dist):
    out = np.zeros((33, len(dist)), np.float32)
    b = t5_bucket(np.maximum(dist, 0), max_dist)
    for i in range(len(dist)):
        out[b[i] if valid[i] else 32, i] = 1.0
    return out


def shape_constants():
    c = {"k_ident": np.eye(P, dtype=np.float32)}
    half = RDK // 2
    inv = np.float32(10000.0) ** (-np.arange(half, dtype=np.float32) / np.float32(half))
    ang = np.arange(S, dtype=np.float32)[None, :] * inv[:, None]
    c["k_cos"] = np.concatenate([np.cos(ang)] * 2).astype(np.float32)
    c["k_sin"] = np.concatenate([np.sin(ang)] * 2).astype(np.float32)
    rot = np.zeros((P, P), np.float32)
    rot[np.arange(half) + half, np.arange(half)] = -1.0
    rot[np.arange(half), np.arange(half) + half] = 1.0
    c["k_rot"] = rot
    log_g = np.log1p(-np.exp2(-5.0 - np.arange(RH, dtype=np.float64)))
    p, f = np.arange(P)[:, None], np.arange(P)[None, :]
    dist = np.stack([128 * t + f - p for t in range(NT)], 1)
    c["k_decay"] = np.stack([np.where(dist >= 0, np.exp(np.maximum(dist, 0) * g), 0.0) * RDK ** -0.5 for g in log_g],
                            1).astype(np.float32)
    q = np.arange(1024)
    hot = [hot_rows(511 - q, (511 - q >= 0) & (511 - q <= 128), 2048)]
    q = np.arange(256)
    hot.append(hot_rows(4 * (127 - q), 127 - q >= 0, 2048))
    hot.append(hot_rows(4 * (127 - q), (127 - q >= 0) & ((127 - q) % 4 == 0), 2048))
    c["k_hot1"] = np.concatenate(hot, 1)
    c["k_before"] = (p < f).astype(np.float32)
    spans = S // CAP - 1
    ids = np.stack([np.repeat(np.arange(EXPERTS), spans), np.tile(CAP * (1 + np.arange(spans)), EXPERTS)])
    c["k_spans"] = np.broadcast_to(ids.astype(np.float32), (P, 2, EXPERTS * spans)).copy()
    c["k_iota"] = np.broadcast_to(np.arange(CAP, dtype=np.float32), (P, CAP)).copy()
    q = np.arange(640)
    c["k_hot2"] = hot_rows(511 - q, 511 - q >= 0, 128)
    same = p // GC == f // GC
    c["k_gla_tri"] = np.stack([same & (p <= f), same], 1).astype(np.float32)
    c["k_gla_heads"] = (p // GDK == np.arange(GH * GDV)[None, :] // GDV).astype(np.float32)
    bands = []
    for win in WINDOWS:
        inside = (f - p >= 0) & (f - p < win)
        eye = (p == f).astype(np.float32)
        head = inside / np.minimum(f + 1, win).astype(np.float32) - eye
        before = ((f + P - p) < win) / np.float32(win)
        bands.append(np.stack([head, inside / np.float32(win) - eye, before], 1))
    c["k_pool"] = np.stack(bands, 1).astype(np.float32)
    c["k_upto"] = (p <= f).astype(np.float32)
    c["k_future"] = np.where(f > p, np.float32(NEG), np.float32(0.0)).astype(np.float32)
    c["k_same_head"] = (p // HD == f // HD).astype(np.float32)
    c["k_head_sel"] = (p // HD == np.arange(2)[None, :]).astype(np.float32)
    c["k_reset"] = np.broadcast_to((np.arange(S) % RWKV_C != 0).astype(np.float32), (P, S)).copy()
    c["k_id2"] = (p % HD == np.arange(HD)[None, :]).astype(np.float32)
    chunk = p // RWKV_C == f // RWKV_C

    def joins(n):
        return (p // (2 * n) == f // (2 * n)) & (p % (2 * n) >= n) & (f % (2 * n) < n)

    c["k_rwkv"] = np.stack([joins(1), chunk & (p < f), chunk & (p <= f)] + [joins(n).T for n in LEVELS] + [joins(1).T],
                           1).astype(np.float32)
    return c


def build(nc, A, out):
    stream = Stream()
    for plan in PLANS:
        plan(stream, A)
    with ExitStack() as ctx:
        K = Kit(nc, ctx, A, out, stream)
        with nc.Block() as block:
            @block.sync
            def _(sp):
                K.load(sp, K.ident[:, :], A["k_ident"])
                sp.wait_ge(K.loads, K.loads_n)

            @block.vector
            def _(ve):
                nc.vector.memset(K.ones[:, :], 1.0)
        for run in RUNS:
            K.scope(run)


_OUT = (1, S, D)


def kernel(**inputs):
    import concourse.bacc as _bacc
    from concourse.bass_utils import run_bass_kernel_spmd as _run

    nc = _bacc.Bacc("TRN2", target_bir_lowering=False, num_devices=1)
    arrays, A = {}, {}
    for name, a in {**{k: inputs[k] for k in INPUTS}, **shape_constants()}.items():
        a = np.ascontiguousarray(a)
        arrays[f"in_{name}"] = a
        A[name] = nc.dram_tensor(f"in_{name}", a.shape, mybir.dt.from_np(a.dtype), kind="ExternalInput").ap()
    out = nc.dram_tensor("out_0", _OUT, F32, kind="ExternalOutput").ap()
    build(nc, A, out)
    r = _run(nc, [arrays], core_ids=[0])
    return r.results[0]["out_0"]


INPUTS = ["x", "c", "w_ada", "b_ada", "g_mix", "w_in", "rel_bias", "w_ret_o", "w_att_o", "w_o", "g_ffn",
          "w_router", "b_router", "w_mlp1", "b_mlp1", "w_mlp2", "b_mlp2", "g_final", "attn_norm_g_2", "w_in_2",
          "q_norm_g_2", "k_norm_g_2", "lambda_vecs_2", "da_subln_g_2", "rel_bias_2", "gla_gate_w_2",
          "gla_gate_b_2", "gla_norm_g_2", "pool_w_2", "pool_scale_2", "w_out_2", "ffn_norm_g_2", "w_gate_2",
          "w_up_2", "w_down_2", "c_3", "w_mod_3", "b_mod_3", "norm_mix_3", "w_in_3", "fox_f_bias_3",
          "rwkv_mu_3", "rwkv_w0_3", "rwkv_w2_3", "rwkv_a0_3", "rwkv_a2_3", "rwkv_g2_3", "rwkv_k_k_3",
          "rwkv_k_a_3", "rwkv_r_k_3", "rwkv_ln_w_3", "rwkv_ln_b_3", "w_out_3", "norm_ffn_3", "w_up_3",
          "conv_w_3", "conv_b_3", "w_down_3", "norm_final_3"]
PLANS = [plan_block1, plan_block2, plan_block3]
RUNS = [block1, block2, block3]
```
